# Optimizing a Trainium2 kernel written in Bass

```python
import math
import jax
import jax.numpy as jnp
from jax import lax
import numpy as np

D_MODEL = 1024
BATCH = 1
SEQ = 512
DEPTH = 2

HEAD_DIM = 64
A_HEADS = 8
A_WIDTH = A_HEADS * HEAD_DIM
DILATED_PATTERNS = ((128, 1), (512, 4), (2048, 16))
DIL_BLOCK = 128
DIFF_HEADS = 4
DIFF_QK_WIDTH = 2 * DIFF_HEADS * HEAD_DIM
DIFF_V_DIM = 2 * HEAD_DIM
DIFF_V_WIDTH = DIFF_HEADS * DIFF_V_DIM
Q_BLOCK = 128
ATT_IN_WIDTH = 3 * A_WIDTH + 2 * DIFF_QK_WIDTH + DIFF_V_WIDTH
ATT_MIX_WIDTH = A_WIDTH + DIFF_V_WIDTH
ROPE_THETA = 10000.0
HGRN_EXPAND = 128
HGRN_HEADS = D_MODEL // HGRN_EXPAND
HGRN_KEY_DIM = HGRN_EXPAND
HGRN_VAL_DIM = D_MODEL // HGRN_HEADS
HGRN_FORGET_WIDTH = HGRN_HEADS * HGRN_KEY_DIM
HGRN_VAL_WIDTH = HGRN_HEADS * HGRN_VAL_DIM
REC_IN_WIDTH = 2 * HGRN_FORGET_WIDTH + 2 * HGRN_VAL_WIDTH
REC_MIX_WIDTH = HGRN_VAL_WIDTH
HGRN_CHUNK = 64
FFN_HIDDEN = (8 * D_MODEL + 3 * 256 - 1) // (3 * 256) * 256
N_ATT_LAYERS = (DEPTH + 1) // 2
N_REC_LAYERS = DEPTH // 2
NORM_EPS = 1e-6
NEG_INF = -1e30

kernel_name = 'hybrid_dilated_diff_hgrn2_trunk'

def rms_norm(x, gain):
    xf = x.astype(jnp.float32)
    y = xf * lax.rsqrt(jnp.mean(xf * xf, axis=-1, keepdims=True) + NORM_EPS)
    return (y * gain.astype(jnp.float32)).astype(x.dtype)

def rope_tables(seq_len, dim):
    inv_freq = ROPE_THETA ** (-jnp.arange(0, dim, 2, dtype=jnp.float32) / dim)
    ang = jnp.arange(seq_len, dtype=jnp.float32)[:, None] * inv_freq[None, :]
    return jnp.cos(ang), jnp.sin(ang)

def apply_rope(x, cos, sin):
    xf = x.astype(jnp.float32)
    x1, x2 = jnp.split(xf, 2, axis=-1)
    out = jnp.concatenate([x1 * cos - x2 * sin, x2 * cos + x1 * sin], axis=-1)
    return out.astype(x.dtype)

def split_heads(t, n_heads, head_dim):
    b, s, _ = t.shape
    return t.reshape(b, s, n_heads, head_dim).transpose(0, 2, 1, 3)

def merge_heads(t):
    b, h, s, d = t.shape
    return t.transpose(0, 2, 1, 3).reshape(b, s, h * d)

def dilated_window_attention(q, k, v, window, dilation):
    b, h, s, d = q.shape
    span = window // dilation
    L = s // dilation
    nb = -(-L // DIL_BLOCK)
    Lp = nb * DIL_BLOCK

    def to_blocks(t):
        t = t.reshape(b, h, L, dilation, d).transpose(0, 1, 3, 2, 4)
        t = jnp.pad(t, ((0, 0), (0, 0), (0, 0), (0, Lp - L), (0, 0)))
        return t.reshape(b, h, dilation, nb, DIL_BLOCK, d)

    qb, kb, vb = to_blocks(q), to_blocks(k), to_blocks(v)

    def with_prev(t):
        prev = jnp.pad(t, ((0, 0), (0, 0), (0, 0), (1, 0), (0, 0), (0, 0)))[:, :, :, :-1]
        return jnp.concatenate([prev, t], axis=4)

    kc, vc = with_prev(kb), with_prev(vb)
    scores = jnp.einsum('bhrnqd,bhrnkd->bhrnqk', qb, kc).astype(jnp.float32) * (d ** -0.5)
    qi = jnp.arange(DIL_BLOCK)[:, None]
    ki = jnp.arange(2 * DIL_BLOCK)[None, :] - DIL_BLOCK
    rel = qi - ki
    key_idx = jnp.arange(nb)[:, None, None] * DIL_BLOCK + ki[None]
    mask = (rel >= 0) & (rel <= span) & (key_idx >= 0)
    scores = jnp.where(mask, scores, NEG_INF)
    lse = jax.nn.logsumexp(scores, axis=-1)
    probs = jnp.exp(scores - lse[..., None])
    out = jnp.einsum('bhrnqk,bhrnkd->bhrnqd', probs, vc.astype(jnp.float32))

    def from_blocks(t):
        t = t.reshape(b, h, dilation, Lp, t.shape[-1])[:, :, :, :L]
        return t.transpose(0, 1, 3, 2, 4).reshape(b, h, s, t.shape[-1])

    return from_blocks(out), from_blocks(lse[..., None])[..., 0]

def longnet_attention(q, k, v):
    outs, lses = [], []
    for window, dilation in DILATED_PATTERNS:
        o, l = dilated_window_attention(q, k, v, window, dilation)
        outs.append(o)
        lses.append(l)
    weights = jax.nn.softmax(jnp.stack(lses), axis=0)
    return jnp.einsum('pbhs,pbhsd->bhsd', weights, jnp.stack(outs)).astype(q.dtype)

def differential_attention(q, k, v, lam):
    b, h2, s, d = q.shape
    h = h2 // 2
    nb = s // Q_BLOCK
    q_blocks = q.reshape(b, h2, nb, Q_BLOCK, d).transpose(2, 0, 1, 3, 4)
    key_pos = jnp.arange(s)
    vf = v.astype(jnp.float32)

    def one_block(args):
        q_blk, blk_idx = args
        sc = jnp.einsum('bhqd,bhkd->bhqk', q_blk, k).astype(jnp.float32) * (d ** -0.5)
        q_pos = blk_idx * Q_BLOCK + jnp.arange(Q_BLOCK)
        sc = jnp.where(key_pos[None, :] <= q_pos[:, None], sc, NEG_INF)
        p = jax.nn.softmax(sc, axis=-1).reshape(b, h, 2, Q_BLOCK, s)
        w = p[:, :, 0] - lam * p[:, :, 1]
        return jnp.einsum('bhqk,bhkd->bhqd', w, vf)

    out = lax.map(one_block, (q_blocks, jnp.arange(nb)))
    return out.transpose(1, 2, 0, 3, 4).reshape(b, h, s, v.shape[-1])

def attention_mixer(h, w_in, lambda_params, subln_gain, w_out, lambda_init, cos, sin):
    proj = h @ w_in
    cuts = [A_WIDTH, 2 * A_WIDTH, 3 * A_WIDTH, 3 * A_WIDTH + DIFF_QK_WIDTH,
            3 * A_WIDTH + 2 * DIFF_QK_WIDTH]
    qa, ka, va, qd, kd, vd = jnp.split(proj, cuts, axis=-1)
    qa = apply_rope(split_heads(qa, A_HEADS, HEAD_DIM), cos, sin)
    ka = apply_rope(split_heads(ka, A_HEADS, HEAD_DIM), cos, sin)
    oa = longnet_attention(qa, ka, split_heads(va, A_HEADS, HEAD_DIM))
    qd = apply_rope(split_heads(qd, 2 * DIFF_HEADS, HEAD_DIM), cos, sin)
    kd = apply_rope(split_heads(kd, 2 * DIFF_HEADS, HEAD_DIM), cos, sin)
    lp = lambda_params.astype(jnp.float32)
    lam = jnp.exp(jnp.sum(lp[0] * lp[1])) - jnp.exp(jnp.sum(lp[2] * lp[3])) + lambda_init
    od = differential_attention(qd, kd, split_heads(vd, DIFF_HEADS, DIFF_V_DIM), lam)
    od = rms_norm(od, subln_gain) * (1.0 - lambda_init)
    mixed = jnp.concatenate([merge_heads(oa), merge_heads(od).astype(h.dtype)], axis=-1)
    return mixed @ w_out

def hgrn2_chunkwise(q, k, v, log_f):
    b, h, s, kd = q.shape
    vd = v.shape[-1]
    n = s // HGRN_CHUNK

    def chunks(t):
        return t.reshape(b, h, n, HGRN_CHUNK, t.shape[-1]).transpose(2, 0, 1, 3, 4)

    causal = jnp.tril(jnp.ones((HGRN_CHUNK, HGRN_CHUNK), dtype=bool))[:, :, None]

    def step(state, inp):
        qc, kc, vc, gc = inp
        bcum = jnp.cumsum(gc, axis=2)
        inter = jnp.einsum('bhtk,bhkv->bhtv', qc * jnp.exp(bcum), state)
        diff = bcum[:, :, :, None, :] - bcum[:, :, None, :, :]
        decay = jnp.where(causal, jnp.exp(jnp.where(causal, diff, 0.0)), 0.0)
        attn = jnp.einsum('bhtk,bhsk,bhtsk->bhts', qc, kc, decay)
        intra = jnp.einsum('bhts,bhsv->bhtv', attn, vc)
        b_last = bcum[:, :, -1]
        state = jnp.exp(b_last)[..., None] * state + jnp.einsum(
            'bhsk,bhsv->bhkv', kc * jnp.exp(b_last[:, :, None, :] - bcum), vc)
        return state, inter + intra

    state0 = jnp.zeros((b, h, kd, vd), jnp.float32)
    _, out = lax.scan(step, state0, (chunks(q), chunks(k), chunks(v), chunks(log_f)))
    return out.transpose(1, 2, 0, 3, 4).reshape(b, h, s, vd)

def hgrn2_mixer(h, w_in, lower_bound, g_gain, w_out):
    b, s, _ = h.shape
    proj = h @ w_in
    q, f, i, g = jnp.split(proj, [HGRN_FORGET_WIDTH, 2 * HGRN_FORGET_WIDTH,
                                  2 * HGRN_FORGET_WIDTH + HGRN_VAL_WIDTH], axis=-1)
    forget = lower_bound + (1.0 - lower_bound) * jax.nn.sigmoid(f.astype(jnp.float32))
    log_f = jnp.log(forget)
    k = 1.0 - forget
    qf = jax.nn.silu(q.astype(jnp.float32)) * (HGRN_KEY_DIM ** -0.5)
    o = hgrn2_chunkwise(split_heads(qf, HGRN_HEADS, HGRN_KEY_DIM),
                        split_heads(k, HGRN_HEADS, HGRN_KEY_DIM),
                        split_heads(i.astype(jnp.float32), HGRN_HEADS, HGRN_VAL_DIM),
                        split_heads(log_f, HGRN_HEADS, HGRN_KEY_DIM))
    o = o.transpose(0, 2, 1, 3)
    gate = jax.nn.silu(g.astype(jnp.float32)).reshape(b, s, HGRN_HEADS, HGRN_VAL_DIM)
    o = rms_norm(o, g_gain) * gate
    return o.reshape(b, s, REC_MIX_WIDTH).astype(h.dtype) @ w_out

def swiglu_ffn(h, w_in, w_out):
    gate, up = jnp.split(h @ w_in, 2, axis=-1)
    return (jax.nn.silu(gate) * up) @ w_out

def setup_inputs(seed: int = 0) -> dict:
    key = jax.random.key(seed)
    ks = jax.random.split(key, 12)

    def dense(k, shape, fan_in):
        return jax.random.normal(k, shape, jnp.float32) * fan_in ** -0.5

    x = jax.random.normal(ks[0], (BATCH, SEQ, D_MODEL), jnp.float32)
    norm_gains = 1.0 + 0.05 * jax.random.normal(ks[1], (DEPTH, 4, D_MODEL), jnp.float32)
    att_w_in = dense(ks[2], (N_ATT_LAYERS, D_MODEL, ATT_IN_WIDTH), D_MODEL)
    att_lambda = 0.1 * jax.random.normal(ks[3], (N_ATT_LAYERS, 4, HEAD_DIM), jnp.float32)
    att_subln = 1.0 + 0.05 * jax.random.normal(ks[4], (N_ATT_LAYERS, DIFF_V_DIM), jnp.float32)
    att_w_out = dense(ks[5], (N_ATT_LAYERS, ATT_MIX_WIDTH, D_MODEL), ATT_MIX_WIDTH)
    rec_w_in = dense(ks[6], (N_REC_LAYERS, D_MODEL, REC_IN_WIDTH), D_MODEL)
    rec_lower_bounds = 0.5 * jax.random.normal(ks[7], (N_REC_LAYERS, HGRN_FORGET_WIDTH), jnp.float32)
    rec_gnorm = 1.0 + 0.05 * jax.random.normal(ks[8], (N_REC_LAYERS, HGRN_VAL_DIM), jnp.float32)
    rec_w_out = dense(ks[9], (N_REC_LAYERS, REC_MIX_WIDTH, D_MODEL), REC_MIX_WIDTH)
    ffn_w_in = dense(ks[10], (DEPTH, D_MODEL, 2 * FFN_HIDDEN), D_MODEL)
    ffn_w_out = dense(ks[11], (DEPTH, FFN_HIDDEN, D_MODEL), FFN_HIDDEN)
    return {'x': x, 'norm_gains': norm_gains, 'att_w_in': att_w_in, 'att_lambda': att_lambda,
            'att_subln': att_subln, 'att_w_out': att_w_out, 'rec_w_in': rec_w_in,
            'rec_lower_bounds': rec_lower_bounds, 'rec_gnorm': rec_gnorm, 'rec_w_out': rec_w_out,
            'ffn_w_in': ffn_w_in, 'ffn_w_out': ffn_w_out}

def reference(x, norm_gains, att_w_in, att_lambda, att_subln, att_w_out, rec_w_in,
              rec_lower_bounds, rec_gnorm, rec_w_out, ffn_w_in, ffn_w_out):
    cos, sin = rope_tables(x.shape[1], HEAD_DIM)
    lb_p = jax.nn.softmax(rec_lower_bounds.astype(jnp.float32), axis=0)
    lower_bounds = jnp.cumsum(lb_p, axis=0) - lb_p[0]
    for layer in range(DEPTH):
        gains = norm_gains[layer]
        j = layer // 2
        h = rms_norm(x, gains[0])
        if layer % 2 == 0:
            lambda_init = 0.8 - 0.6 * math.exp(-0.3 * layer)
            m = attention_mixer(h, att_w_in[j], att_lambda[j], att_subln[j], att_w_out[j],
                                lambda_init, cos, sin)
        else:
            m = hgrn2_mixer(h, rec_w_in[j], lower_bounds[j], rec_gnorm[j], rec_w_out[j])
        x = x + rms_norm(m, gains[1])
        h = rms_norm(x, gains[2])
        x = x + rms_norm(swiglu_ffn(h, ffn_w_in[layer], ffn_w_out[layer]), gains[3])
    return x


_drawn_inputs = setup_inputs


def setup_inputs(seed=0):
    import zlib

    import numpy as np

    out = dict(_drawn_inputs(seed))
    spreads = {}
    factors = {'att_lambda': 6.858}
    for name, (base, spread) in spreads.items():
        noise = np.random.default_rng([zlib.crc32(name.encode()), seed]).standard_normal(out[name].shape)
        drawn = base * np.exp(spread * noise) if base else spread * noise
        out[name] = jnp.asarray(drawn.astype(out[name].dtype))
    for name, factor in factors.items():
        out[name] = (out[name] * factor).astype(out[name].dtype)
    return out
```

```python
from contextlib import ExitStack

import numpy as np

import concourse.bass as bass
from concourse import mybir

P = 128
F32 = mybir.dt.float32
F32R = mybir.dt.float32r
U8 = mybir.dt.uint8
ALU = mybir.AluOpType
ACT = mybir.ActivationFunctionType
AXX = mybir.AxisListType.X

D = 1024
T = 512
KT = D // P
TT = T // P
HD = 64
SCALE = HD ** -0.5
FFN = 2816
FT = FFN // P
UC = 256
EPS = 1e-6
LAMBDA_INIT = 0.8 - 0.6 * float(np.exp(-0.3 * 0.0))
BIG = 1e30
CH = 128
LEVELS = (64, 32, 16, 8, 4, 2, 1)
NL = len(LEVELS)
EXP_LN = "natural_log_exp_and_others"

ATT_IN = 0
ATT_OUT = ATT_IN + 12
FFN_IN = (ATT_OUT + 4, ATT_OUT + 4 + 22 + 12 + 16 + 4)
FFN_OUT = (FFN_IN[0] + 22, FFN_IN[1] + 22)
REC_IN = FFN_OUT[0] + 12
REC_OUT = REC_IN + 16
UNITS = FFN_OUT[1] + 12

C_GAIN, C_SUB, C_GN, C_LB, C_ALL = 0, 64, 65, 66, 74


class Steps:

    def __init__(self, sem, names):
        self.sem, self.names, self.k = sem, names, 0
        self.at = {n: k + 1 for k, n in enumerate(names)}
        assert len(self.at) == len(names)

    def wait(self, eng, name, i=0):
        eng.wait_ge(self.sem, i * len(self.names) + self.at[name])

    def done(self, ins, name):
        assert self.names[self.k % len(self.names)] == name, (name, self.names[self.k % len(self.names)])
        self.k += 1
        ins.then_inc(self.sem, 1)


def trunk(nc, x, norm_gains, att_w_in, att_lambda, att_subln, att_w_out, rec_w_in,
          rec_lower_bounds, rec_gnorm, rec_w_out, ffn_w_in, ffn_w_out,
          cos_t, sin_t, mask_a, mask_b, ident_in, level_masks, out):
    with ExitStack() as ctx:
        def sb(name, shape, dt=F32):
            return ctx.enter_context(nc.sbuf_tensor(name, shape, dt))

        def sem(name):
            return ctx.enter_context(nc.semaphore(name))

        def phase(*items):
            with ExitStack() as e:
                return [e.enter_context(nc.sbuf_tensor(n, s, d)) for n, s, d in items]

        bank = [ctx.enter_context(nc.psum_tensor(f"bank{i}", [P, T], F32)) for i in range(8)]

        xres = sb("xres", [P, KT, T])
        act_hi = sb("act_hi", [P, KT, T], F32R)
        (act_lo,) = phase(("act_lo", [P, KT, T], F32R))
        mix_ffn = sb("mix_ffn", [P, KT, T])
        raw = sb("raw", [P, 2, 8, UC])
        whi = sb("whi", [P, 2, 8, UC], F32R)
        wlo = sb("wlo", [P, 2, 8, UC], F32R)
        ident = sb("ident", [P, P])
        ones = sb("ones", [P, P])
        eps_col = sb("eps_col", [P, 1])
        one_col = sb("one_col", [P, 1])
        pad = sb("pad", [P, 8])
        cols = sb("cols", [P, C_ALL])
        rB = sb("rB", [P, T])
        rM = sb("rM", [P, T])
        rT = sb("rT", [P, TT])
        ln_tmp = sb("ln_tmp", [P, T])
        lnT_tmp = sb("lnT_tmp", [P, TT])
        sq_ring = sb("sq_ring", [P, 2, T])
        xsq = sb("xsq", [P, T])
        (msq,) = (sb("msq", [P, T]),)

        rope, vtok, qk_st, mskA, mskB, cosr, sinr, rtmp = phase(
            ("rope", [P, 4, 2, 2, T], F32), ("vtok", [P, TT, D], F32),
            ("qk_st", [HD, 2, 2, T], F32), ("mskA", [P, T], F32), ("mskB", [P, T], F32),
            ("cosr", [P, T], F32), ("sinr", [P, T], F32), ("rtmp", [P, 2, 4, T], F32))
        (x_in, _v, _q, _ma, _mb, negs, prob, probT, o_st, rsum, nmax, rinv, osq, oss, lam_in,
         lam_s, colsrc) = phase(
             ("x_in", [P, 2, 2, 2, 2, T], F32), ("_v", [P, TT, D], F32), ("_q", [HD, 2, 2, T], F32),
             ("_ma", [P, T], F32), ("_mb", [P, T], F32),
             ("negs", [P, 4, T], F32), ("prob", [P, 4, T], F32), ("probT", [P, 2, T], F32),
             ("o_st", [P, 2, TT, P], F32), ("rsum", [P, 4, 4], F32), ("nmax", [P, 4, 4], F32),
             ("rinv", [P, 4, 4], F32), ("osq", [P, T], F32), ("oss", [P, 3, TT], F32),
             ("lam_in", [P, 4, HD], F32), ("lam_s", [P, 8], F32), ("colsrc", [P, P], F32))
        x_in = x_in[:, 0:1].rearrange("p a b c d t -> p (a b c d t)").rearrange("p (a b) -> p a b", a=TT)
        (mix_att,) = phase(("mix_att", [P, KT, T], F32))
        hid_hi, hid_lo, f_g, f_u = phase(
            ("hid_hi", [P, FT, T], F32R), ("hid_lo", [P, FT, T], F32R),
            ("f_g", [P, 2, T], F32), ("f_u", [P, T], F32))
        (y_out,) = phase(("y_out", [P, TT, D], F32))
        (rv, rmask, rzero, lb, ro, b_sb, e_sb, m_sb, qb_sb, ke_sb, keT, att, state, r_sq,
         r_rs, ebl, q_sb, k_sb) = phase(
             ("rv", [P, TT, D], F32), ("rmask", [P, NL, P], U8),
             ("rzero", [P, 2 * T], F32), ("lb", [P, 5, 8], F32), ("ro", [P, TT, D], F32),
             ("b_sb", [P, 2, T], F32), ("e_sb", [P, 2, 2, T], F32),
             ("m_sb", [P, 4, 2, T], F32), ("qb_sb", [P, 2, T], F32), ("ke_sb", [P, 2, T], F32),
             ("keT", [P, 2, 3, P], F32), ("att", [P, 2, T], F32), ("state", [P, 2, 3, P], F32),
             ("r_sq", [P, T], F32), ("r_rs", [P, 3, 8, TT], F32), ("ebl", [P, 2, TT], F32),
             ("q_sb", [P, 2, T], F32), ("k_sb", [P, 2, T], F32))
        (mix_rec,) = phase(("mix_rec", [P, KT, T], F32))
        gate, og = phase(
            ("_rv", [P, TT, D], F32), ("_rm", [P, NL, P], U8), ("_rz", [P, 2 * T], F32),
            ("_lb", [P, 5, 8], F32), ("_ro", [P, TT, D], F32), ("gate", [P, 2, TT, UC], F32),
            ("og", [P, 2, TT, UC], F32))[-2:]

        raw_in = [sem("raw_in0"), sem("raw_in1")]
        w_hi = sem("w_hi")
        w_lo = sem("w_lo")
        unit_done = sem("unit_done")
        x_in_sem = [sem(f"x_in{t}") for t in range(TT)]
        rmask_ready = sem("rmask_ready")
        ident_in_sem, small_in, rope_in, masks_in, rmask_in = (
            sem("ident_in"), sem("small_in"), sem("rope_in"), sem("masks_in"), sem("rmask_in"))
        setup = sem("setup")
        colsT, colsR = sem("colsT"), sem("colsR")
        lam_v, lam_a, lam_t = sem("lam_v"), sem("lam_a"), sem("lam_t")
        xT_done = sem("xT_done")
        x_new = sem("x_new")
        x_hi, x_lo = sem("x_hi"), sem("x_lo")
        x_sq, x_acc = sem("x_sq"), sem("x_acc")
        stat_mm, stat_ln, r_ready = sem("stat_mm"), sem("stat_ln"), sem("r_ready")
        m_evac, m_acc = sem("m_evac"), sem("m_acc")
        m_mm, m_ln, rM_ready, m_scaled = sem("m_mm"), sem("m_ln"), sem("rM_ready"), sem("m_scaled")
        rope_tab, rope_mul, rope_out, v_evac = (
            sem("rope_tab"), sem("rope_mul"), sem("rope_out"), sem("v_evac"))
        qk_in = [sem("qk_in0"), sem("qk_in1")]
        bsc_done, bneg_done, bp_done, bT_done, bT_act, bpv_done = (
            sem("bsc_done"), sem("bneg_done"), sem("bp_done"), sem("bT_done"), sem("bT_act"), sem("bpv_done"))
        sc_done, neg_done, p_done, pT_done = sem("sc_done"), sem("neg_done"), sem("p_done"), sem("pT_done")
        pT_act, pT_dve, pv_done, rinv_done, o_done = (
            sem("pT_act"), sem("pT_dve"), sem("pv_done"), sem("rinv_done"), sem("o_done"))
        oT_done, oa_hi, oa_lo = sem("oT_done"), sem("oa_hi"), sem("oa_lo")
        bw_done, bn_a, bn_v = sem("bw_done"), sem("bn_a"), sem("bn_v")
        yT_done, y_copied, y_out_sem = sem("yT_done"), sem("y_copied"), sem("y_out_sem")
        ffn_v = [sem("ffn_v0"), sem("ffn_v1")]
        ffn_a = [sem("ffn_a0"), sem("ffn_a1")]
        lb_v, lb_a = sem("lb_v"), sem("lb_a")
        rv_evac = sem("rv_evac")
        s_qf = sem("qf_evac")
        hg_v, hg_a, hg_p = sem("hg_v"), sem("hg_a"), sem("hg_p")
        hg_t, hg_s, hg_k, hg_o = sem("hg_t"), sem("hg_s"), sem("hg_k"), sem("hg_o")
        g_silu, g_mul, gT_done, gT_hi, gT_lo = (
            sem("g_silu"), sem("g_mul"), sem("gT_done"), sem("gT_hi"), sem("gT_lo"))
        rrs_a = sem("rrs_a")

        fview = lambda ap: ap.bitcast(F32)

        def weight_rows(w, k0, nk, col):
            return w.rearrange("(k p) n -> p k n", p=P)[:, k0:k0 + nk, bass.ds(col, UC)]

        def load(sp, pair, slot, src):
            if not (isinstance(pair, int) and pair == 0):
                sp.wait_ge(w_lo, pair * 2 + (slot - 1))
            nk = src.shape[1]
            sp.dma_start(raw[:, slot, 0:nk, :], src).then_inc(raw_in[slot], 16)

        def of_unit(w, slot, halves):
            if not halves:
                return w[:, slot, :, :]
            v = w[:, slot, :, :].rearrange("p k n -> p (k n)")
            if w is raw:
                return v.rearrange("p (kh a x) -> p a kh x", a=2, x=HD // 2)
            return v.rearrange("p (a kh x) -> p a kh x", a=2, x=HD // 2)

        def split_hi(act, pair, slot, halves=False):
            if isinstance(pair, int) and pair * 2 + slot >= UNITS:
                return
            if not (isinstance(pair, int) and pair == 0):
                act.wait_ge(unit_done, pair * 2 + (slot - 1))
            act.wait_ge(raw_in[slot], pair * 16 + 16)
            nc.scalar.activation(of_unit(whi, slot, halves), of_unit(raw, slot, halves), ACT.Copy).then_inc(w_hi, 1)

        def split_lo(dve, pair, slot, halves=False):
            if isinstance(pair, int) and pair * 2 + slot >= UNITS:
                return
            dve.wait_ge(w_hi, pair * 2 + slot + 1)
            nc.vector.tensor_tensor(of_unit(wlo, slot, halves), of_unit(raw, slot, halves),
                                    fview(of_unit(whi, slot, halves)), ALU.subtract).then_inc(w_lo, 1)

        def unit_features(pe, pair, slot, nk, hi, lo, banks, k0=0, first=True, last=True,
                          rope_cols=False, ready=None, free=None):
            pe.wait_ge(w_lo, pair * 2 + slot + 1)
            if free is not None:
                pe.wait_ge(*free)
            for k in range(nk):
                if ready is not None:
                    pe.wait_ge(ready[0], ready[1] + k0 + k + 1)
                for m in range(2):
                    if rope_cols:
                        pick = lambda w: w[:, slot].rearrange("p k n -> p (k n)")[:, (m * KT + k) * P:(m * KT + k + 1) * P]
                    else:
                        pick = lambda w: w[:, slot, k, m * P:(m + 1) * P]
                    o = bank[banks + m][:, :]
                    nc.tensor.matmul(o, pick(whi), hi[:, k0 + k, :], start=first and k == 0, stop=False)
                    nc.tensor.matmul(o, pick(whi), lo[:, k0 + k, :], start=False, stop=False)
                    mm = nc.tensor.matmul(o, pick(wlo), hi[:, k0 + k, :], start=False,
                                          stop=last and k == nk - 1)
            mm.then_inc(unit_done, 1)

        def unit_tokens(pe, pair, slot, banks, ready=None, free=None):
            pe.wait_ge(w_lo, pair * 2 + slot + 1)
            if free is not None:
                pe.wait_ge(*free)
            for k in range(KT):
                if ready is not None:
                    pe.wait_ge(ready[0], ready[1] + k + 1)
                for t in range(TT):
                    o = bank[banks + t // 2][:, (t % 2) * UC:(t % 2 + 1) * UC]
                    a_hi, a_lo = (a[:, k, t * P:(t + 1) * P] for a in (act_hi, act_lo))
                    nc.tensor.matmul(o, a_hi, whi[:, slot, k, :], start=k == 0 and t % 2 == 0,
                                     stop=False, skip_group_check=True)
                    nc.tensor.matmul(o, a_lo, whi[:, slot, k, :], start=False, stop=False,
                                     skip_group_check=True)
                    mm = nc.tensor.matmul(o, a_hi, wlo[:, slot, k, :], start=False,
                                          stop=k == KT - 1, skip_group_check=True)
            mm.then_inc(unit_done, 1)

        def gain(row, c):
            return cols[:, C_GAIN + row * KT + c:C_GAIN + row * KT + c + 1]

        def tile_act(act, b, c):
            act.wait_ge(x_new, KT * b + c + 1)
            nc.scalar.activation(act_hi[:, c, :], xres[:, c, :], ACT.Copy, scale=gain(2 * b, c)).then_inc(x_hi, 1)
            if c >= 3:
                act.wait_ge(x_acc, 7 * b + c - 2)
            dst = xsq[:, :] if c == 0 else sq_ring[:, c % 2, :]
            nc.scalar.activation(dst, xres[:, c, :], ACT.Square).then_inc(x_sq, 1)

        def tile_lo(dve, b, c):
            dve.wait_ge(x_hi, KT * b + c + 1)
            nc.vector.scalar_tensor_tensor(out=act_lo[:, c, :], in0=xres[:, c, :], scalar=gain(2 * b, c),
                                           in1=fview(act_hi[:, c, :]), op0=ALU.mult,
                                           op1=ALU.subtract).then_inc(x_lo, 1)

        def squares_pool(pool, b):
            for c in range(1, KT):
                pool.wait_ge(x_sq, KT * b + c + 1)
                if c > 1:
                    pool.wait_ge(x_acc, 7 * b + c - 1)
                nc.gpsimd.tensor_tensor(xsq[:, :], xsq[:, :], sq_ring[:, c % 2, :], ALU.add).then_inc(x_acc, 1)

        def stat_pe(pe, b):
            pe.wait_ge(x_acc, 7 * (b + 1))
            nc.tensor.matmul(bank[4][:, :], ones[:, :], xsq[:, :], start=True, stop=True)
            for t in range(TT):
                mm = nc.tensor.matmul(bank[5][:, t:t + 1], xsq[:, t * P:(t + 1) * P], ones[:, 0:1],
                                      start=True, stop=True)
            mm.then_inc(stat_mm, 1)

        def stat_act(act, b):
            act.wait_ge(stat_mm, b + 1)
            nc.scalar.activation(ln_tmp[:, :], bank[4][:, :], ACT.Ln, scale=1.0 / D, bias=eps_col[:, :])
            nc.scalar.activation(lnT_tmp[:, :], bank[5][:, 0:TT], ACT.Ln, scale=1.0 / D,
                                 bias=eps_col[:, :]).then_inc(stat_ln, 1)
            act.wait_ge(stat_ln, b + 1)
            nc.scalar.activation(rB[:, :], ln_tmp[:, :], ACT.Exp, scale=-0.5)
            nc.scalar.activation(rT[:, :], lnT_tmp[:, :], ACT.Exp, scale=-0.5).then_inc(r_ready, 1)

        def mixer_evac_act(act, b, mix, unit, tile, banks):
            act.wait_ge(unit_done, unit + 1)
            for m in range(2):
                if not (isinstance(tile, int) and tile == 0):
                    act.wait_ge(m_acc, tile + (9 * (b - 1) + m))
                nc.scalar.activation(mix[:, bass.ds(tile + m, 1), :].rearrange("p a t -> p (a t)"),
                                     bank[banks + m][:, :], ACT.Copy)
                nc.scalar.activation(sq_ring[:, m, :], bank[banks + m][:, :], ACT.Square).then_inc(m_evac, 1)

        def mixer_zero_dve(dve, b):
            if b > 1:
                dve.wait_ge(m_mm, b - 1)
            nc.vector.memset(msq[:, :], 0.0).then_inc(m_acc, 1)

        def mixer_sum_dve(dve, b, tile):
            for m in range(2):
                dve.wait_ge(m_evac, tile + (KT * (b - 1) + m + 1))
                dve.wait_ge(m_acc, tile + (9 * (b - 1) + m + 1))
                nc.vector.tensor_tensor(msq[:, :], msq[:, :], sq_ring[:, m, :], ALU.add).then_inc(m_acc, 1)

        def post_pe(pe, b):
            pe.wait_ge(m_acc, 9 * b)
            nc.tensor.matmul(bank[4][:, :], ones[:, :], msq[:, :], start=True, stop=True).then_inc(m_mm, 1)

        def post_act(act, b):
            act.wait_ge(m_mm, b)
            nc.scalar.activation(ln_tmp[:, :], bank[4][:, :], ACT.Ln, scale=1.0 / D,
                                 bias=eps_col[:, :]).then_inc(m_ln, 1)
            act.wait_ge(m_ln, b)
            nc.scalar.activation(rM[:, :], ln_tmp[:, :], ACT.Exp, scale=-0.5).then_inc(rM_ready, 1)
            if b < 4:
                for c in range(KT):
                    tile_act(act, b, c)

        def post_dve(dve, b, mix):
            dve.wait_ge(rM_ready, b)
            for c in range(KT + 2):
                if c < KT:
                    nc.vector.scalar_tensor_tensor(out=mix[:, c, :], in0=mix[:, c, :], scalar=gain(2 * b - 1, c),
                                                   in1=rM[:, :], op0=ALU.mult, op1=ALU.mult).then_inc(m_scaled, 1)
                if 1 <= c <= KT:
                    dve.wait_ge(m_scaled, KT * (b - 1) + c)
                    nc.vector.tensor_tensor(xres[:, c - 1, :], xres[:, c - 1, :], mix[:, c - 1, :],
                                            ALU.add).then_inc(x_new, 1)
                if c >= 2 and b < 4:
                    tile_lo(dve, b, c - 2)

        block = ctx.enter_context(nc.Block())

        @block.sync
        def _(sp):
            for t in range(TT):
                sp.dma_start(x_in[:, t, :], x[0, t * P:(t + 1) * P, :]).then_inc(x_in_sem[t], 16)
            w = att_w_in[0]
            for pair, (a, b) in enumerate(((0, 512), (256, 768), (1536, 2048), (1792, 2304),
                                           (1024, 1280), (2560, 2816))):
                load(sp, pair, 0, weight_rows(w, 0, KT, a))
                load(sp, pair, 1, weight_rows(w, 0, KT, b))
            load(sp, ATT_OUT // 2, 0, weight_rows(att_w_out[0], 0, KT, 0))
            load(sp, ATT_OUT // 2, 1, weight_rows(att_w_out[0], 0, KT, UC))
            def stage(r, pair):
                for half in range(2):
                    sp.dma_start(
                        qk_st[32 * half:32 * half + 32, r % 2, :, :],
                        rope[32 * r:32 * r + 32, bass.ds(pair, 1), :, half, :]
                        .rearrange("p a q t -> p (a q) t")).then_inc(qk_in[r % 2], 16)

            sp.wait_ge(rope_out, 16)
            stage(0, 0)
            stage(1, 0)
            with sp.Fori(0, 2) as g:
                for n, r in enumerate((2, 3, 0, 1)):
                    sp.wait_ge(sc_done, g * 16 + 4 * (n + 1))
                    stage(r, g + (1 if n >= 2 else 0))
            for h in range(10, 16):
                sp.wait_ge(bsc_done, 8 * ((h - 10) // 2) + 7 + h % 2)
                stage(h % 4, h // 4)
            load(sp, ATT_OUT // 2 + 1, 0, weight_rows(att_w_out[0], 0, KT, 2 * UC))
            load(sp, ATT_OUT // 2 + 1, 1, weight_rows(att_w_out[0], 0, KT, 3 * UC))
            for layer in range(2):
                w1, w2 = ffn_w_in[layer], ffn_w_out[layer]
                with sp.Fori(0, FFN // UC) as i:
                    load(sp, i + FFN_IN[layer] // 2, 0, weight_rows(w1, 0, KT, i * UC))
                    load(sp, i + FFN_IN[layer] // 2, 1, weight_rows(w1, 0, KT, i * UC + FFN))
                with sp.Fori(0, 2) as i:
                    for v in range(6):
                        m, kc = divmod(v, 3)
                        load(sp, i * 3 + (FFN_OUT[layer] // 2 + v // 2), v % 2,
                             weight_rows(w2, 8 * kc, min(8, FT - 8 * kc), i * (2 * UC) + m * UC))
                if layer == 0:
                    w = rec_w_in[0]
                    with sp.Fori(0, 2) as i:
                        for s in range(2):
                            load(sp, i + REC_IN // 2, s, weight_rows(w, 0, KT, i * (2 * UC) + (2 * D + s * UC)))
                    sp.wait_ge(m_mm, 2)
                    sp.dma_start(qb_sb[:, :, :].rearrange("p a t -> p (a t)")[:, 0:NL * P], level_masks).then_inc(rmask_in, 16)
                    with sp.Fori(0, 4) as i:
                        for s in range(2):
                            load(sp, i + (REC_IN // 2 + 2), s, weight_rows(w, 0, KT, i * UC + s * D))
                    with sp.Fori(0, 2) as i:
                        for s in range(2):
                            load(sp, i + (REC_IN // 2 + 6), s, weight_rows(w, 0, KT, i * (2 * UC) + (3 * D + s * UC)))
                    with sp.Fori(0, 2) as i:
                        for s in range(2):
                            load(sp, i + REC_OUT // 2, s, weight_rows(rec_w_out[0], 0, KT, i * (2 * UC) + s * UC))
            for half in range(2):
                sp.wait_ge(y_copied, 4 * half + 4)
                cs = slice(half * T, half * T + T)
                sp.dma_start(out[0].rearrange("(a p) d -> p a d", p=P)[:, :, cs], y_out[:, :, cs]).then_inc(y_out_sem, 16)
            sp.wait_ge(y_out_sem, 32)

        H_STEPS_T = ["keT0", "keT1", "diag0", "diag1"] + [f"lev{l}_{a}" for l in range(NL) for a in range(2)] \
            + ["u0", "u1", "o0", "o1"]
        H_STEPS_S = ["diag0", "diag1"] + [f"lev{l}_{a}" for l in range(NL) for a in range(2)]
        EV = ["qgate", "forget", "key", "scan", "dke", "d0", "qb", "ke", "d1", "mq0", "d2", "mq1", "d3",
              "mq2", "mq3", "d4", "d5", "mq4", "d6", "mq5", "mq6"]
        EA = ["qe", "ql", "qs", "fe", "fl", "fs", "g", "eb", "ebl", "eke"] \
            + [f"{x}{l}" for l in range(NL) for x in ("et", "es")]
        ev, ea = Steps(hg_v, EV), Steps(hg_a, EA)
        ep = Steps(hg_p, [f"mk{l}" for l in range(NL)])
        ht, hs = Steps(hg_t, H_STEPS_T), Steps(hg_s, H_STEPS_S)
        hk = Steps(hg_k, ["keT0", "keT1", "ocopy0", "osq0", "ocopy1", "osq1"])
        ho = Steps(hg_o, [f"s{c}_{a}" for a in range(2) for c in range(1, 4)] + ["ss0", "ss1"])

        qf = REC_IN // 2 + 2
        bw = Steps(bw_done, ["rinv", "lrinv", "scaled", "w"])
        bn = Steps(bn_v, ["ss", "o"])
        bna = Steps(bn_a, ["sq", "ln", "r"])
        FV = ["g0", "g1", "u0", "h0", "u1", "h1", "lo0", "lo1"]
        FA = ["s0", "s1", "hi0", "hi1"]
        fvs = [Steps(v, FV) for v in ffn_v]
        fas = [Steps(v, FA) for v in ffn_a]

        def a_pT_wait(eng, g, n):
            r, i = divmod(n, 4)
            if i == 3:
                eng.wait_ge(pT_dve, g * 4 + (r + 1))
            else:
                eng.wait_ge(pT_act, g * 12 + (3 * r + i + 1))

        @block.tensor
        def _(pe):
            mm = nc.tensor.matmul
            tr = nc.tensor.transpose
            pe.wait_ge(ident_in_sem, 16)
            pe.wait_ge(small_in, 16 * 5)
            tr(bank[7][:, 0:C_ALL], colsrc[0:C_ALL, :], ident[0:C_ALL, 0:C_ALL]).then_inc(colsT, 1)
            for c in range(KT):
                if c >= 4:
                    pe.wait_ge(x_new, c - 3)
                for t in range(TT):
                    if c == 0:
                        pe.wait_ge(x_in_sem[t], 16)
                    last = tr(bank[c % 4][:, t * P:(t + 1) * P], x_in[:, t, c * P:(c + 1) * P], ident[:, :])
                last.then_inc(xT_done, 1)
            pe.wait_ge(setup, 1)
            pe.wait_ge(lam_v, 3)
            mm(bank[6][:, 0:1], ones[0:1, :], lam_s[0:1, 4:5], start=True, stop=True).then_inc(lam_t, 1)

            def qk_pair(p):
                for s in range(2):
                    first = isinstance(p, int) and p == 0
                    unit_features(pe, p, s, KT, act_hi, act_lo, 2 * s, rope_cols=True,
                                  ready=(x_lo, 0) if first and s == 0 else None,
                                  free=(x_new, 8) if first else (rope_mul, p * 2 + (s - 1)))
                    if first and s == 0:
                        stat_pe(pe, 0)
            qk_pair(0)
            with pe.Fori(1, 4) as p:
                qk_pair(p)
            for s in range(4):
                unit_tokens(pe, 4 + s // 2, s % 2, 2 * (s % 2),
                            free=(rope_mul, 7 + s) if s < 2 else (v_evac, s - 1))


            def a_scores(g, n):
                r, i = divmod(n, 4)
                if i == 0:
                    pe.wait_ge(qk_in[r % 2], g * 64 + 32 * (r // 2 + 1))
                if n >= 2:
                    pe.wait_ge(neg_done, g * 16 + (n - 1))
                mm(bank[n % 2][:, 0:(i + 1) * P], qk_st[:, r % 2, 0, i * P:(i + 1) * P],
                   qk_st[:, r % 2, 1, 0:(i + 1) * P], start=True, stop=True).then_inc(sc_done, 1)

            def a_transposes(g, n):
                i = n % 4
                pe.wait_ge(p_done, g * 16 + (n + 1))
                if n >= 2:
                    a_pT_wait(pe, g, n - 2)
                for k in range(i + 1):
                    last = tr(bank[2 + n % 2][:, k * P:(k + 1) * P], prob[:, n % 4, k * P:(k + 1) * P], ident[:, :])
                last.then_inc(pT_done, 1)

            def a_values(g, n):
                r, i = divmod(n, 4)
                a_pT_wait(pe, g, n)
                if i == 0 and r >= 2:
                    pe.wait_ge(o_done, g * 4 + (r - 1))
                for k in range(i + 1):
                    last = mm(bank[4 + r % 2][:, i * HD:(i + 1) * HD], probT[:, n % 2, k * P:(k + 1) * P],
                              vtok[:, k, bass.ds(g * UC + r * HD, HD)], start=k == 0, stop=k == i)
                last.then_inc(pv_done, 1)

            def o_transposes(slot, b):
                for i in range(TT):
                    last = tr(bank[b][:, i * P:(i + 1) * P], o_st[:, slot, i, :], ident[:, :])
                last.then_inc(oT_done, 1)

            pe.wait_ge(v_evac, 4)
            with pe.Fori(0, 2) as g:
                for n in range(16 + 3):
                    if n < 16:
                        a_scores(g, n)
                    if 2 <= n < 18:
                        a_transposes(g, n - 2)
                    if n >= 3:
                        a_values(g, n - 3)
                for h in range(2):
                    pe.wait_ge(o_done, g * 4 + (2 * h + 2))
                    o_transposes(h, 6 + h)
                pe.wait_ge(oa_lo, g * 2 + 2)

            def b_scores(g, n):
                q, i = divmod(n, 4)
                for s in range(2):
                    if i == 0:
                        pe.wait_ge(qk_in[s], g * 64 + (128 + 32 * (q + 1)))
                    if n >= 2:
                        pe.wait_ge(bneg_done, g * 16 + (2 * (n - 2) + s + 1))
                    mm(bank[2 * (n % 2) + s][:, 0:(i + 1) * P], qk_st[:, s, 0, i * P:(i + 1) * P],
                       qk_st[:, s, 1, 0:(i + 1) * P], start=True, stop=True).then_inc(bsc_done, 1)

            def b_transposes(g, n):
                i = n % 4
                bw.wait(pe, "w", g * 8 + n)
                if n >= 2:
                    pe.wait_ge(bT_act, g * 8 + (n - 1))
                for k in range(i + 1):
                    last = tr(bank[4 + n % 2][:, k * P:(k + 1) * P], prob[:, 2 * (n % 2), k * P:(k + 1) * P], ident[:, :])
                last.then_inc(bT_done, 1)

            def b_values(g, n):
                q, i = divmod(n, 4)
                pe.wait_ge(bT_act, g * 8 + (n + 1))
                for k in range(i + 1):
                    last = mm(bank[6 + q][:, i * P:(i + 1) * P], probT[:, n % 2, k * P:(k + 1) * P],
                              vtok[:, k, bass.ds(g * UC + (512 + q * P), P)], start=k == 0, stop=k == i)
                last.then_inc(bpv_done, 1)

            with pe.Fori(0, 2) as g:
                for n in range(8 + 3):
                    if n < 8:
                        b_scores(g, n)
                    if 2 <= n < 10:
                        b_transposes(g, n - 2)
                    if n >= 3:
                        b_values(g, n - 3)
                for q in range(2):
                    bn.wait(pe, "o", g * 2 + q)
                    o_transposes(q, 4 + q)
                pe.wait_ge(oa_lo, g * 2 + 6)

            def out_projection(base, ready, b):
                for u in range(4):
                    unit_features(pe, base // 2 + u // 2, u % 2, KT, act_hi, act_lo, 2 * (u % 2),
                                  ready=ready if u == 0 else None,
                                  free=(m_evac, KT * (b - 1) + 2 * (u - 1)) if u >= 2 else None)
                post_pe(pe, b)

            def ffn(layer):
                b = 1 + 2 * layer
                fv = fvs[layer]

                def pair(i):
                    peeled = isinstance(i, int)
                    for s in range(2):
                        unit_features(pe, i + FFN_IN[layer] // 2, s, KT, act_hi, act_lo, 2 * s,
                                      ready=(x_lo, KT * b) if peeled and s == 0 else None,
                                      free=None if peeled else (fv.sem, i * len(fv.names) - (len(fv.names) - fv.at["g1" if s == 0 else "u1"])))
                        if peeled and s == 0:
                            stat_pe(pe, b)
                pair(0)
                with pe.Fori(1, FFN // UC) as i:
                    pair(i)
                with pe.Fori(0, 2) as i:
                    for v in range(6):
                        m, kc = divmod(v, 3)
                        nk = min(8, FT - 8 * kc)
                        if kc == 0:
                            fv.wait(pe, "u1", FFN // UC - 1)
                            if m == 0:
                                pe.wait_ge(m_evac, i * 4 + KT * b - 2) if b else None
                            else:
                                pe.wait_ge(m_evac, i * 4 + KT * b)
                        fv.wait(pe, "lo1", (8 * kc + nk) // 2 - 1)
                        unit_features(pe, i * 3 + (FFN_OUT[layer] // 2 + v // 2), v % 2, nk, hid_hi, hid_lo,
                                      2 * m, k0=8 * kc, first=kc == 0, last=kc == 2)
                post_pe(pe, b + 1)

            out_projection(ATT_OUT, (oa_lo, 0), 1)
            ffn(0)

            for u in range(4):
                unit_tokens(pe, REC_IN // 2 + u // 2, u % 2, 2 * (u % 2),
                            ready=(x_lo, 2 * KT) if u == 0 else None,
                            free=(rv_evac, u - 1) if u >= 2 else (m_evac, 2 * KT))
                if u == 0:
                    stat_pe(pe, 2)

            def qf_pair(j):
                for s in range(2):
                    unit_features(pe, j + (REC_IN // 2 + 2), s, KT, act_hi, act_lo, 2 * s,
                                  free=(rv_evac, 3 + s) if isinstance(j, int) else (s_qf, j * 2 + (s - 1)))

            def heads(j):
                for a in range(2):
                    ev.wait(pe, "ke", j)
                    for c in range(3):
                        last = tr(bank[4 + a][:, c * P:(c + 1) * P], ke_sb[:, a, c * P:(c + 1) * P], ident[:, :])
                    ht.done(last, f"keT{a}")
                for a in range(2):
                    for c in range(TT):
                        cs = slice(c * P, (c + 1) * P)
                        last = mm(bank[6 + a][:, cs], k_sb[:, a, cs], q_sb[:, a, cs], start=True, stop=True)
                    ht.done(last, f"diag{a}")
                for l in range(NL):
                    for a in range(2):
                        if a == 0:
                            ev.wait(pe, f"mq{l}", j)
                            ep.wait(pe, f"mk{l}", j)
                        hs.wait(pe, f"diag{a}" if l == 0 else f"lev{l - 1}_{a}", j)
                        for c in range(TT):
                            m = m_sb[:, l % 4, a, c * P:(c + 1) * P]
                            last = mm(bank[6 + a][:, c * P:(c + 1) * P], m, m, start=True, stop=True)
                        ht.done(last, f"lev{l}_{a}")
                for a in range(2):
                    hk.wait(pe, f"keT{a}", j)
                    for c in range(3):
                        last = mm(bank[4 + a][:, c * P:(c + 1) * P], keT[:, a, c, :],
                                  rv[:, c, bass.ds(j * UC + a * P, P)], start=True, stop=True)
                    ht.done(last, f"u{a}")
                for a in range(2):
                    hs.wait(pe, f"lev{NL - 1}_{a}", j)
                    ho.wait(pe, f"s3_{a}", j)
                    for c in range(TT):
                        cs = slice(c * P, (c + 1) * P)
                        last = mm(bank[6 + a][:, cs], att[:, a, cs], rv[:, c, bass.ds(j * UC + a * P, P)],
                                  start=True, stop=c == 0)
                        if c:
                            last = mm(bank[6 + a][:, cs], qb_sb[:, a, cs], state[:, a, c - 1, :],
                                      start=False, stop=True)
                    ht.done(last, f"o{a}")
                hk.wait(pe, "osq1", j)

            def gates(u, free):
                unit_tokens(pe, REC_IN // 2 + 6 + u // 2, u % 2, 2 * (u % 2), free=free)

            def gated_transposes(u):
                pe.wait_ge(g_mul, 8 * (u + 1))
                for h in range(2):
                    if 2 * u + h >= 2:
                        pe.wait_ge(gT_lo, 2 * u + h - 1)
                    for t in range(TT):
                        last = tr(bank[4 + h][:, t * P:(t + 1) * P], og[:, u % 2, t, h * P:(h + 1) * P], ident[:, :])
                    last.then_inc(gT_done, 1)

            qf_pair(0)
            with pe.Fori(1, 4) as j:
                qf_pair(j)
                heads(j - 1)
            gates(0, (s_qf, 8))
            gates(1, None)
            heads(3)
            gates(2, (g_silu, 4))
            gates(3, (g_silu, 8))
            for u in range(4):
                gated_transposes(u)
            out_projection(REC_OUT, (gT_lo, 0), 3)
            ffn(1)
            for c in range(KT):
                pe.wait_ge(x_new, 4 * KT + c + 1)
                b = (0, 1, 2, 3, 5, 6, 7, 4)[c]
                for t in range(TT):
                    last = tr(bank[b][:, t * P:(t + 1) * P], xres[:, c, t * P:(t + 1) * P], ident[:, :])
                last.then_inc(yT_done, 1)

        @block.gpsimd
        def _(pool):
            g = nc.gpsimd
            g.memset(ones[:, :], 1.0)
            g.memset(eps_col[:, :], EPS)
            g.memset(one_col[:, :], 1.0).then_inc(setup, 1)
            squares_pool(pool, 0)

            def rope_add(p):
                for s in range(2):
                    dst = rope[:, bass.ds(p, 1), s, :, :].rearrange("p a h t -> p (a h) t")
                    pool.wait_ge(rope_mul, p * 2 + (s + 1))
                    g.tensor_tensor(dst[:, 0, :], rtmp[:, s, 0, :], rtmp[:, s, 1, :], ALU.subtract).then_inc(rope_out, 1)
                    g.tensor_tensor(dst[:, 1, :], rtmp[:, s, 2, :], rtmp[:, s, 3, :], ALU.add).then_inc(rope_out, 1)
            with pool.Fori(0, 4) as p:
                rope_add(p)
            squares_pool(pool, 1)
            pool.wait_ge(m_mm, 2)
            g.memset(rzero[:, :], 1.0).then_inc(setup, 1)
            pool.wait_ge(setup, 2)
            g.memset(rzero[:, :].rearrange("p (c t) -> p c t", t=CH)[:, :, 0:1], 0.0).then_inc(setup, 1)
            squares_pool(pool, 2)

            def level_keys(j):
                for l, L in enumerate(LEVELS):
                    ea.wait(pool, f"es{l}", j)
                    if l >= 4:
                        ht.wait(pool, f"lev{l - 4}_1", j)
                    elif not isinstance(j, int):
                        ht.wait(pool, f"lev{l + 4 if l < 3 else 3}_1", j - 1)
                    v = lambda ap: ap.rearrange("p a t -> p (a t)").rearrange("p (b h t) -> p b h t", h=2, t=L)[:, :, 0, :]
                    ep.done(g.tensor_tensor(v(m_sb[:, l % 4]), v(e_sb[:, l % 2]), v(k_sb[:, :, :]), ALU.mult), f"mk{l}")
            level_keys(0)
            with pool.Fori(1, 4) as j:
                level_keys(j)
            squares_pool(pool, 3)

        @block.scalar
        def _(act):
            A = nc.scalar.activation
            act.preload_act_table_set(EXP_LN)
            act.dma_start(ident[:, :], ident_in).then_inc(ident_in_sem, 16)
            act.dma_start(colsrc[C_GAIN:C_GAIN + 64, :], norm_gains.rearrange("l n (k p) -> (l n k) p", p=P)).then_inc(small_in, 16)
            act.dma_start(colsrc[C_SUB:C_SUB + 1, :], att_subln).then_inc(small_in, 16)
            act.dma_start(colsrc[C_GN:C_GN + 1, :], rec_gnorm).then_inc(small_in, 16)
            act.dma_start(colsrc[C_LB:C_LB + 8, :], rec_lower_bounds.rearrange("a (h p) -> (a h) p", p=P)).then_inc(small_in, 16)
            act.dma_start(lam_in[0:1, :, :], att_lambda).then_inc(small_in, 16)
            act.dma_start(cosr[:, :], cos_t).then_inc(rope_in, 16)
            act.dma_start(sinr[:, :], sin_t).then_inc(rope_in, 16)
            act.dma_start(mskA[:, :], mask_a).then_inc(masks_in, 16)
            act.dma_start(mskB[:, :], mask_b).then_inc(masks_in, 16)
            act.wait_ge(colsT, 1)
            A(cols[:, :], bank[7][:, 0:C_ALL], ACT.Copy).then_inc(colsR, 1)
            act.wait_ge(colsR, 1)
            for c in range(KT):
                tile_act(act, 0, c)
                if c == 1:
                    split_hi(act, 0, 0, True)
            act.wait_ge(lam_v, 2)
            A(lam_s[0:1, 2:4], lam_s[0:1, 0:2], ACT.Exp).then_inc(lam_a, 1)

            split_hi(act, 0, 1, True)
            stat_act(act, 0)
            split_hi(act, 1, 0, True)
            with act.Fori(1, 3) as p:
                split_hi(act, p, 1, True)
                split_hi(act, p + 1, 0, True)
            split_hi(act, 3, 1, True)
            split_hi(act, 4, 0)

            def tokens_evac(u, unit, dst, base, count, stat):
                act.wait_ge(r_ready, stat + 1)
                act.wait_ge(unit_done, unit + 1)
                for t in range(TT):
                    last = A(dst[:, t, base:base + UC], bank[2 * (u % 2) + t // 2][:, (t % 2) * UC:(t % 2 + 1) * UC],
                             ACT.Copy, scale=rT[:, t:t + 1])
                last.then_inc(count, 1)
            for u in range(4):
                pair = 4 + u // 2
                if u % 2 == 0:
                    split_hi(act, pair, 1)
                tokens_evac(u, 8 + u, vtok, u * UC, v_evac, 0)
                if u % 2 == 0:
                    split_hi(act, pair + 1, 0)

            def a_exp(g, n):
                r, i = divmod(n, 4)
                act.wait_ge(neg_done, g * 16 + (n + 1))
                if n >= 4:
                    act.wait_ge(pT_done, g * 16 + (n - 3))
                A(prob[:, n % 4, 0:(i + 1) * P], negs[:, n % 2, 0:(i + 1) * P], ACT.Exp, scale=-1.0,
                  bias=nmax[:, r, i:i + 1], accum_out=rsum[:, r, i:i + 1]).then_inc(p_done, 1)

            def a_pT(g, n):
                i = n % 4
                act.wait_ge(pT_done, g * 16 + (n + 1))
                if n >= 2:
                    act.wait_ge(pv_done, g * 16 + (n - 1))
                A(probT[:, n % 2, 0:(i + 1) * P], bank[2 + n % 2][:, 0:(i + 1) * P], ACT.Copy).then_inc(pT_act, 1)

            def o_hi(c, b, count, scale=1.0):
                act.wait_ge(oT_done, count)
                A(act_hi[:, bass.ds(c, 1), :].rearrange("p a t -> p (a t)"), bank[b][:, :], ACT.Copy,
                  scale=scale).then_inc(oa_hi, 1)

            with act.Fori(0, 2) as g:
                for n in range(16 + 2):
                    if n < 16:
                        a_exp(g, n)
                    if n >= 2 and (n - 2) % 4 != 3:
                        a_pT(g, n - 2)
                for h in range(2):
                    o_hi(g * 2 + h, 6 + h, g * 2 + (h + 1))

            def b_exp(g, n):
                q, i = divmod(n, 4)
                for s in range(2):
                    act.wait_ge(bneg_done, g * 16 + (2 * n + s + 1))
                    if n >= 2:
                        act.wait_ge(bT_done, g * 8 + (n - 1))
                    A(prob[:, 2 * (n % 2) + s, 0:(i + 1) * P], negs[:, 2 * (n % 2) + s, 0:(i + 1) * P], ACT.Exp, scale=-1.0,
                      bias=nmax[:, 2 * q + s, i:i + 1], accum_out=rsum[:, 2 * q + s, i:i + 1]).then_inc(bp_done, 1)

            def b_pT(g, n):
                i = n % 4
                act.wait_ge(bT_done, g * 8 + (n + 1))
                if n >= 2:
                    act.wait_ge(bpv_done, g * 8 + (n - 1))
                A(probT[:, n % 2, 0:(i + 1) * P], bank[4 + n % 2][:, 0:(i + 1) * P], ACT.Copy).then_inc(bT_act, 1)

            def b_norm(g, q):
                act.wait_ge(bpv_done, g * 8 + 4 * (q + 1))
                bna.done(A(osq[:, :], bank[6 + q][:, :], ACT.Square), "sq")
                bn.wait(act, "ss", g * 2 + q)
                bna.done(A(oss[:, 1, :], oss[:, 0, :], ACT.Ln, scale=1.0 / P, bias=eps_col[:, :]), "ln")
                bna.wait(act, "ln", g * 2 + q)
                bna.done(A(oss[:, 2, :], oss[:, 1, :], ACT.Exp, scale=-0.5), "r")

            with act.Fori(0, 2) as g:
                for n in range(8 + 3):
                    if n < 8:
                        b_exp(g, n)
                    if 2 <= n < 10:
                        b_pT(g, n - 2)
                    if n in (7, 10):
                        b_norm(g, (n - 7) // 3)
                for q in range(2):
                    o_hi(g * 2 + (4 + q), 4 + q, g * 2 + (5 + q), scale=lam_s[:, 6:7])

            def out_projection(base, b, mix):
                for u in range(4):
                    if u % 2 == 0:
                        split_hi(act, base // 2 + u // 2, 1)
                    mixer_evac_act(act, b, mix, base + u, 2 * u, 2 * (u % 2))
                    if u % 2 == 0:
                        split_hi(act, base // 2 + u // 2 + 1, 0)
                post_act(act, b)

            def ffn(layer):
                b = 1 + 2 * layer
                fv, fa = fvs[layer], fas[layer]
                base = FFN_IN[layer] // 2

                def pair(i):
                    split_hi(act, i + base, 1)
                    if isinstance(i, int):
                        stat_act(act, b)
                    for m in range(2):
                        fv.wait(act, f"g{m}", i)
                        fa.done(A(f_g[:, m, :], f_g[:, m, :], ACT.Silu), f"s{m}")
                    split_hi(act, i + (base + 1), 0)
                    for m in range(2):
                        fv.wait(act, f"h{m}", i)
                        fa.done(A(hid_hi[:, bass.ds(i * 2 + m, 1), :].rearrange("p a t -> p (a t)"),
                                  f_g[:, m, :], ACT.Copy), f"hi{m}")
                pair(0)
                with act.Fori(1, FFN // UC) as i:
                    pair(i)
                act.preload_act_table_set(EXP_LN)
                base = FFN_OUT[layer] // 2

                def six_units(i):
                    for v in range(6):
                        m, kc = divmod(v, 3)
                        if v % 2 == 0:
                            split_hi(act, i * 3 + (base + v // 2), 1)
                        if kc == 2:
                            mixer_evac_act(act, b + 1, mix_ffn, i * 6 + (FFN_OUT[layer] + v), i * 4 + 2 * m, 2 * m)
                        if v % 2 == 0:
                            split_hi(act, i * 3 + (base + v // 2 + 1), 0)
                if layer == 0:
                    with act.Fori(0, 2) as i:
                        six_units(i)
                else:
                    six_units(0)
                    six_units(1)
                post_act(act, b + 1)

            out_projection(ATT_OUT, 1, mix_att)
            ffn(0)

            for u in range(4):
                pair = REC_IN // 2 + u // 2
                if u % 2 == 0:
                    split_hi(act, pair, 1)
                if u == 0:
                    stat_act(act, 2)
                    act.wait_ge(lb_v, 1)
                    A(lb[:, 1, :], lb[:, 0, :], ACT.Exp).then_inc(lb_a, 1)
                tokens_evac(u, REC_IN + u, rv, u * UC, rv_evac, 2)
                if u % 2 == 0:
                    split_hi(act, pair + 1, 0)

            flat = lambda ap: ap.rearrange("p a t -> p (a t)")
            blocks = lambda ap, L: flat(ap).rearrange("p (b h t) -> p b h t", h=2, t=L)

            def level_exps(j, ls):
                for l in ls:
                    ev.wait(act, f"d{l}", j)
                    for x, h, sgn in (("et", 1, 1.0), ("es", 0, -1.0)):
                        v = blocks(e_sb[:, l % 2], LEVELS[l])[:, :, h, :]
                        ea.done(A(v, v, ACT.Exp, scale=sgn), f"{x}{l}")

            def gates_and_decays(j):
                for x, src, e, s in (("q", q_sb, 0, 1), ("f", k_sb, 1, 2)):
                    v = flat(e_sb[:, e])
                    act.wait_ge(s_qf, j * 2 + s)
                    ea.done(A(v, flat(src[:, :, :]), ACT.Exp, scale=-1.0), f"{x}e")
                    ea.wait(act, f"{x}e", j)
                    ea.done(A(v, v, ACT.Ln, bias=one_col[:, :]), f"{x}l")
                    ea.wait(act, f"{x}l", j)
                    ea.done(A(v, v, ACT.Exp, scale=-1.0), f"{x}s")
                ev.wait(act, "key", j)
                ea.done(A(flat(e_sb[:, 1]), flat(e_sb[:, 1]), ACT.Ln), "g")
                ev.wait(act, "scan", j)
                ea.done(A(flat(qb_sb[:, :, :]), flat(b_sb[:, :, :]), ACT.Exp), "eb")
                ea.done(A(ebl[:, :, :], b_sb[:, :, :].rearrange("p a (c t) -> p a c t", t=CH)[:, :, :, CH - 1], ACT.Exp), "ebl")
                ev.wait(act, "dke", j)
                ea.done(A(flat(ke_sb[:, :, :]), flat(ke_sb[:, :, :]), ACT.Exp, scale=-1.0), "eke")
                level_exps(j, range(4))

            def heads(j):
                for a in range(2):
                    ht.wait(act, f"keT{a}", j)
                    hk.done(A(keT[:, a, :, :].rearrange("p c t -> p (c t)"), bank[4 + a][:, 0:3 * P], ACT.Copy), f"keT{a}")
                level_exps(j, range(4, NL))
                for a in range(2):
                    ht.wait(act, f"o{a}", j)
                    v = bank[6 + a][:, :].rearrange("p (c t) -> p c t", c=TT)
                    hk.done(A(ro[:, :, bass.ds(j * UC + a * P, P)], v, ACT.Copy), f"ocopy{a}")
                    if a:
                        ho.wait(act, "ss0", j)
                    elif not isinstance(j, int):
                        pass
                    hk.done(A(r_sq[:, :], bank[6 + a][:, :], ACT.Square), f"osq{a}")

            split_hi(act, qf, 1)
            split_hi(act, qf + 1, 0)
            with act.Fori(1, 4) as j:
                split_hi(act, j + qf, 1)
                gates_and_decays(j - 1)
                split_hi(act, j + (qf + 1), 0)
                heads(j - 1)
            split_hi(act, qf + 4, 1)
            gates_and_decays(3)
            split_hi(act, qf + 5, 0)
            heads(3)
            ho.wait(act, "ss1", 3)
            A(r_rs[:, 1, :, :], r_rs[:, 0, :, :], ACT.Ln, scale=1.0 / P, bias=eps_col[:, :]).then_inc(rrs_a, 1)
            act.wait_ge(rrs_a, 1)
            A(r_rs[:, 2, :, :], r_rs[:, 1, :, :], ACT.Exp, scale=-0.5).then_inc(rrs_a, 1)

            def gate_silu(u):
                act.wait_ge(unit_done, REC_IN + 12 + u + 1)
                if u >= 2:
                    act.wait_ge(g_mul, 8 * (u - 1))
                for t in range(TT):
                    A(gate[:, u % 2, t, :], bank[2 * (u % 2) + t // 2][:, (t % 2) * UC:(t % 2 + 1) * UC],
                      ACT.Silu, scale=rT[:, t:t + 1]).then_inc(g_silu, 1)
            gate_silu(0)
            split_hi(act, qf + 5, 1)
            gate_silu(1)
            gate_silu(2)
            split_hi(act, qf + 6, 0)
            gate_silu(3)
            for c in range(KT):
                act.wait_ge(gT_done, c + 1)
                A(act_hi[:, c, :], bank[4 + c % 2][:, :], ACT.Copy, scale=cols[:, C_GN:C_GN + 1]).then_inc(gT_hi, 1)
            act.preload_act_table_set(EXP_LN)
            out_projection(REC_OUT, 3, mix_rec)
            ffn(1)
            for c in range(KT):
                act.wait_ge(yT_done, c + 1)
                b = (0, 1, 2, 3, 5, 6, 7, 4)[c]
                A(y_out[:, :, c * P:(c + 1) * P], bank[b][:, :].rearrange("p (a f) -> p a f", a=TT), ACT.Copy).then_inc(y_copied, 1)

        @block.vector
        def _(dve):
            V = nc.vector
            TTo, STT, TS = V.tensor_tensor, V.scalar_tensor_tensor, V.tensor_scalar
            turn = [0]

            def waited(dve):
                turn[0] += 1
                k = turn[0] % 8
                V.memset(pad[:, k:k + 1], 0.0)

            dve.wait_ge(small_in, 16 * 5)
            TTo(lam_in[0:1, 0, :], lam_in[0:1, 0, :], lam_in[0:1, 1, :], ALU.mult)
            TTo(lam_in[0:1, 2, :], lam_in[0:1, 2, :], lam_in[0:1, 3, :], ALU.mult).then_inc(lam_v, 1)
            dve.wait_ge(lam_v, 1)
            V.tensor_reduce(lam_s[0:1, 0:2], lam_in[0:1, :, :].rearrange("p (a b) d -> p a b d", b=2)[:, :, 0, :],
                            axis=AXX, op=ALU.add).then_inc(lam_v, 1)
            for c in range(KT + 1):
                if c < KT:
                    dve.wait_ge(xT_done, c + 1)
                    V.tensor_copy(xres[:, c, :], bank[c % 4][:, :]).then_inc(x_new, 1)
                if c >= 1:
                    tile_lo(dve, 0, c - 1)
                if c == 2:
                    split_lo(dve, 0, 0, True)
            dve.wait_ge(lam_a, 1)
            STT(out=lam_s[0:1, 4:5], in0=lam_s[0:1, 2:3], scalar=LAMBDA_INIT, in1=lam_s[0:1, 3:4],
                op0=ALU.add, op1=ALU.subtract).then_inc(lam_v, 1)
            dve.wait_ge(lam_t, 1)
            V.tensor_copy(lam_s[:, 5:6], bank[6][:, 0:1])
            dve.wait_ge(colsR, 1)
            TS(lam_s[:, 6:7], cols[:, C_SUB:C_SUB + 1], 1.0 - LAMBDA_INIT, None, ALU.mult).then_inc(lam_v, 1)
            split_lo(dve, 0, 1, True)
            dve.wait_ge(r_ready, 1)
            dve.wait_ge(rope_in, 32)
            TTo(cosr[:, :], cosr[:, :], rB[:, :], ALU.mult)
            TTo(sinr[:, :], sinr[:, :], rB[:, :], ALU.mult).then_inc(rope_tab, 1)
            dve.wait_ge(rope_tab, 1)

            def rotate(p, next_qk=True):
                for s in range(2):
                    if s == 1:
                        split_lo(dve, p + 1, 0, next_qk)
                    dve.wait_ge(unit_done, p * 2 + (s + 1))
                    if not (isinstance(p, int) and p == 0):
                        dve.wait_ge(rope_out, p * 4 + (2 * s - 2))
                    for n, (h, tab) in enumerate(((0, cosr), (1, sinr), (1, cosr), (0, sinr))):
                        last = TTo(rtmp[:, s, n, :], bank[2 * s + h][:, :], tab[:, :], ALU.mult)
                    last.then_inc(rope_mul, 1)
            rotate(0)
            with dve.Fori(1, 3) as p:
                split_lo(dve, p, 1, True)
                rotate(p)
            split_lo(dve, 3, 1, True)
            rotate(3, False)
            split_lo(dve, 4, 1)
            split_lo(dve, 5, 0)
            split_lo(dve, 5, 1)
            split_lo(dve, 6, 0)

            def scores_out(n_slot, b, msk, i, stat, count):
                N = (i + 1) * P
                V.tensor_tensor_reduce(out=negs[:, n_slot, 0:N], in0=bank[b][:, 0:N], in1=msk[:, T - N:T],
                                       scale=-SCALE, scalar=3e38, op0=ALU.add, op1=ALU.min,
                                       accum_out=stat).then_inc(count, 1)

            def a_neg(g, n):
                r, i = divmod(n, 4)
                dve.wait_ge(sc_done, g * 16 + (n + 1))
                if n >= 2:
                    dve.wait_ge(p_done, g * 16 + (n - 1))
                waited(dve)
                scores_out(n % 2, n % 2, mskA, i, nmax[:, r, i:i + 1], neg_done)

            def a_pT(g, n):
                dve.wait_ge(pT_done, g * 16 + (n + 1))
                dve.wait_ge(pv_done, g * 16 + (n - 1))
                V.tensor_copy(probT[:, n % 2, :], bank[2 + n % 2][:, :]).then_inc(pT_dve, 1)

            def a_out(g, r):
                dve.wait_ge(p_done, g * 16 + 4 * (r + 1))
                V.reciprocal(rinv[:, r, :], rsum[:, r, :]).then_inc(rinv_done, 1)
                dve.wait_ge(rinv_done, g * 4 + (r + 1))
                dve.wait_ge(pv_done, g * 16 + 4 * (r + 1))
                TTo(o_st[:, r // 2, :, HD * (r % 2):HD * (r % 2 + 1)],
                    bank[4 + r % 2][:, 0:TT * HD].rearrange("p (i d) -> p i d", i=TT),
                    rinv[:, r, :].unsqueeze(2).to_broadcast([P, TT, HD]), ALU.mult).then_inc(o_done, 1)

            def o_lo(c, b, count, scale=1.0):
                dve.wait_ge(oa_hi, count)
                dst, hi = (t[:, bass.ds(c, 1), :].rearrange("p a t -> p (a t)") for t in (act_lo, act_hi))
                STT(out=dst, in0=bank[b][:, :], scalar=scale, in1=fview(hi), op0=ALU.mult,
                    op1=ALU.subtract).then_inc(oa_lo, 1)

            dve.wait_ge(masks_in, 32)
            dve.wait_ge(rope_out, 16)
            with dve.Fori(0, 2) as g:
                for n in range(16 + 5):
                    if n < 16:
                        a_neg(g, n)
                    if n >= 2 and n < 18 and (n - 2) % 4 == 3:
                        a_pT(g, n - 2)
                    if n >= 5 and (n - 5) % 4 == 3:
                        a_out(g, (n - 5) // 4)
                for h in range(2):
                    o_lo(g * 2 + h, 6 + h, g * 2 + (h + 1))

            def b_neg(g, n):
                q, i = divmod(n, 4)
                for s in range(2):
                    dve.wait_ge(bsc_done, g * 16 + (2 * n + s + 1))
                    if n >= 2:
                        dve.wait_ge(bp_done, g * 16 + (2 * (n - 2) + s + 1))
                    k = 2 * (n % 2) + s
                    waited(dve)
                    scores_out(k, k, mskB, i, nmax[:, 2 * q + s, i:i + 1], bneg_done)

            def b_weights(g, n):
                q, i = divmod(n, 4)
                N = (i + 1) * P
                r0, r1 = rinv[:, 2 * q, i:i + 1], rinv[:, 2 * q + 1, i:i + 1]
                p0, p1 = prob[:, 2 * (n % 2), 0:N], prob[:, 2 * (n % 2) + 1, 0:N]
                dve.wait_ge(bp_done, g * 16 + (2 * n + 2))
                bw.done(V.reciprocal(rinv[:, 2 * q:2 * q + 2, i], rsum[:, 2 * q:2 * q + 2, i]), "rinv")
                bw.wait(dve, "rinv", g * 8 + n)
                bw.done(TTo(r1, r1, lam_s[:, 5:6], ALU.mult), "lrinv")
                bw.wait(dve, "lrinv", g * 8 + n)
                bw.done(TS(p1, p1, r1, None, ALU.mult), "scaled")
                bw.wait(dve, "scaled", g * 8 + n)
                bw.done(STT(out=p0, in0=p0, scalar=r0, in1=p1, op0=ALU.mult, op1=ALU.subtract), "w")

            def b_norm(g, q):
                bna.wait(dve, "sq", g * 2 + q)
                bn.done(V.tensor_reduce(oss[:, 0, :], osq[:, :].rearrange("p (i d) -> p i d", i=TT),
                                        axis=AXX, op=ALU.add), "ss")
                bna.wait(dve, "r", g * 2 + q)
                bn.done(TTo(o_st[:, q, :, :], bank[6 + q][:, :].rearrange("p (i d) -> p i d", i=TT),
                            oss[:, 2, :].unsqueeze(2).to_broadcast([P, TT, P]), ALU.mult), "o")

            dve.wait_ge(lam_v, 4)
            with dve.Fori(0, 2) as g:
                for n in range(8 + 3):
                    if n < 8:
                        b_neg(g, n)
                    if 1 <= n < 9:
                        b_weights(g, n - 1)
                    if n in (7, 10):
                        b_norm(g, (n - 7) // 3)
                for q in range(2):
                    o_lo(g * 2 + (4 + q), 4 + q, g * 2 + (5 + q), scale=lam_s[:, 6:7])

            def out_projection(base, b, mix):
                mixer_zero_dve(dve, b)
                for u in range(4):
                    if u % 2 == 0:
                        split_lo(dve, base // 2 + u // 2, 1)
                        split_lo(dve, base // 2 + u // 2 + 1, 0)
                    mixer_sum_dve(dve, b, 2 * u)
                post_dve(dve, b, mix)

            def ffn(layer):
                b = 1 + 2 * layer
                fv, fa = fvs[layer], fas[layer]
                base = FFN_IN[layer] // 2

                def pair(i):
                    split_lo(dve, i + base, 1)
                    if isinstance(i, int):
                        dve.wait_ge(r_ready, b + 1)
                    dve.wait_ge(unit_done, i * 2 + (FFN_IN[layer] + 1))
                    for m in range(2):
                        if not isinstance(i, int):
                            fv.wait(dve, f"lo{m}", i - 1)
                        fv.done(TTo(f_g[:, m, :], bank[m][:, :], rB[:, :], ALU.mult), f"g{m}")
                    split_lo(dve, i + (base + 1), 0)
                    dve.wait_ge(unit_done, i * 2 + (FFN_IN[layer] + 2))
                    for m in range(2):
                        if m:
                            fv.wait(dve, "h0", i)
                        elif not isinstance(i, int):
                            fv.wait(dve, "h1", i - 1)
                        fv.done(TTo(f_u[:, :], bank[2 + m][:, :], rB[:, :], ALU.mult), f"u{m}")
                        fv.wait(dve, f"u{m}", i)
                        fa.wait(dve, f"s{m}", i)
                        fv.done(TTo(f_g[:, m, :], f_g[:, m, :], f_u[:, :], ALU.mult), f"h{m}")
                    for m in range(2):
                        fa.wait(dve, f"hi{m}", i)
                        dst, hi = (t[:, bass.ds(i * 2 + m, 1), :].rearrange("p a t -> p (a t)") for t in (hid_lo, hid_hi))
                        fv.done(TTo(dst, f_g[:, m, :], fview(hi), ALU.subtract), f"lo{m}")
                pair(0)
                with dve.Fori(1, FFN // UC) as i:
                    pair(i)
                mixer_zero_dve(dve, b + 1)
                base = FFN_OUT[layer] // 2

                def six_units(i):
                    for v in range(6):
                        m, kc = divmod(v, 3)
                        if v % 2 == 0:
                            split_lo(dve, i * 3 + (base + v // 2), 1)
                        if kc == 2:
                            mixer_sum_dve(dve, b + 1, i * 4 + 2 * m)
                        if v % 2 == 0:
                            split_lo(dve, i * 3 + (base + v // 2 + 1), 0)
                if layer == 0:
                    with dve.Fori(0, 2) as i:
                        six_units(i)
                else:
                    six_units(0)
                    six_units(1)
                post_dve(dve, b + 1, mix_ffn)

            out_projection(ATT_OUT, 1, mix_att)
            ffn(0)

            lbc = cols[:, C_LB:C_LB + 8]
            TTo(lb[:, 0, :], lbc, lbc, ALU.subtract).then_inc(lb_v, 1)
            split_lo(dve, REC_IN // 2, 1)
            dve.wait_ge(lb_a, 1)
            V.reciprocal(lb[:, 2, :], lb[:, 1, :]).then_inc(lb_v, 1)
            dve.wait_ge(lb_v, 2)
            TTo(lb[:, 1, :], lb[:, 1, :], lb[:, 2, :], ALU.mult).then_inc(lb_v, 1)
            dve.wait_ge(lb_v, 3)
            TTo(lb[:, 3, :], lb[:, 1, :], lb[:, 1, :], ALU.subtract).then_inc(lb_v, 1)
            dve.wait_ge(lb_v, 4)
            TS(lb[:, 4, :], lb[:, 3, :], -1.0, 1.0, ALU.mult, ALU.add).then_inc(lb_v, 1)
            split_lo(dve, REC_IN // 2 + 1, 0)
            split_lo(dve, REC_IN // 2 + 1, 1)
            split_lo(dve, REC_IN // 2 + 2, 0)

            flat = lambda ap: ap.rearrange("p a t -> p (a t)")
            blocks = lambda ap, L: flat(ap).rearrange("p (b h t) -> p b h t", h=2, t=L)
            chunks = lambda ap: flat(ap).rearrange("p (c t) -> p c t", t=CH)

            def qf_evac(j):
                for s, dst in ((0, q_sb), (1, k_sb)):
                    dve.wait_ge(unit_done, j * 2 + (REC_IN + 4 + s + 1))
                    for a in range(2):
                        last = TTo(dst[:, a, :], bank[2 * s + a][:, :], rB[:, :], ALU.mult)
                    last.then_inc(s_qf, 1)

            def diff(j, l):
                L = LEVELS[l]
                if l >= 2:
                    ev.wait(dve, f"mq{l - 2}", j)
                    ep.wait(dve, f"mk{l - 2}", j)
                else:
                    ev.wait(dve, "scan", j)
                v = flat(b_sb[:, :, :]).rearrange("p (b t) -> p b t", t=2 * L)
                ev.done(TTo(flat(e_sb[:, l % 2]).rearrange("p (b t) -> p b t", t=2 * L), v,
                            v[:, :, L - 1:L].to_broadcast([P, 2 * T // (2 * L), 2 * L]), ALU.subtract), f"d{l}")

            def queries(j, l):
                ea.wait(dve, f"et{l}", j)
                if l >= 4:
                    ht.wait(dve, f"lev{l - 4}_1", j)
                v = lambda ap: blocks(ap, LEVELS[l])[:, :, 1, :]
                ev.done(TTo(v(m_sb[:, l % 4]), v(e_sb[:, l % 2]), v(q_sb[:, :, :]), ALU.mult), f"mq{l}")

            def gates_and_decays(j):
                ea.wait(dve, "qs", j)
                ev.done(STT(out=flat(q_sb[:, :, :]), in0=flat(q_sb[:, :, :]), scalar=float(P) ** -0.5,
                            in1=flat(e_sb[:, 0]), op0=ALU.mult, op1=ALU.mult), "qgate")
                ea.wait(dve, "fs", j)
                for a in range(2):
                    col = lambda r: lb[:, r, bass.ds(j * 2 + a, 1)]
                    last = TS(e_sb[:, 1, a, :], e_sb[:, 1, a, :], col(4), col(3), ALU.mult, ALU.add)
                ev.done(last, "forget")
                ev.wait(dve, "forget", j)
                ev.done(TS(flat(k_sb[:, :, :]), flat(e_sb[:, 1]), -1.0, 1.0, ALU.mult, ALU.add), "key")
                ea.wait(dve, "g", j)
                dve.wait_ge(setup, 3)
                ev.done(V.tensor_tensor_scan(flat(b_sb[:, :, :]), rzero[:, :], flat(e_sb[:, 1]), 0.0,
                                             ALU.mult, ALU.add), "scan")
                ev.wait(dve, "scan", j)
                ev.done(TTo(chunks(ke_sb[:, :, :]), chunks(b_sb[:, :, :]),
                            chunks(b_sb[:, :, :])[:, :, CH - 1:CH].to_broadcast([P, 2 * TT, CH]), ALU.subtract), "dke")
                diff(j, 0)
                ea.wait(dve, "eb", j)
                ev.done(TTo(flat(qb_sb[:, :, :]), flat(qb_sb[:, :, :]), flat(q_sb[:, :, :]), ALU.mult), "qb")
                ea.wait(dve, "eke", j)
                ev.done(TTo(flat(ke_sb[:, :, :]), flat(ke_sb[:, :, :]), flat(k_sb[:, :, :]), ALU.mult), "ke")
                diff(j, 1)
                queries(j, 0)
                diff(j, 2)
                queries(j, 1)
                diff(j, 3)
                queries(j, 2)
                queries(j, 3)

            def select(j, name, l, a):
                ht.wait(dve, name, j)
                v = lambda ap: ap.rearrange("p (c t) -> p c t", t=CH)
                if l is None:
                    hs.done(TTo(v(att[:, a, :]), v(bank[6 + a][:, :]),
                                ident[:, :].unsqueeze(1).to_broadcast([P, TT, P]), ALU.mult), name)
                else:
                    hs.wait(dve, f"diag{a}" if l == 0 else f"lev{l - 1}_{a}", j)
                    if not isinstance(j, int):
                        waited(dve)
                    hs.done(V.copy_predicated(v(att[:, a, :]), rmask[:, l, :].unsqueeze(1).to_broadcast([P, TT, P]),
                                              v(bank[6 + a][:, :])), name)

            def heads(j, then):
                lev = lambda l: [select(j, f"lev{l}_{a}", l, a) for a in range(2)]
                for a in range(2):
                    select(j, f"diag{a}", None, a)
                diff(j, 4)
                lev(0)
                diff(j, 5)
                queries(j, 4)
                lev(1)
                diff(j, 6)
                queries(j, 5)
                lev(2)
                queries(j, 6)
                lev(3)
                if then is not None:
                    ev.wait(dve, "mq6", j)
                    ep.wait(dve, "mk6", j)
                    qf_evac(then)
                for l in (4, 5, 6):
                    lev(l)
                for a in range(2):
                    ht.wait(dve, f"u{a}", j)
                    for c in range(1, 4):
                        u = bank[4 + a][:, (c - 1) * P:c * P]
                        if c == 1:
                            ho.done(V.tensor_copy(state[:, a, 0, :], u), f"s1_{a}")
                        else:
                            ho.wait(dve, f"s{c - 1}_{a}", j)
                            ho.done(STT(out=state[:, a, c - 1, :], in0=state[:, a, c - 2, :],
                                        scalar=ebl[:, a, c - 1:c], in1=u, op0=ALU.mult, op1=ALU.add), f"s{c}_{a}")
                for a in range(2):
                    hk.wait(dve, f"osq{a}", j)
                    ho.done(V.tensor_reduce(r_rs[:, 0, bass.ds(j * 2 + a, 1), :].rearrange("p a c -> p (a c)"),
                                            r_sq[:, :].rearrange("p (c v) -> p c v", c=TT), axis=AXX, op=ALU.add), f"ss{a}")

            dve.wait_ge(rmask_in, 16)
            V.tensor_copy(rmask[:, :, :], flat(qb_sb[:, :, :])[:, 0:NL * P].rearrange("p (l t) -> p l t", l=NL)).then_inc(rmask_ready, 1)
            dve.wait_ge(rmask_ready, 1)
            split_lo(dve, qf, 1)
            qf_evac(0)
            split_lo(dve, qf + 1, 0)
            with dve.Fori(1, 4) as j:
                split_lo(dve, j + qf, 1)
                gates_and_decays(j - 1)
                split_lo(dve, j + (qf + 1), 0)
                heads(j - 1, j)
            split_lo(dve, qf + 4, 1)
            gates_and_decays(3)
            split_lo(dve, qf + 5, 0)
            heads(3, None)

            def gate_mul(u):
                dve.wait_ge(rrs_a, 2)
                if u >= 2:
                    dve.wait_ge(gT_done, 2 * (u - 1))
                for t in range(TT):
                    dve.wait_ge(g_silu, 4 * u + t + 1)
                    for h in range(2):
                        hs_ = slice(h * P, (h + 1) * P)
                        STT(out=og[:, u % 2, t, hs_], in0=ro[:, t, (2 * u + h) * P:(2 * u + h + 1) * P],
                            scalar=r_rs[:, 2, 2 * u + h, t:t + 1], in1=gate[:, u % 2, t, hs_],
                            op0=ALU.mult, op1=ALU.mult).then_inc(g_mul, 1)

            def gated_lo(c):
                dve.wait_ge(gT_hi, c + 1)
                STT(out=act_lo[:, c, :], in0=bank[4 + c % 2][:, :], scalar=cols[:, C_GN:C_GN + 1],
                    in1=fview(act_hi[:, c, :]), op0=ALU.mult, op1=ALU.subtract).then_inc(gT_lo, 1)
            split_lo(dve, qf + 5, 1)
            gate_mul(0)
            gate_mul(1)
            split_lo(dve, qf + 6, 0)
            for u in range(2):
                gated_lo(2 * u)
                gated_lo(2 * u + 1)
                gate_mul(u + 2)
            for c in range(4, KT):
                gated_lo(c)
            out_projection(REC_OUT, 3, mix_rec)
            ffn(1)


def constants():
    half = HD // 2
    inv = (10000.0 ** (-np.arange(0, HD, 2, dtype=np.float32) / HD)).astype(np.float32)
    ang = np.arange(T, dtype=np.float32)[None, :] * inv[:, None]
    cos, sin = (np.tile(f(ang).astype(np.float32), (P // half, 1)) for f in (np.cos, np.sin))
    rel = (T - P) + np.arange(P)[:, None] - np.arange(T)[None, :]
    causal = rel >= 0
    held = sum(((rel <= w) & (rel % d == 0) & causal).astype(np.int64) for w, d in ((128, 1), (512, 4), (2048, 16)))
    mask_a = np.where(held > 0, np.log(np.maximum(held, 1)) / SCALE, -BIG).astype(np.float32)
    mask_b = np.where(causal, 0.0, -BIG).astype(np.float32)
    s, t = np.arange(P)[:, None], np.arange(P)[None, :]
    levels = np.stack([(s // (2 * L) == t // (2 * L)) & (s % (2 * L) < L) & (t % (2 * L) >= L) for L in LEVELS], 1)
    return dict(cos_t=cos, sin_t=sin, mask_a=mask_a, mask_b=mask_b, ident_in=np.eye(P, dtype=np.float32),
                level_masks=levels.reshape(P, NL * P).astype(np.float32))


_INS = ["x", "norm_gains", "att_w_in", "att_lambda", "att_subln", "att_w_out", "rec_w_in",
        "rec_lower_bounds", "rec_gnorm", "rec_w_out", "ffn_w_in", "ffn_w_out"]


def kernel(**inputs):
    import concourse.bacc as bacc
    from concourse.bass_utils import run_bass_kernel_spmd

    nc = bacc.Bacc("TRN2", target_bir_lowering=False, num_devices=1)
    given = {n: np.ascontiguousarray(inputs[n]) for n in _INS} | constants()
    arrays, args = {}, []
    for name, a in given.items():
        arrays[f"in_{name}"] = a
        args.append(nc.dram_tensor(f"in_{name}", a.shape, mybir.dt.from_np(a.dtype), kind="ExternalInput").ap())
    args.append(nc.dram_tensor("out_0", (1, T, D), F32, kind="ExternalOutput").ap())
    trunk(nc, *args)
    return run_bass_kernel_spmd(nc, [arrays], core_ids=[0]).results[0]["out_0"]
```

```python
from contextlib import ExitStack

import numpy as np

import concourse.bass as bass
from concourse import mybir

P = 128
F32 = mybir.dt.float32
F32R = mybir.dt.float32r
U8 = mybir.dt.uint8
ALU = mybir.AluOpType
ACT = mybir.ActivationFunctionType
AXX = mybir.AxisListType.X

D = 1024
T = 512
KT = D // P
TT = T // P
HD = 64
SCALE = HD ** -0.5
FFN = 2816
FT = FFN // P
UC = 256
EPS = 1e-6
LAMBDA_INIT = 0.8 - 0.6 * float(np.exp(-0.3 * 0.0))
BIG = 1e30
CH = 128
LEVELS = (64, 32, 16, 8, 4, 2, 1)
NL = len(LEVELS)
EXP_LN = "natural_log_exp_and_others"

ATT_IN = 0
ATT_OUT = ATT_IN + 12
FFN_IN = (ATT_OUT + 4, ATT_OUT + 4 + 22 + 12 + 16 + 4)
FFN_OUT = (FFN_IN[0] + 22, FFN_IN[1] + 22)
REC_IN = FFN_OUT[0] + 12
REC_OUT = REC_IN + 16
UNITS = FFN_OUT[1] + 12

C_GAIN, C_SUB, C_GN, C_LB, C_ALL = 0, 64, 65, 66, 74


class Steps:

    def __init__(self, sem, names):
        self.sem, self.names, self.k = sem, names, 0
        self.at = {n: k + 1 for k, n in enumerate(names)}
        assert len(self.at) == len(names)

    def wait(self, eng, name, i=0):
        eng.wait_ge(self.sem, i * len(self.names) + self.at[name])

    def done(self, ins, name):
        assert self.names[self.k % len(self.names)] == name, (name, self.names[self.k % len(self.names)])
        self.k += 1
        ins.then_inc(self.sem, 1)


def trunk(nc, x, norm_gains, att_w_in, att_lambda, att_subln, att_w_out, rec_w_in,
          rec_lower_bounds, rec_gnorm, rec_w_out, ffn_w_in, ffn_w_out,
          cos_t, sin_t, mask_a, mask_b, ident_in, level_masks, out):
    with ExitStack() as ctx:
        def sb(name, shape, dt=F32):
            return ctx.enter_context(nc.sbuf_tensor(name, shape, dt))

        def sem(name):
            return ctx.enter_context(nc.semaphore(name))

        def phase(*items):
            with ExitStack() as e:
                return [e.enter_context(nc.sbuf_tensor(n, s, d)) for n, s, d in items]

        bank = [ctx.enter_context(nc.psum_tensor(f"bank{i}", [P, T], F32)) for i in range(8)]

        xres = sb("xres", [P, KT, T])
        act_hi = sb("act_hi", [P, KT, T], F32R)
        (act_lo,) = phase(("act_lo", [P, KT, T], F32R))
        mix_ffn = sb("mix_ffn", [P, KT, T])
        raw = sb("raw", [P, 2, 8, UC])
        whi = sb("whi", [P, 2, 8, UC], F32R)
        wlo = sb("wlo", [P, 2, 8, UC], F32R)
        ident = sb("ident", [P, P])
        ones = sb("ones", [P, P])
        eps_col = sb("eps_col", [P, 1])
        one_col = sb("one_col", [P, 1])
        pad = sb("pad", [P, 8])
        cols = sb("cols", [P, C_ALL])
        rB = sb("rB", [P, T])
        rM = sb("rM", [P, T])
        rT = sb("rT", [P, TT])
        ln_tmp = sb("ln_tmp", [P, T])
        lnT_tmp = sb("lnT_tmp", [P, TT])
        sq_ring = sb("sq_ring", [P, 2, T])
        xsq = sb("xsq", [P, T])
        (msq,) = (sb("msq", [P, T]),)

        (rope, vtok, qk_st, mskA, mskB, cosr, sinr, rtmp, prob, probT, rsum, nmax, rinv, oss,
         lam_s) = phase(
             ("rope", [P, 4, 2, 2, T], F32), ("vtok", [P, TT, D], F32),
             ("qk_st", [P, 2, 2, T], F32), ("mskA", [P, T], F32), ("mskB", [P, T], F32),
             ("cosr", [P, T], F32), ("sinr", [P, T], F32), ("rtmp", [P, 4, T], F32),
             ("prob", [P, 8, T], F32), ("probT", [P, 2, T], F32),
             ("rsum", [P, 4, 4], F32), ("nmax", [P, 4, 4], F32), ("rinv", [P, 4, 4], F32),
             ("oss", [P, 3, TT], F32), ("lam_s", [P, 8], F32))
        x_in, _skip, lam_in, colsrc = phase(
            ("x_in", [P, TT, D], F32), ("_skip", [P, TT, D], F32), ("lam_in", [P, 4, HD], F32),
            ("colsrc", [P, P], F32))
        by_block = lambda ap: ap.rearrange("p (i d) -> p i d", i=TT)
        oA = [by_block(ap) for ap in (sq_ring[:, 0, :], sq_ring[:, 1, :], xsq[:, :], msq[:, :])]
        osq, oB = ln_tmp, by_block(rM[:, :])
        (mix_att,) = phase(("mix_att", [P, KT, T], F32))
        hid_hi, hid_lo, f_g, f_u = phase(
            ("hid_hi", [P, FT, T], F32R), ("hid_lo", [P, FT, T], F32R),
            ("f_g", [P, 2, T], F32), ("f_u", [P, T], F32))
        (y_out,) = phase(("y_out", [P, TT, D], F32))
        (rv, rmask, rzero, lb, ro, b_sb, e_sb, m_sb, qb_sb, ke_sb, keT, att, state, r_sq,
         r_rs, ebl, q_sb, k_sb) = phase(
             ("rv", [P, TT, D], F32), ("rmask", [P, NL, P], U8),
             ("rzero", [P, 2 * T], F32), ("lb", [P, 5, 8], F32), ("ro", [P, TT, D], F32),
             ("b_sb", [P, 2, T], F32), ("e_sb", [P, 2, 2, T], F32),
             ("m_sb", [P, 4, 2, T], F32), ("qb_sb", [P, 2, T], F32), ("ke_sb", [P, 2, T], F32),
             ("keT", [P, 2, 3, P], F32), ("att", [P, 2, T], F32), ("state", [P, 2, 3, P], F32),
             ("r_sq", [P, T], F32), ("r_rs", [P, 3, 8, TT], F32), ("ebl", [P, 2, TT], F32),
             ("q_sb", [P, 2, T], F32), ("k_sb", [P, 2, T], F32))
        (mix_rec,) = phase(("mix_rec", [P, KT, T], F32))
        gate, og = phase(
            ("_rv", [P, TT, D], F32), ("_rm", [P, NL, P], U8), ("_rz", [P, 2 * T], F32),
            ("_lb", [P, 5, 8], F32), ("_ro", [P, TT, D], F32), ("gate", [P, 2, TT, UC], F32),
            ("og", [P, 2, TT, UC], F32))[-2:]

        raw_in = [sem("raw_in0"), sem("raw_in1")]
        w_hi = sem("w_hi")
        w_lo = sem("w_lo")
        unit_done = sem("unit_done")
        x_in_sem = [sem(f"x_in{t}") for t in range(TT)]
        rmask_ready = sem("rmask_ready")
        ident_in_sem, small_in, rope_in, masks_in, rmask_in = (
            sem("ident_in"), sem("small_in"), sem("rope_in"), sem("masks_in"), sem("rmask_in"))
        setup = sem("setup")
        colsT, colsR = sem("colsT"), sem("colsR")
        lam_v, lam_a, lam_t = sem("lam_v"), sem("lam_a"), sem("lam_t")
        xT_done = sem("xT_done")
        x_new = sem("x_new")
        x_hi, x_lo = sem("x_hi"), sem("x_lo")
        x_sq, x_acc = sem("x_sq"), sem("x_acc")
        stat_mm, stat_ln, r_ready = sem("stat_mm"), sem("stat_ln"), sem("r_ready")
        m_evac, m_acc = sem("m_evac"), sem("m_acc")
        m_mm, m_ln, rM_ready, m_scaled = sem("m_mm"), sem("m_ln"), sem("rM_ready"), sem("m_scaled")
        rope_tab, rope_mul, rope_out, v_evac = (
            sem("rope_tab"), sem("rope_mul"), sem("rope_out"), sem("v_evac"))
        qk_evac = sem("qk_evac")
        qk_in = [sem("qk_in0"), sem("qk_in1")]
        qd_in = [sem("qd_in0"), sem("qd_in1")]
        sc_done, neg_done, p_done, pT_done = sem("sc_done"), sem("neg_done"), sem("p_done"), sem("pT_done")
        pT_act, pT_dve, pv_done, rinv_done, o_done = (
            sem("pT_act"), sem("pT_dve"), sem("pv_done"), sem("rinv_done"), sem("o_done"))
        oT_done, oa_hi, oa_lo = sem("oT_done"), sem("oa_hi"), sem("oa_lo")
        bw_done, bn_a, bn_v = sem("bw_done"), sem("bn_a"), sem("bn_v")
        yT_done, y_copied, y_out_sem = sem("yT_done"), sem("y_copied"), sem("y_out_sem")
        ffn_v = [sem("ffn_v0"), sem("ffn_v1")]
        ffn_a = [sem("ffn_a0"), sem("ffn_a1")]
        lb_v, lb_a = sem("lb_v"), sem("lb_a")
        rv_evac = sem("rv_evac")
        s_qf = sem("qf_evac")
        hg_v, hg_a, hg_p = sem("hg_v"), sem("hg_a"), sem("hg_p")
        hg_t, hg_s, hg_k, hg_o = sem("hg_t"), sem("hg_s"), sem("hg_k"), sem("hg_o")
        g_silu, g_mul, gT_done, gT_hi, gT_lo = (
            sem("g_silu"), sem("g_mul"), sem("gT_done"), sem("gT_hi"), sem("gT_lo"))
        rrs_a = sem("rrs_a")

        fview = lambda ap: ap.bitcast(F32)

        def weight_rows(w, k0, nk, col):
            return w.rearrange("(k p) n -> p k n", p=P)[:, k0:k0 + nk, bass.ds(col, UC)]

        def load(sp, pair, slot, src):
            if not (isinstance(pair, int) and pair == 0):
                sp.wait_ge(w_lo, pair * 2 + (slot - 1))
            nk = src.shape[1]
            sp.dma_start(raw[:, slot, 0:nk, :], src).then_inc(raw_in[slot], 16)

        def of_unit(w, slot, halves, part):
            if not halves:
                v = w[:, slot, :, :]
                return v if part is None else v[:, 4 * part:4 * part + 4, :]
            v = w[:, slot, :, :].rearrange("p k n -> p (k n)")
            if w is raw:
                v = v.rearrange("p (kh a x) -> p a kh x", a=2, x=HD // 2)
            else:
                v = v.rearrange("p (a kh x) -> p a kh x", a=2, x=HD // 2)
            n = v.shape[2] // 2
            return v if part is None else v[:, :, n * part:n * part + n, :]

        def split_hi(act, pair, slot, halves=False, part=None):
            if isinstance(pair, int) and pair * 2 + slot >= UNITS:
                return
            if not (isinstance(pair, int) and pair == 0):
                act.wait_ge(unit_done, pair * 2 + (slot - 1))
            act.wait_ge(raw_in[slot], pair * 16 + 16)
            a = nc.scalar.activation(of_unit(whi, slot, halves, part), of_unit(raw, slot, halves, part), ACT.Copy)
            if part != 0:
                a.then_inc(w_hi, 1)

        def split_lo(dve, pair, slot, halves=False, part=None):
            if isinstance(pair, int) and pair * 2 + slot >= UNITS:
                return
            dve.wait_ge(w_hi, pair * 2 + slot + 1)
            v = nc.vector.tensor_tensor(of_unit(wlo, slot, halves, part), of_unit(raw, slot, halves, part),
                                        fview(of_unit(whi, slot, halves, part)), ALU.subtract)
            if part != 0:
                v.then_inc(w_lo, 1)

        def unit_features(pe, pair, slot, nk, hi, lo, banks, k0=0, first=True, last=True,
                          rope_cols=False, ready=None, free=None, w0=0, part=False):
            pe.wait_ge(w_lo, pair * 2 + slot + 1)
            if free is not None:
                pe.wait_ge(*free)
            for k in range(nk):
                if ready is not None:
                    pe.wait_ge(ready[0], ready[1] + k0 + k + 1)
                for m in range(2):
                    if rope_cols:
                        pick = lambda w: w[:, slot].rearrange("p k n -> p (k n)")[:, (m * KT + w0 + k) * P:(m * KT + w0 + k + 1) * P]
                    else:
                        pick = lambda w: w[:, slot, w0 + k, m * P:(m + 1) * P]
                    o = bank[banks + m][:, :]
                    nc.tensor.matmul(o, pick(whi), hi[:, k0 + k, :], start=first and k == 0, stop=False)
                    nc.tensor.matmul(o, pick(whi), lo[:, k0 + k, :], start=False, stop=False)
                    mm = nc.tensor.matmul(o, pick(wlo), hi[:, k0 + k, :], start=False,
                                          stop=last and k == nk - 1)
            if not part:
                mm.then_inc(unit_done, 1)

        def unit_tokens(pe, pair, slot, banks, ready=None, free=None, ks=range(KT)):
            pe.wait_ge(w_lo, pair * 2 + slot + 1)
            if free is not None:
                pe.wait_ge(*free)
            for k in ks:
                if ready is not None:
                    pe.wait_ge(ready[0], ready[1] + k + 1)
                for t in range(TT):
                    o = bank[banks + t // 2][:, (t % 2) * UC:(t % 2 + 1) * UC]
                    a_hi, a_lo = (a[:, k, t * P:(t + 1) * P] for a in (act_hi, act_lo))
                    nc.tensor.matmul(o, a_hi, whi[:, slot, k, :], start=k == 0 and t % 2 == 0,
                                     stop=False, skip_group_check=True)
                    nc.tensor.matmul(o, a_lo, whi[:, slot, k, :], start=False, stop=False,
                                     skip_group_check=True)
                    mm = nc.tensor.matmul(o, a_hi, wlo[:, slot, k, :], start=False,
                                          stop=k == KT - 1, skip_group_check=True)
            if ks[-1] == KT - 1:
                mm.then_inc(unit_done, 1)

        def gain(row, c):
            return cols[:, C_GAIN + row * KT + c:C_GAIN + row * KT + c + 1]

        def tile_act(act, b, c):
            act.wait_ge(x_new, KT * b + c + 1)
            nc.scalar.activation(act_hi[:, c, :], xres[:, c, :], ACT.Copy, scale=gain(2 * b, c)).then_inc(x_hi, 1)
            if c >= 3:
                act.wait_ge(x_acc, 7 * b + c - 2)
            dst = xsq[:, :] if c == 0 else sq_ring[:, c % 2, :]
            nc.scalar.activation(dst, xres[:, c, :], ACT.Square).then_inc(x_sq, 1)

        def tile_lo(dve, b, c):
            dve.wait_ge(x_hi, KT * b + c + 1)
            nc.vector.scalar_tensor_tensor(out=act_lo[:, c, :], in0=xres[:, c, :], scalar=gain(2 * b, c),
                                           in1=fview(act_hi[:, c, :]), op0=ALU.mult,
                                           op1=ALU.subtract).then_inc(x_lo, 1)

        def squares_pool(pool, b):
            for c in range(1, KT):
                pool.wait_ge(x_sq, KT * b + c + 1)
                if c > 1:
                    pool.wait_ge(x_acc, 7 * b + c - 1)
                nc.gpsimd.tensor_tensor(xsq[:, :], xsq[:, :], sq_ring[:, c % 2, :], ALU.add).then_inc(x_acc, 1)

        def stat_pe(pe, b):
            pe.wait_ge(x_acc, 7 * (b + 1))
            nc.tensor.matmul(bank[4][:, :], ones[:, :], xsq[:, :], start=True, stop=True)
            for t in range(TT):
                mm = nc.tensor.matmul(bank[5][:, t:t + 1], xsq[:, t * P:(t + 1) * P], ones[:, 0:1],
                                      start=True, stop=True)
            mm.then_inc(stat_mm, 1)

        def stat_act(act, b):
            act.wait_ge(stat_mm, b + 1)
            nc.scalar.activation(ln_tmp[:, :], bank[4][:, :], ACT.Ln, scale=1.0 / D, bias=eps_col[:, :])
            nc.scalar.activation(lnT_tmp[:, :], bank[5][:, 0:TT], ACT.Ln, scale=1.0 / D,
                                 bias=eps_col[:, :]).then_inc(stat_ln, 1)
            act.wait_ge(stat_ln, b + 1)
            nc.scalar.activation(rB[:, :], ln_tmp[:, :], ACT.Exp, scale=-0.5)
            nc.scalar.activation(rT[:, :], lnT_tmp[:, :], ACT.Exp, scale=-0.5).then_inc(r_ready, 1)

        def mixer_evac_act(act, b, mix, unit, tile, banks):
            act.wait_ge(unit_done, unit + 1)
            for m in range(2):
                if not (isinstance(tile, int) and tile == 0):
                    act.wait_ge(m_acc, tile + (9 * (b - 1) + m))
                nc.scalar.activation(mix[:, bass.ds(tile + m, 1), :].rearrange("p a t -> p (a t)"),
                                     bank[banks + m][:, :], ACT.Copy)
                nc.scalar.activation(sq_ring[:, m, :], bank[banks + m][:, :], ACT.Square).then_inc(m_evac, 1)

        def mixer_zero_dve(dve, b):
            if b > 1:
                dve.wait_ge(m_mm, b - 1)
            nc.vector.memset(msq[:, :], 0.0).then_inc(m_acc, 1)

        def mixer_sum_dve(dve, b, tile):
            for m in range(2):
                dve.wait_ge(m_evac, tile + (KT * (b - 1) + m + 1))
                dve.wait_ge(m_acc, tile + (9 * (b - 1) + m + 1))
                nc.vector.tensor_tensor(msq[:, :], msq[:, :], sq_ring[:, m, :], ALU.add).then_inc(m_acc, 1)

        def post_pe(pe, b):
            pe.wait_ge(m_acc, 9 * b)
            nc.tensor.matmul(bank[4][:, :], ones[:, :], msq[:, :], start=True, stop=True).then_inc(m_mm, 1)

        def post_act(act, b):
            act.wait_ge(m_mm, b)
            nc.scalar.activation(ln_tmp[:, :], bank[4][:, :], ACT.Ln, scale=1.0 / D,
                                 bias=eps_col[:, :]).then_inc(m_ln, 1)
            act.wait_ge(m_ln, b)
            nc.scalar.activation(rM[:, :], ln_tmp[:, :], ACT.Exp, scale=-0.5).then_inc(rM_ready, 1)
            if b < 4:
                for c in range(KT):
                    tile_act(act, b, c)

        def post_dve(dve, b, mix):
            dve.wait_ge(rM_ready, b)
            for c in range(KT + 2):
                if c < KT:
                    nc.vector.scalar_tensor_tensor(out=mix[:, c, :], in0=mix[:, c, :], scalar=gain(2 * b - 1, c),
                                                   in1=rM[:, :], op0=ALU.mult, op1=ALU.mult).then_inc(m_scaled, 1)
                if 1 <= c <= KT:
                    dve.wait_ge(m_scaled, KT * (b - 1) + c)
                    nc.vector.tensor_tensor(xres[:, c - 1, :], xres[:, c - 1, :], mix[:, c - 1, :],
                                            ALU.add).then_inc(x_new, 1)
                if c >= 2 and b < 4:
                    tile_lo(dve, b, c - 2)

        block = ctx.enter_context(nc.Block())

        @block.sync
        def _(sp):
            for t in range(TT):
                sp.dma_start(x_in[:, t, :], x[0, t * P:(t + 1) * P, :]).then_inc(x_in_sem[t], 16)
            w = att_w_in[0]
            def stage(h, slot, into):
                r, q = h % 4, h % 2
                for half in range(2):
                    d = HD * q + 32 * half
                    sp.dma_start(qk_st[d:d + 32, slot, :, :],
                                 rope[32 * r:32 * r + 32, h // 4, :, half, :]).then_inc(into, 16)

            def att_load(u):
                if u < 12:
                    col = (0, 512, 256, 768, 1024, 1280, 1536, 2048, 2560, 1792, 2304, 2816)[u]
                    load(sp, u // 2, u % 2, weight_rows(w, 0, KT, col))
                else:
                    load(sp, u // 2, u % 2, weight_rows(att_w_out[0], 0, KT, (u - ATT_OUT) * UC))

            def stage(h, slot, into):
                row, q = h % 4, h % 2
                for half in range(2):
                    d = HD * q + 32 * half
                    sp.dma_start(qk_st[d:d + 32, slot, :, :],
                                 rope[32 * row:32 * row + 32, h // 4, :, half, :]).then_inc(into, 16)

            def stage_a(h):
                if h == 4:
                    sp.wait_ge(rope_out, 8)
                sp.wait_ge(sc_done, 4 * (h - 1))
                stage(h, 0, qk_in[h % 2])

            def stage_b(d):
                if d == 0:
                    sp.wait_ge(rope_out, 12)
                elif d == 1:
                    sp.wait_ge(sc_done, 32)
                elif d == 2:
                    sp.wait_ge(rope_out, 16)
                if d >= 2:
                    sp.wait_ge(sc_done, 32 + 8 * (d - 1))
                for q in range(2):
                    stage(8 + 2 * d + q, (d + 1) % 2, qd_in[(d + 1) % 2])

            for u in range(6):
                att_load(u)
            sp.wait_ge(rope_out, 4)
            stage(0, 0, qk_in[0])
            stage(1, 0, qk_in[1])
            for u in (6, 7, 8):
                att_load(u)
            stage_a(2)
            att_load(9)
            stage_a(3)
            stage_a(4)
            att_load(10)
            stage_a(5)
            stage_a(6)
            att_load(11)
            stage_a(7)
            stage_b(0)
            att_load(12)
            stage_b(1)
            att_load(13)
            stage_b(2)
            stage_b(3)
            att_load(14)
            att_load(15)
            for layer in range(2):
                w1, w2 = ffn_w_in[layer], ffn_w_out[layer]
                with sp.Fori(0, FFN // UC) as i:
                    load(sp, i + FFN_IN[layer] // 2, 0, weight_rows(w1, 0, KT, i * UC))
                    load(sp, i + FFN_IN[layer] // 2, 1, weight_rows(w1, 0, KT, i * UC + FFN))
                with sp.Fori(0, 2) as i:
                    for v in range(6):
                        m, kc = divmod(v, 3)
                        load(sp, i * 3 + (FFN_OUT[layer] // 2 + v // 2), v % 2,
                             weight_rows(w2, 8 * kc, min(8, FT - 8 * kc), i * (2 * UC) + m * UC))
                if layer == 0:
                    w = rec_w_in[0]
                    with sp.Fori(0, 2) as i:
                        for s in range(2):
                            load(sp, i + REC_IN // 2, s, weight_rows(w, 0, KT, i * (2 * UC) + (2 * D + s * UC)))
                    sp.wait_ge(m_mm, 2)
                    sp.dma_start(qb_sb[:, :, :].rearrange("p a t -> p (a t)")[:, 0:NL * P], level_masks).then_inc(rmask_in, 16)
                    with sp.Fori(0, 4) as i:
                        for s in range(2):
                            load(sp, i + (REC_IN // 2 + 2), s, weight_rows(w, 0, KT, i * UC + s * D))
                    with sp.Fori(0, 2) as i:
                        for s in range(2):
                            load(sp, i + (REC_IN // 2 + 6), s, weight_rows(w, 0, KT, i * (2 * UC) + (3 * D + s * UC)))
                    with sp.Fori(0, 2) as i:
                        for s in range(2):
                            load(sp, i + REC_OUT // 2, s, weight_rows(rec_w_out[0], 0, KT, i * (2 * UC) + s * UC))
            for half in range(2):
                sp.wait_ge(y_copied, 4 * half + 4)
                cs = slice(half * T, half * T + T)
                sp.dma_start(out[0].rearrange("(a p) d -> p a d", p=P)[:, :, cs], y_out[:, :, cs]).then_inc(y_out_sem, 16)
            sp.wait_ge(y_out_sem, 32)

        H_STEPS_T = ["keT0", "keT1", "diag0", "diag1"] + [f"lev{l}_{a}" for l in range(NL) for a in range(2)] \
            + ["u0", "u1", "o0", "o1"]
        H_STEPS_S = ["diag0", "diag1"] + [f"lev{l}_{a}" for l in range(NL) for a in range(2)]
        EV = ["qgate", "forget", "key", "scan", "dke", "d0", "qb", "ke", "d1", "mq0", "d2", "mq1", "d3",
              "mq2", "mq3", "d4", "d5", "mq4", "d6", "mq5", "mq6"]
        EA = ["qe", "ql", "qs", "fe", "fl", "fs", "g", "eb", "ebl", "eke"] \
            + [f"{x}{l}" for l in range(NL) for x in ("et", "es")]
        ev, ea = Steps(hg_v, EV), Steps(hg_a, EA)
        ep = Steps(hg_p, [f"mk{l}" for l in range(NL)])
        ht, hs = Steps(hg_t, H_STEPS_T), Steps(hg_s, H_STEPS_S)
        hk = Steps(hg_k, ["keT0", "keT1", "ocopy0", "osq0", "ocopy1", "osq1"])
        ho = Steps(hg_o, [f"s{c}_{a}" for a in range(2) for c in range(1, 4)] + ["ss0", "ss1"])

        qf = REC_IN // 2 + 2
        bw = Steps(bw_done, ["rinv", "ratio", "w"])
        bn = Steps(bn_v, ["s2", "ss", "ss_eps", "o"])
        bna = Steps(bn_a, ["sq", "ln", "r"])
        FV = ["g0", "g1", "u0", "h0", "u1", "h1", "lo0", "lo1"]
        FA = ["s0", "s1", "hi0", "hi1"]
        fvs = [Steps(v, FV) for v in ffn_v]
        fas = [Steps(v, FA) for v in ffn_a]

        A_ITEMS, ITEMS = 32, 48

        def scores_of_step(m):
            if m + 3 < A_ITEMS:
                return [m + 3]
            b = m + 3 - A_ITEMS
            return [A_ITEMS + 2 * b, A_ITEMS + 2 * b + 1] if 0 <= b < 16 else []

        def score(n):
            if n < A_ITEMS:
                return n // 4, n // 4 % 2, n % 4, 2 + n // 4 % 2
            d, q = divmod(n - A_ITEMS, 8)
            return d, q % 2, q // 2, 2 * (d % 2) + q % 2

        UNIT_K = ((0, 1), (2, 3), (4,), (5, 6), (7,), ())

        def unit_of_step(m):
            return (6 + m // 6, UNIT_K[m % 6]) if m < 30 else (11, (m - 30,)) if m < 38 else (None, ())

        def evac_of_step(m):
            return 6 + m // 6 if m in (5, 11, 17, 23, 29) else 11 if m == 38 else None

        ROPE_UNITS = {0: (0, 0), 1: (0, 1), 2: (1, 0), 3: (1, 1), 6: (2, 0), 7: (2, 1), 9: (3, 0), 10: (3, 1)}
        ROPE_AT = {u: n for n, u in enumerate(ROPE_UNITS)}
        V_UNITS = (4, 5, 8, 11)
        HI_AT = {0: 7, 5: 8, 11: 9, 17: 10, 23: 11, 33: 12, 40: 13}

        def split_of_step(m, lag):
            for half in range(2):
                if m - lag - half in HI_AT:
                    return HI_AT[m - lag - half], half
            return None

        OUT_AT = {39: 0, 40: 1, 41: 2, 42: 3, 43: 4, 45: 5}
        OUT_BANK = (6, 7, 6, 7, 3, 3, 3, 3)

        def copied(eng, m):
            if m >= A_ITEMS:
                eng.wait_ge(pT_act, 24 + m - A_ITEMS + 1)
            elif m % 4 == 3:
                eng.wait_ge(pT_dve, m // 4 + 1)
            else:
                eng.wait_ge(pT_act, 3 * (m // 4) + m % 4 + 1)

        @block.tensor
        def _(pe):
            mm = nc.tensor.matmul
            tr = nc.tensor.transpose
            pe.wait_ge(ident_in_sem, 16)
            pe.wait_ge(small_in, 16 * 5)
            tr(bank[7][:, 0:C_ALL], colsrc[0:C_ALL, :], ident[0:C_ALL, 0:C_ALL]).then_inc(colsT, 1)
            for c in range(KT):
                if c >= 4:
                    pe.wait_ge(x_new, c - 3)
                for t in range(TT):
                    if c == 0:
                        pe.wait_ge(x_in_sem[t], 16)
                    last = tr(bank[c % 4][:, t * P:(t + 1) * P], x_in[:, t, c * P:(c + 1) * P], ident[:, :])
                last.then_inc(xT_done, 1)
            pe.wait_ge(setup, 1)
            pe.wait_ge(lam_v, 3)
            mm(bank[6][:, 0:1], ones[0:1, :], lam_s[0:1, 4:5], start=True, stop=True).then_inc(lam_t, 1)

            for u in range(4):
                unit_features(pe, u // 2, u % 2, KT, act_hi, act_lo, 2 * (u % 2), rope_cols=True,
                              ready=(x_lo, 0) if u == 0 else None,
                              free=(x_new, 8) if u < 2 else (qk_evac, u - 1))
                if u == 0:
                    stat_pe(pe, 0)
            def scores(n):
                head, sub, i, _ = score(n)
                if n < A_ITEMS:
                    slot = 0
                    if i == 0:
                        pe.wait_ge(qk_in[sub], 32 * (head // 2 + 1))
                else:
                    slot = (head + 1) % 2
                    if i == 0 and sub == 0:
                        pe.wait_ge(qd_in[slot], 64 * (head // 2 + 1))
                if n >= 3:
                    pe.wait_ge(neg_done, n - 2)
                h = slice(HD * sub, HD * sub + HD)
                mm(bank[n % 3][:, 0:(i + 1) * P], qk_st[h, slot, 0, i * P:(i + 1) * P],
                   qk_st[h, slot, 1, 0:(i + 1) * P], start=True, stop=True).then_inc(sc_done, 1)

            def transposes(m):
                if m < A_ITEMS:
                    pe.wait_ge(p_done, m + 1)
                    slot = m % 8
                else:
                    bw.wait(pe, "w", m - A_ITEMS)
                    slot = 2 * (m % 4)
                if m:
                    copied(pe, m - 1)
                if m - 1 in OUT_AT and OUT_AT[m - 1] >= 4:
                    pe.wait_ge(oa_lo, OUT_AT[m - 1] + 1)
                for k in range(m % 4 + 1):
                    last = tr(bank[3][:, k * P:(k + 1) * P], prob[:, slot, k * P:(k + 1) * P], ident[:, :])
                last.then_inc(pT_done, 1)

            def values(m):
                copied(pe, m)
                h, i = divmod(m, 4)
                if m < A_ITEMS:
                    width, col = HD, h * HD
                    if i == 0 and h >= 2:
                        pe.wait_ge(o_done, h - 1)
                else:
                    d = h - 8
                    width, col = P, 512 + d * P
                    if i == 0 and d < 2:
                        pe.wait_ge(o_done, 7 + d)
                    elif i == 0:
                        bn.wait(pe, "o", d - 2)
                    if m == A_ITEMS + 8:
                        pe.wait_ge(v_evac, 4)
                for k in range(i + 1):
                    last = mm(bank[4 + h % 2][:, i * width:(i + 1) * width], probT[:, m % 2, k * P:(k + 1) * P],
                              vtok[:, k, col:col + width], start=k == 0, stop=k == i)
                last.then_inc(pv_done, 1)

            def output_tile(c):
                if c < 4:
                    src = oA[c]
                    if c == 0:
                        pe.wait_ge(v_evac, 4)
                    pe.wait_ge(o_done, 2 * c + 2)
                else:
                    src = oB
                    bn.wait(pe, "o", c - 4)
                    copied(pe, {4: 43, 5: 45}.get(c, ITEMS - 1))
                if c >= 2:
                    pe.wait_ge(oa_lo, c - 1 if c < 4 else c)
                for i in range(TT):
                    last = tr(bank[OUT_BANK[c]][:, i * P:(i + 1) * P], src[:, i, :], ident[:, :])
                last.then_inc(oT_done, 1)

            def output_part(u, k):
                unit_features(pe, ATT_OUT // 2, u, 1, act_hi, act_lo, (6, 0)[u], ready=(oa_lo, 0), k0=k, w0=k,
                              first=k == 0, last=k == 7, part=k < 7, free=((oa_lo, 4), (neg_done, 64))[u] if k == 0 else None)

            for u in (4, 5):
                unit_tokens(pe, u // 2, u % 2, 4 + 2 * (u % 2), free=((r_ready, 1), (lam_v, 4))[u - 4])
                if u == 4:
                    pe.wait_ge(qk_evac, 4)
                    for n in range(3):
                        scores(n)
            pe.wait_ge(v_evac, 1)

            for m in range(ITEMS):
                unit, ks = unit_of_step(m)
                half = 0
                def projections(ks):
                    for k in ks:
                        free = None
                        if k == 0:
                            before = unit - 1
                            free = (qk_evac, ROPE_AT[before] + 1) if before in ROPE_AT else (v_evac, V_UNITS.index(before) + 1)
                        if unit in ROPE_AT:
                            unit_features(pe, unit // 2, unit % 2, 1, act_hi, act_lo, 6, k0=k, w0=k, first=k == 0,
                                          last=k == KT - 1, rope_cols=True, free=free, part=k < KT - 1)
                        else:
                            unit_tokens(pe, unit // 2, unit % 2, 6, free=free, ks=(k,))
                transposes(m)
                for n in scores_of_step(m):
                    scores(n)
                projections(ks[0:1])
                if m:
                    if m == 1:
                        pe.wait_ge(v_evac, 2)
                    values(m - 1)
                projections(ks[1:])
                if m in OUT_AT:
                    output_tile(OUT_AT[m])
                if m >= 43:
                    output_part(0, m - 43)
            values(ITEMS - 1)
            output_part(0, 5)
            output_tile(6)
            for k in range(6):
                output_part(1, k)
            output_tile(7)
            for u in range(2):
                output_part(u, 6)
                output_part(u, 7)

            def out_projection(base, ready, b):
                for u in range(2 if base == ATT_OUT else 0, 4):
                    unit_features(pe, base // 2 + u // 2, u % 2, KT, act_hi, act_lo,
                                  2 * (u % 2) + (2 if base == ATT_OUT else 0),
                                  ready=ready if u == 0 else None,
                                  free=(m_evac, KT * (b - 1) + 2 * (u - 1)) if u >= 2 and base != ATT_OUT else None)
                post_pe(pe, b)

            def ffn(layer):
                b = 1 + 2 * layer
                fv = fvs[layer]

                def pair(i):
                    peeled = isinstance(i, int)
                    for s in range(2):
                        unit_features(pe, i + FFN_IN[layer] // 2, s, KT, act_hi, act_lo, 2 * s,
                                      ready=(x_lo, KT * b) if peeled and s == 0 else None,
                                      free=None if peeled else (fv.sem, i * len(fv.names) - (len(fv.names) - fv.at["g1" if s == 0 else "u1"])))
                        if peeled and s == 0:
                            stat_pe(pe, b)
                pair(0)
                with pe.Fori(1, FFN // UC) as i:
                    pair(i)
                with pe.Fori(0, 2) as i:
                    for v in range(6):
                        m, kc = divmod(v, 3)
                        nk = min(8, FT - 8 * kc)
                        if kc == 0:
                            fv.wait(pe, "u1", FFN // UC - 1)
                            if m == 0:
                                pe.wait_ge(m_evac, i * 4 + KT * b - 2) if b else None
                            else:
                                pe.wait_ge(m_evac, i * 4 + KT * b)
                        fv.wait(pe, "lo1", (8 * kc + nk) // 2 - 1)
                        unit_features(pe, i * 3 + (FFN_OUT[layer] // 2 + v // 2), v % 2, nk, hid_hi, hid_lo,
                                      2 * m, k0=8 * kc, first=kc == 0, last=kc == 2)
                post_pe(pe, b + 1)

            out_projection(ATT_OUT, (oa_lo, 0), 1)
            ffn(0)

            for u in range(4):
                unit_tokens(pe, REC_IN // 2 + u // 2, u % 2, 2 * (u % 2),
                            ready=(x_lo, 2 * KT) if u == 0 else None,
                            free=(rv_evac, u - 1) if u >= 2 else (m_evac, 2 * KT))
                if u == 0:
                    stat_pe(pe, 2)

            def qf_pair(j):
                for s in range(2):
                    unit_features(pe, j + (REC_IN // 2 + 2), s, KT, act_hi, act_lo, 2 * s,
                                  free=(rv_evac, 3 + s) if isinstance(j, int) else (s_qf, j * 2 + (s - 1)))

            def heads(j):
                for a in range(2):
                    ev.wait(pe, "ke", j)
                    for c in range(3):
                        last = tr(bank[4 + a][:, c * P:(c + 1) * P], ke_sb[:, a, c * P:(c + 1) * P], ident[:, :])
                    ht.done(last, f"keT{a}")
                for a in range(2):
                    for c in range(TT):
                        cs = slice(c * P, (c + 1) * P)
                        last = mm(bank[6 + a][:, cs], k_sb[:, a, cs], q_sb[:, a, cs], start=True, stop=True)
                    ht.done(last, f"diag{a}")
                for l in range(NL):
                    for a in range(2):
                        if a == 0:
                            ev.wait(pe, f"mq{l}", j)
                            ep.wait(pe, f"mk{l}", j)
                        hs.wait(pe, f"diag{a}" if l == 0 else f"lev{l - 1}_{a}", j)
                        for c in range(TT):
                            m = m_sb[:, l % 4, a, c * P:(c + 1) * P]
                            last = mm(bank[6 + a][:, c * P:(c + 1) * P], m, m, start=True, stop=True)
                        ht.done(last, f"lev{l}_{a}")
                for a in range(2):
                    hk.wait(pe, f"keT{a}", j)
                    for c in range(3):
                        last = mm(bank[4 + a][:, c * P:(c + 1) * P], keT[:, a, c, :],
                                  rv[:, c, bass.ds(j * UC + a * P, P)], start=True, stop=True)
                    ht.done(last, f"u{a}")
                for a in range(2):
                    hs.wait(pe, f"lev{NL - 1}_{a}", j)
                    ho.wait(pe, f"s3_{a}", j)
                    for c in range(TT):
                        cs = slice(c * P, (c + 1) * P)
                        last = mm(bank[6 + a][:, cs], att[:, a, cs], rv[:, c, bass.ds(j * UC + a * P, P)],
                                  start=True, stop=c == 0)
                        if c:
                            last = mm(bank[6 + a][:, cs], qb_sb[:, a, cs], state[:, a, c - 1, :],
                                      start=False, stop=True)
                    ht.done(last, f"o{a}")
                hk.wait(pe, "osq1", j)

            def gates(u, free):
                unit_tokens(pe, REC_IN // 2 + 6 + u // 2, u % 2, 2 * (u % 2), free=free)

            def gated_transposes(u):
                pe.wait_ge(g_mul, 8 * (u + 1))
                for h in range(2):
                    if 2 * u + h >= 2:
                        pe.wait_ge(gT_lo, 2 * u + h - 1)
                    for t in range(TT):
                        last = tr(bank[4 + h][:, t * P:(t + 1) * P], og[:, u % 2, t, h * P:(h + 1) * P], ident[:, :])
                    last.then_inc(gT_done, 1)

            qf_pair(0)
            with pe.Fori(1, 4) as j:
                qf_pair(j)
                heads(j - 1)
            gates(0, (s_qf, 8))
            gates(1, None)
            heads(3)
            gates(2, (g_silu, 4))
            gates(3, (g_silu, 8))
            for u in range(4):
                gated_transposes(u)
            out_projection(REC_OUT, (gT_lo, 0), 3)
            ffn(1)
            for c in range(KT):
                pe.wait_ge(x_new, 4 * KT + c + 1)
                b = (0, 1, 2, 3, 5, 6, 7, 4)[c]
                for t in range(TT):
                    last = tr(bank[b][:, t * P:(t + 1) * P], xres[:, c, t * P:(t + 1) * P], ident[:, :])
                last.then_inc(yT_done, 1)

        @block.gpsimd
        def _(pool):
            g = nc.gpsimd
            g.memset(ones[:, :], 1.0)
            g.memset(eps_col[:, :], EPS)
            g.memset(one_col[:, :], 1.0).then_inc(setup, 1)
            squares_pool(pool, 0)

            for n, (p, s) in enumerate(ROPE_UNITS.values()):
                pool.wait_ge(rope_mul, 2 * (n + 1))
                g.tensor_tensor(rope[:, p, s, 0, :], rtmp[:, 0, :], rtmp[:, 3, :], ALU.subtract).then_inc(rope_out, 1)
                g.tensor_tensor(rope[:, p, s, 1, :], rtmp[:, 1, :], rtmp[:, 2, :], ALU.add).then_inc(rope_out, 1)
            squares_pool(pool, 1)
            pool.wait_ge(m_mm, 2)
            g.memset(rzero[:, :], 1.0).then_inc(setup, 1)
            pool.wait_ge(setup, 2)
            g.memset(rzero[:, :].rearrange("p (c t) -> p c t", t=CH)[:, :, 0:1], 0.0).then_inc(setup, 1)
            squares_pool(pool, 2)

            def level_keys(j):
                for l, L in enumerate(LEVELS):
                    ea.wait(pool, f"es{l}", j)
                    if l >= 4:
                        ht.wait(pool, f"lev{l - 4}_1", j)
                    elif not isinstance(j, int):
                        ht.wait(pool, f"lev{l + 4 if l < 3 else 3}_1", j - 1)
                    v = lambda ap: ap.rearrange("p a t -> p (a t)").rearrange("p (b h t) -> p b h t", h=2, t=L)[:, :, 0, :]
                    ep.done(g.tensor_tensor(v(m_sb[:, l % 4]), v(e_sb[:, l % 2]), v(k_sb[:, :, :]), ALU.mult), f"mk{l}")
            level_keys(0)
            with pool.Fori(1, 4) as j:
                level_keys(j)
            squares_pool(pool, 3)

        @block.scalar
        def _(act):
            A = nc.scalar.activation
            act.preload_act_table_set(EXP_LN)
            act.dma_start(ident[:, :], ident_in).then_inc(ident_in_sem, 16)
            act.dma_start(colsrc[C_GAIN:C_GAIN + 64, :], norm_gains.rearrange("l n (k p) -> (l n k) p", p=P)).then_inc(small_in, 16)
            act.dma_start(colsrc[C_SUB:C_SUB + 1, :], att_subln).then_inc(small_in, 16)
            act.dma_start(colsrc[C_GN:C_GN + 1, :], rec_gnorm).then_inc(small_in, 16)
            act.dma_start(colsrc[C_LB:C_LB + 8, :], rec_lower_bounds.rearrange("a (h p) -> (a h) p", p=P)).then_inc(small_in, 16)
            act.dma_start(lam_in[0:1, :, :], att_lambda).then_inc(small_in, 16)
            act.dma_start(cosr[:, :], cos_t).then_inc(rope_in, 16)
            act.dma_start(sinr[:, :], sin_t).then_inc(rope_in, 16)
            act.dma_start(mskA[:, :], mask_a).then_inc(masks_in, 16)
            act.dma_start(mskB[:, :], mask_b).then_inc(masks_in, 16)
            act.wait_ge(colsT, 1)
            A(cols[:, :], bank[7][:, 0:C_ALL], ACT.Copy).then_inc(colsR, 1)
            act.wait_ge(colsR, 1)
            for c in range(KT):
                tile_act(act, 0, c)
                if c == 1:
                    split_hi(act, 0, 0, True)
            act.wait_ge(lam_v, 2)
            A(lam_s[0:1, 2:4], lam_s[0:1, 0:2], ACT.Exp).then_inc(lam_a, 1)

            def evac_qk(u, banks):
                n = ROPE_AT[u]
                act.wait_ge(unit_done, u + 1)
                if n:
                    act.wait_ge(rope_out, 2 * n)
                for h in range(2):
                    last = A(rtmp[:, h, :], bank[banks + h][:, :], ACT.Copy)
                last.then_inc(qk_evac, 1)
            split_hi(act, 0, 1, True)
            stat_act(act, 0)
            for u in range(4):
                split_hi(act, (u + 2) // 2, u % 2, u + 2 in ROPE_AT)
                evac_qk(u, 2 * (u % 2))

            def tokens_evac(u, unit, dst, base, count, stat, banks, tiles=range(TT)):
                act.wait_ge(r_ready, stat + 1)
                act.wait_ge(unit_done, unit + 1)
                for t in tiles:
                    last = A(dst[:, t, base:base + UC], bank[banks + 2 * (u % 2) + t // 2][:, (t % 2) * UC:(t % 2 + 1) * UC],
                             ACT.Copy, scale=rT[:, t:t + 1])
                last.then_inc(count, 1)
            def exponential(n):
                _, _, i, row = score(n)
                act.wait_ge(neg_done, n + 1)
                A(prob[:, n % 8, 0:(i + 1) * P], prob[:, n % 8, 0:(i + 1) * P], ACT.Exp, scale=-1.0,
                  bias=nmax[:, row, i:i + 1], accum_out=rsum[:, row, i:i + 1]).then_inc(p_done, 1)

            def copy_pT(m):
                N = (m % 4 + 1) * P
                act.wait_ge(pT_done, m + 1)
                if m >= 2:
                    act.wait_ge(pv_done, m - 1)
                A(probT[:, m % 2, 0:N], bank[3][:, 0:N], ACT.Copy).then_inc(pT_act, 1)

            def output_hi(c):
                act.wait_ge(oT_done, c + 1)
                A(act_hi[:, c, :], bank[OUT_BANK[c]][:, :], ACT.Copy,
                  scale=1.0 if c < 4 else lam_s[:, 6:7]).then_inc(oa_hi, 1)

            def norm_squares(d):
                act.wait_ge(pv_done, A_ITEMS + 4 * (d + 1))
                bna.done(A(osq[:, :], bank[4 + d % 2][:, :], ACT.Square), "sq")

            def norm_root(d):
                bn.wait(act, "ss_eps", d)
                bna.done(A(oss[:, 1, :], oss[:, 0, :], ACT.Ln, scale=1.0 / P), "ln")
                bna.wait(act, "ln", d)
                bna.done(A(oss[:, 2, :], oss[:, 1, :], ACT.Exp, scale=-0.5), "r")

            tokens_evac(0, 4, vtok, 0, v_evac, 0, 4)
            split_hi(act, 3, 0, True)
            for n in range(3):
                exponential(n)
            tokens_evac(1, 5, vtok, UC, v_evac, 0, 4)
            for m in range(ITEMS):
                if m >= A_ITEMS or m % 4 != 3:
                    copy_pT(m)
                for n in scores_of_step(m):
                    exponential(n)
                u = evac_of_step(m)
                if u in ROPE_AT:
                    evac_qk(u, 6)
                elif u is not None:
                    tokens_evac(1, u, vtok, V_UNITS.index(u) * UC, v_evac, 0, 4)
                if split_of_step(m, 0):
                    u, half = split_of_step(m, 0)
                    split_hi(act, u // 2, u % 2, u in ROPE_AT, half)
                d, phase_ = divmod(m - A_ITEMS - 4, 4)
                if d >= 0 and phase_ == 0:
                    norm_squares(d)
                elif d >= 0 and phase_ == 1:
                    norm_root(d)
                if m in OUT_AT:
                    output_hi(OUT_AT[m])
            output_hi(6)
            norm_squares(3)
            norm_root(3)
            output_hi(7)

            def out_projection(base, b, mix):
                for u in range(4):
                    if u == 2 or u == 0 and base != ATT_OUT:
                        split_hi(act, base // 2 + u // 2, 1)
                    banks = (6, 0, 2, 4)[u] if base == ATT_OUT else 2 * (u % 2)
                    mixer_evac_act(act, b, mix, base + u, 2 * u, banks)
                    if u % 2 == 0:
                        split_hi(act, base // 2 + u // 2 + 1, 0)
                post_act(act, b)

            def ffn(layer):
                b = 1 + 2 * layer
                fv, fa = fvs[layer], fas[layer]
                base = FFN_IN[layer] // 2

                def pair(i):
                    split_hi(act, i + base, 1)
                    if isinstance(i, int):
                        stat_act(act, b)
                    for m in range(2):
                        fv.wait(act, f"g{m}", i)
                        fa.done(A(f_g[:, m, :], f_g[:, m, :], ACT.Silu), f"s{m}")
                    split_hi(act, i + (base + 1), 0)
                    for m in range(2):
                        fv.wait(act, f"h{m}", i)
                        fa.done(A(hid_hi[:, bass.ds(i * 2 + m, 1), :].rearrange("p a t -> p (a t)"),
                                  f_g[:, m, :], ACT.Copy), f"hi{m}")
                pair(0)
                with act.Fori(1, FFN // UC) as i:
                    pair(i)
                act.preload_act_table_set(EXP_LN)
                base = FFN_OUT[layer] // 2

                def six_units(i):
                    for v in range(6):
                        m, kc = divmod(v, 3)
                        if v % 2 == 0:
                            split_hi(act, i * 3 + (base + v // 2), 1)
                        if kc == 2:
                            mixer_evac_act(act, b + 1, mix_ffn, i * 6 + (FFN_OUT[layer] + v), i * 4 + 2 * m, 2 * m)
                        if v % 2 == 0:
                            split_hi(act, i * 3 + (base + v // 2 + 1), 0)
                if layer == 0:
                    with act.Fori(0, 2) as i:
                        six_units(i)
                else:
                    six_units(0)
                    six_units(1)
                post_act(act, b + 1)

            out_projection(ATT_OUT, 1, mix_att)
            ffn(0)

            for u in range(4):
                pair = REC_IN // 2 + u // 2
                if u % 2 == 0:
                    split_hi(act, pair, 1)
                if u == 0:
                    stat_act(act, 2)
                    act.wait_ge(lb_v, 1)
                    A(lb[:, 1, :], lb[:, 0, :], ACT.Exp).then_inc(lb_a, 1)
                tokens_evac(u, REC_IN + u, rv, u * UC, rv_evac, 2, 0)
                if u % 2 == 0:
                    split_hi(act, pair + 1, 0)

            flat = lambda ap: ap.rearrange("p a t -> p (a t)")
            blocks = lambda ap, L: flat(ap).rearrange("p (b h t) -> p b h t", h=2, t=L)

            def level_exps(j, ls):
                for l in ls:
                    ev.wait(act, f"d{l}", j)
                    for x, h, sgn in (("et", 1, 1.0), ("es", 0, -1.0)):
                        v = blocks(e_sb[:, l % 2], LEVELS[l])[:, :, h, :]
                        ea.done(A(v, v, ACT.Exp, scale=sgn), f"{x}{l}")

            def gates_and_decays(j):
                for x, src, e, s in (("q", q_sb, 0, 1), ("f", k_sb, 1, 2)):
                    v = flat(e_sb[:, e])
                    act.wait_ge(s_qf, j * 2 + s)
                    ea.done(A(v, flat(src[:, :, :]), ACT.Exp, scale=-1.0), f"{x}e")
                    ea.wait(act, f"{x}e", j)
                    ea.done(A(v, v, ACT.Ln, bias=one_col[:, :]), f"{x}l")
                    ea.wait(act, f"{x}l", j)
                    ea.done(A(v, v, ACT.Exp, scale=-1.0), f"{x}s")
                ev.wait(act, "key", j)
                ea.done(A(flat(e_sb[:, 1]), flat(e_sb[:, 1]), ACT.Ln), "g")
                ev.wait(act, "scan", j)
                ea.done(A(flat(qb_sb[:, :, :]), flat(b_sb[:, :, :]), ACT.Exp), "eb")
                ea.done(A(ebl[:, :, :], b_sb[:, :, :].rearrange("p a (c t) -> p a c t", t=CH)[:, :, :, CH - 1], ACT.Exp), "ebl")
                ev.wait(act, "dke", j)
                ea.done(A(flat(ke_sb[:, :, :]), flat(ke_sb[:, :, :]), ACT.Exp, scale=-1.0), "eke")
                level_exps(j, range(4))

            def heads(j):
                for a in range(2):
                    ht.wait(act, f"keT{a}", j)
                    hk.done(A(keT[:, a, :, :].rearrange("p c t -> p (c t)"), bank[4 + a][:, 0:3 * P], ACT.Copy), f"keT{a}")
                level_exps(j, range(4, NL))
                for a in range(2):
                    ht.wait(act, f"o{a}", j)
                    v = bank[6 + a][:, :].rearrange("p (c t) -> p c t", c=TT)
                    hk.done(A(ro[:, :, bass.ds(j * UC + a * P, P)], v, ACT.Copy), f"ocopy{a}")
                    if a:
                        ho.wait(act, "ss0", j)
                    elif not isinstance(j, int):
                        pass
                    hk.done(A(r_sq[:, :], bank[6 + a][:, :], ACT.Square), f"osq{a}")

            split_hi(act, qf, 1)
            split_hi(act, qf + 1, 0)
            with act.Fori(1, 4) as j:
                split_hi(act, j + qf, 1)
                gates_and_decays(j - 1)
                split_hi(act, j + (qf + 1), 0)
                heads(j - 1)
            split_hi(act, qf + 4, 1)
            gates_and_decays(3)
            split_hi(act, qf + 5, 0)
            heads(3)
            ho.wait(act, "ss1", 3)
            A(r_rs[:, 1, :, :], r_rs[:, 0, :, :], ACT.Ln, scale=1.0 / P, bias=eps_col[:, :]).then_inc(rrs_a, 1)
            act.wait_ge(rrs_a, 1)
            A(r_rs[:, 2, :, :], r_rs[:, 1, :, :], ACT.Exp, scale=-0.5).then_inc(rrs_a, 1)

            def gate_silu(u):
                act.wait_ge(unit_done, REC_IN + 12 + u + 1)
                if u >= 2:
                    act.wait_ge(g_mul, 8 * (u - 1))
                for t in range(TT):
                    A(gate[:, u % 2, t, :], bank[2 * (u % 2) + t // 2][:, (t % 2) * UC:(t % 2 + 1) * UC],
                      ACT.Silu, scale=rT[:, t:t + 1]).then_inc(g_silu, 1)
            gate_silu(0)
            split_hi(act, qf + 5, 1)
            gate_silu(1)
            gate_silu(2)
            split_hi(act, qf + 6, 0)
            gate_silu(3)
            for c in range(KT):
                act.wait_ge(gT_done, c + 1)
                A(act_hi[:, c, :], bank[4 + c % 2][:, :], ACT.Copy, scale=cols[:, C_GN:C_GN + 1]).then_inc(gT_hi, 1)
            act.preload_act_table_set(EXP_LN)
            out_projection(REC_OUT, 3, mix_rec)
            ffn(1)
            for c in range(KT):
                act.wait_ge(yT_done, c + 1)
                b = (0, 1, 2, 3, 5, 6, 7, 4)[c]
                A(y_out[:, :, c * P:(c + 1) * P], bank[b][:, :].rearrange("p (a f) -> p a f", a=TT), ACT.Copy).then_inc(y_copied, 1)

        @block.vector
        def _(dve):
            V = nc.vector
            TTo, STT, TS = V.tensor_tensor, V.scalar_tensor_tensor, V.tensor_scalar
            turn = [0]

            def waited(dve):
                turn[0] += 1
                k = turn[0] % 8
                V.memset(pad[:, k:k + 1], 0.0)

            dve.wait_ge(small_in, 16 * 5)
            TTo(lam_in[0:1, 0, :], lam_in[0:1, 0, :], lam_in[0:1, 1, :], ALU.mult)
            TTo(lam_in[0:1, 2, :], lam_in[0:1, 2, :], lam_in[0:1, 3, :], ALU.mult).then_inc(lam_v, 1)
            dve.wait_ge(lam_v, 1)
            V.tensor_reduce(lam_s[0:1, 0:2], lam_in[0:1, :, :].rearrange("p (a b) d -> p a b d", b=2)[:, :, 0, :],
                            axis=AXX, op=ALU.add).then_inc(lam_v, 1)
            for c in range(KT + 1):
                if c < KT:
                    dve.wait_ge(xT_done, c + 1)
                    V.tensor_copy(xres[:, c, :], bank[c % 4][:, :]).then_inc(x_new, 1)
                if c >= 1:
                    tile_lo(dve, 0, c - 1)
                if c == 2:
                    split_lo(dve, 0, 0, True)
            dve.wait_ge(lam_a, 1)
            STT(out=lam_s[0:1, 4:5], in0=lam_s[0:1, 2:3], scalar=LAMBDA_INIT, in1=lam_s[0:1, 3:4],
                op0=ALU.add, op1=ALU.subtract).then_inc(lam_v, 1)
            dve.wait_ge(lam_t, 1)
            TS(lam_s[:, 5:6], bank[6][:, 0:1], -1.0, None, ALU.mult)
            dve.wait_ge(colsR, 1)
            TS(lam_s[:, 6:7], cols[:, C_SUB:C_SUB + 1], 1.0 - LAMBDA_INIT, None, ALU.mult).then_inc(lam_v, 1)
            split_lo(dve, 0, 1, True)
            dve.wait_ge(r_ready, 1)
            dve.wait_ge(rope_in, 32)
            TTo(cosr[:, :], cosr[:, :], rB[:, :], ALU.mult)
            TTo(sinr[:, :], sinr[:, :], rB[:, :], ALU.mult).then_inc(rope_tab, 1)
            dve.wait_ge(rope_tab, 1)

            def rotate(u, step):
                n = ROPE_AT[u]
                tab = (sinr, cosr)[step][:, :].unsqueeze(1).to_broadcast([P, 2, T])
                if step == 0:
                    dve.wait_ge(qk_evac, n + 1)
                else:
                    dve.wait_ge(rope_mul, 2 * n + 1)
                dst = rtmp[:, 2:4, :] if step == 0 else rtmp[:, 0:2, :]
                TTo(dst, rtmp[:, 0:2, :], tab, ALU.mult).then_inc(rope_mul, 1)
            for u in range(4):
                split_lo(dve, (u + 2) // 2, u % 2, u + 2 in ROPE_AT)
                rotate(u, 0)
                rotate(u, 1)

            def negated(n):
                _, _, i, row = score(n)
                N, msk = (i + 1) * P, mskA if n < A_ITEMS else mskB
                dve.wait_ge(sc_done, n + 1)
                if n >= 8:
                    dve.wait_ge(pT_done, n - 7 if n < A_ITEMS + 8 else A_ITEMS + (n - A_ITEMS) // 2 - 3)
                waited(dve)
                V.tensor_tensor_reduce(out=prob[:, n % 8, 0:N], in0=bank[n % 3][:, 0:N], in1=msk[:, T - N:T],
                                       scale=-SCALE, scalar=3e38, op0=ALU.add, op1=ALU.min,
                                       accum_out=nmax[:, row, i:i + 1]).then_inc(neg_done, 1)

            def copy_pT(m):
                dve.wait_ge(pT_done, m + 1)
                dve.wait_ge(pv_done, m - 1)
                V.tensor_copy(probT[:, m % 2, :], bank[3][:, :]).then_inc(pT_dve, 1)

            def head_out(h):
                row = 2 + h % 2
                dve.wait_ge(p_done, 4 * (h + 1))
                V.reciprocal(rinv[:, row, :], rsum[:, row, :]).then_inc(rinv_done, 1)
                dve.wait_ge(rinv_done, h + 1)
                dve.wait_ge(pv_done, 4 * (h + 1))
                TTo(oA[h // 2][:, :, HD * (h % 2):HD * (h % 2 + 1)], by_block(bank[4 + h % 2][:, 0:TT * HD]),
                    rinv[:, row, :].unsqueeze(2).to_broadcast([P, TT, HD]), ALU.mult).then_inc(o_done, 1)

            def weights(b):
                d, i = divmod(b, 4)
                N, q = (i + 1) * P, 2 * (d % 2)
                s0, r1 = rsum[:, q, i:i + 1], rinv[:, q + 1, i:i + 1]
                p0, p1 = prob[:, 2 * (b % 4), 0:N], prob[:, 2 * (b % 4) + 1, 0:N]
                dve.wait_ge(p_done, A_ITEMS + 2 * b + 2)
                bw.done(V.reciprocal(r1, rsum[:, q + 1, i:i + 1]), "rinv")
                bw.wait(dve, "rinv", b)
                bw.done(STT(out=r1, in0=s0, scalar=lam_s[:, 5:6], in1=r1, op0=ALU.mult, op1=ALU.mult), "ratio")
                bw.wait(dve, "ratio", b)
                bw.done(STT(out=p0, in0=p1, scalar=r1, in1=p0, op0=ALU.mult, op1=ALU.add), "w")

            def norm_sum(d):
                bna.wait(dve, "sq", d)
                s0 = rsum[:, 2 * (d % 2), :]
                bn.done(TTo(oss[:, 2, :], s0, s0, ALU.mult), "s2")
                bn.done(V.tensor_reduce(oss[:, 0, :], by_block(osq[:, :]), axis=AXX, op=ALU.add), "ss")
                bn.wait(dve, "ss", d)
                bn.done(STT(out=oss[:, 0, :], in0=oss[:, 2, :], scalar=EPS * P, in1=oss[:, 0, :],
                            op0=ALU.mult, op1=ALU.add), "ss_eps")

            def norm_out(d):
                bna.wait(dve, "r", d)
                if d:
                    dve.wait_ge(oT_done, 4 + d)
                bn.done(TTo(oB, by_block(bank[4 + d % 2][:, :]),
                            oss[:, 2, :].unsqueeze(2).to_broadcast([P, TT, P]), ALU.mult), "o")

            def output_lo(c):
                dve.wait_ge(oa_hi, c + 1)
                STT(out=act_lo[:, c, :], in0=bank[OUT_BANK[c]][:, :], scalar=1.0 if c < 4 else lam_s[:, 6:7],
                    in1=fview(act_hi[:, c, :]), op0=ALU.mult, op1=ALU.subtract).then_inc(oa_lo, 1)

            dve.wait_ge(lam_v, 4)
            dve.wait_ge(masks_in, 32)
            split_lo(dve, 3, 0, True)
            for n in range(3):
                negated(n)
            for m in range(ITEMS):
                if m < A_ITEMS and m % 4 == 3:
                    copy_pT(m)
                if A_ITEMS - 1 <= m < ITEMS - 1:
                    weights(m + 1 - A_ITEMS)
                if m - 1 in OUT_AT:
                    output_lo(OUT_AT[m - 1])
                for n in scores_of_step(m):
                    negated(n)
                for step in range(2):
                    if evac_of_step(m - step) in ROPE_AT:
                        rotate(evac_of_step(m - step), step)
                if m <= A_ITEMS and m % 4 == 0 and m:
                    head_out(m // 4 - 1)
                if split_of_step(m, 2):
                    u, half = split_of_step(m, 2)
                    split_lo(dve, u // 2, u % 2, u in ROPE_AT, half)
                d, phase_ = divmod(m - A_ITEMS - 4, 4)
                if d >= 0 and phase_ == 0:
                    norm_sum(d)
                if d >= 0 and phase_ == 3:
                    norm_out(d)
            output_lo(6)
            norm_sum(3)
            norm_out(3)
            output_lo(7)

            def out_projection(base, b, mix):
                mixer_zero_dve(dve, b)
                for u in range(4):
                    if u % 2 == 0:
                        if u == 2 or base != ATT_OUT:
                            split_lo(dve, base // 2 + u // 2, 1)
                        split_lo(dve, base // 2 + u // 2 + 1, 0)
                    mixer_sum_dve(dve, b, 2 * u)
                post_dve(dve, b, mix)

            def ffn(layer):
                b = 1 + 2 * layer
                fv, fa = fvs[layer], fas[layer]
                base = FFN_IN[layer] // 2

                def pair(i):
                    split_lo(dve, i + base, 1)
                    if isinstance(i, int):
                        dve.wait_ge(r_ready, b + 1)
                    dve.wait_ge(unit_done, i * 2 + (FFN_IN[layer] + 1))
                    for m in range(2):
                        if not isinstance(i, int):
                            fv.wait(dve, f"lo{m}", i - 1)
                        fv.done(TTo(f_g[:, m, :], bank[m][:, :], rB[:, :], ALU.mult), f"g{m}")
                    split_lo(dve, i + (base + 1), 0)
                    dve.wait_ge(unit_done, i * 2 + (FFN_IN[layer] + 2))
                    for m in range(2):
                        if m:
                            fv.wait(dve, "h0", i)
                        elif not isinstance(i, int):
                            fv.wait(dve, "h1", i - 1)
                        fv.done(TTo(f_u[:, :], bank[2 + m][:, :], rB[:, :], ALU.mult), f"u{m}")
                        fv.wait(dve, f"u{m}", i)
                        fa.wait(dve, f"s{m}", i)
                        fv.done(TTo(f_g[:, m, :], f_g[:, m, :], f_u[:, :], ALU.mult), f"h{m}")
                    for m in range(2):
                        fa.wait(dve, f"hi{m}", i)
                        dst, hi = (t[:, bass.ds(i * 2 + m, 1), :].rearrange("p a t -> p (a t)") for t in (hid_lo, hid_hi))
                        fv.done(TTo(dst, f_g[:, m, :], fview(hi), ALU.subtract), f"lo{m}")
                pair(0)
                with dve.Fori(1, FFN // UC) as i:
                    pair(i)
                mixer_zero_dve(dve, b + 1)
                base = FFN_OUT[layer] // 2

                def six_units(i):
                    for v in range(6):
                        m, kc = divmod(v, 3)
                        if v % 2 == 0:
                            split_lo(dve, i * 3 + (base + v // 2), 1)
                        if kc == 2:
                            mixer_sum_dve(dve, b + 1, i * 4 + 2 * m)
                        if v % 2 == 0:
                            split_lo(dve, i * 3 + (base + v // 2 + 1), 0)
                if layer == 0:
                    with dve.Fori(0, 2) as i:
                        six_units(i)
                else:
                    six_units(0)
                    six_units(1)
                post_dve(dve, b + 1, mix_ffn)

            out_projection(ATT_OUT, 1, mix_att)
            ffn(0)

            lbc = cols[:, C_LB:C_LB + 8]
            TTo(lb[:, 0, :], lbc, lbc, ALU.subtract).then_inc(lb_v, 1)
            split_lo(dve, REC_IN // 2, 1)
            dve.wait_ge(lb_a, 1)
            V.reciprocal(lb[:, 2, :], lb[:, 1, :]).then_inc(lb_v, 1)
            dve.wait_ge(lb_v, 2)
            TTo(lb[:, 1, :], lb[:, 1, :], lb[:, 2, :], ALU.mult).then_inc(lb_v, 1)
            dve.wait_ge(lb_v, 3)
            TTo(lb[:, 3, :], lb[:, 1, :], lb[:, 1, :], ALU.subtract).then_inc(lb_v, 1)
            dve.wait_ge(lb_v, 4)
            TS(lb[:, 4, :], lb[:, 3, :], -1.0, 1.0, ALU.mult, ALU.add).then_inc(lb_v, 1)
            split_lo(dve, REC_IN // 2 + 1, 0)
            split_lo(dve, REC_IN // 2 + 1, 1)
            split_lo(dve, REC_IN // 2 + 2, 0)

            flat = lambda ap: ap.rearrange("p a t -> p (a t)")
            blocks = lambda ap, L: flat(ap).rearrange("p (b h t) -> p b h t", h=2, t=L)
            chunks = lambda ap: flat(ap).rearrange("p (c t) -> p c t", t=CH)

            def qf_evac(j):
                for s, dst in ((0, q_sb), (1, k_sb)):
                    dve.wait_ge(unit_done, j * 2 + (REC_IN + 4 + s + 1))
                    for a in range(2):
                        last = TTo(dst[:, a, :], bank[2 * s + a][:, :], rB[:, :], ALU.mult)
                    last.then_inc(s_qf, 1)

            def diff(j, l):
                L = LEVELS[l]
                if l >= 2:
                    ev.wait(dve, f"mq{l - 2}", j)
                    ep.wait(dve, f"mk{l - 2}", j)
                else:
                    ev.wait(dve, "scan", j)
                v = flat(b_sb[:, :, :]).rearrange("p (b t) -> p b t", t=2 * L)
                ev.done(TTo(flat(e_sb[:, l % 2]).rearrange("p (b t) -> p b t", t=2 * L), v,
                            v[:, :, L - 1:L].to_broadcast([P, 2 * T // (2 * L), 2 * L]), ALU.subtract), f"d{l}")

            def queries(j, l):
                ea.wait(dve, f"et{l}", j)
                if l >= 4:
                    ht.wait(dve, f"lev{l - 4}_1", j)
                v = lambda ap: blocks(ap, LEVELS[l])[:, :, 1, :]
                ev.done(TTo(v(m_sb[:, l % 4]), v(e_sb[:, l % 2]), v(q_sb[:, :, :]), ALU.mult), f"mq{l}")

            def gates_and_decays(j):
                ea.wait(dve, "qs", j)
                ev.done(STT(out=flat(q_sb[:, :, :]), in0=flat(q_sb[:, :, :]), scalar=float(P) ** -0.5,
                            in1=flat(e_sb[:, 0]), op0=ALU.mult, op1=ALU.mult), "qgate")
                ea.wait(dve, "fs", j)
                for a in range(2):
                    col = lambda r: lb[:, r, bass.ds(j * 2 + a, 1)]
                    last = TS(e_sb[:, 1, a, :], e_sb[:, 1, a, :], col(4), col(3), ALU.mult, ALU.add)
                ev.done(last, "forget")
                ev.wait(dve, "forget", j)
                ev.done(TS(flat(k_sb[:, :, :]), flat(e_sb[:, 1]), -1.0, 1.0, ALU.mult, ALU.add), "key")
                ea.wait(dve, "g", j)
                dve.wait_ge(setup, 3)
                ev.done(V.tensor_tensor_scan(flat(b_sb[:, :, :]), rzero[:, :], flat(e_sb[:, 1]), 0.0,
                                             ALU.mult, ALU.add), "scan")
                ev.wait(dve, "scan", j)
                ev.done(TTo(chunks(ke_sb[:, :, :]), chunks(b_sb[:, :, :]),
                            chunks(b_sb[:, :, :])[:, :, CH - 1:CH].to_broadcast([P, 2 * TT, CH]), ALU.subtract), "dke")
                diff(j, 0)
                ea.wait(dve, "eb", j)
                ev.done(TTo(flat(qb_sb[:, :, :]), flat(qb_sb[:, :, :]), flat(q_sb[:, :, :]), ALU.mult), "qb")
                ea.wait(dve, "eke", j)
                ev.done(TTo(flat(ke_sb[:, :, :]), flat(ke_sb[:, :, :]), flat(k_sb[:, :, :]), ALU.mult), "ke")
                diff(j, 1)
                queries(j, 0)
                diff(j, 2)
                queries(j, 1)
                diff(j, 3)
                queries(j, 2)
                queries(j, 3)

            def select(j, name, l, a):
                ht.wait(dve, name, j)
                v = lambda ap: ap.rearrange("p (c t) -> p c t", t=CH)
                if l is None:
                    hs.done(TTo(v(att[:, a, :]), v(bank[6 + a][:, :]),
                                ident[:, :].unsqueeze(1).to_broadcast([P, TT, P]), ALU.mult), name)
                else:
                    hs.wait(dve, f"diag{a}" if l == 0 else f"lev{l - 1}_{a}", j)
                    if not isinstance(j, int):
                        waited(dve)
                    hs.done(V.copy_predicated(v(att[:, a, :]), rmask[:, l, :].unsqueeze(1).to_broadcast([P, TT, P]),
                                              v(bank[6 + a][:, :])), name)

            def heads(j, then):
                lev = lambda l: [select(j, f"lev{l}_{a}", l, a) for a in range(2)]
                for a in range(2):
                    select(j, f"diag{a}", None, a)
                diff(j, 4)
                lev(0)
                diff(j, 5)
                queries(j, 4)
                lev(1)
                diff(j, 6)
                queries(j, 5)
                lev(2)
                queries(j, 6)
                lev(3)
                if then is not None:
                    ev.wait(dve, "mq6", j)
                    ep.wait(dve, "mk6", j)
                    qf_evac(then)
                for l in (4, 5, 6):
                    lev(l)
                for a in range(2):
                    ht.wait(dve, f"u{a}", j)
                    for c in range(1, 4):
                        u = bank[4 + a][:, (c - 1) * P:c * P]
                        if c == 1:
                            ho.done(V.tensor_copy(state[:, a, 0, :], u), f"s1_{a}")
                        else:
                            ho.wait(dve, f"s{c - 1}_{a}", j)
                            ho.done(STT(out=state[:, a, c - 1, :], in0=state[:, a, c - 2, :],
                                        scalar=ebl[:, a, c - 1:c], in1=u, op0=ALU.mult, op1=ALU.add), f"s{c}_{a}")
                for a in range(2):
                    hk.wait(dve, f"osq{a}", j)
                    ho.done(V.tensor_reduce(r_rs[:, 0, bass.ds(j * 2 + a, 1), :].rearrange("p a c -> p (a c)"),
                                            r_sq[:, :].rearrange("p (c v) -> p c v", c=TT), axis=AXX, op=ALU.add), f"ss{a}")

            dve.wait_ge(rmask_in, 16)
            V.tensor_copy(rmask[:, :, :], flat(qb_sb[:, :, :])[:, 0:NL * P].rearrange("p (l t) -> p l t", l=NL)).then_inc(rmask_ready, 1)
            dve.wait_ge(rmask_ready, 1)
            split_lo(dve, qf, 1)
            qf_evac(0)
            split_lo(dve, qf + 1, 0)
            with dve.Fori(1, 4) as j:
                split_lo(dve, j + qf, 1)
                gates_and_decays(j - 1)
                split_lo(dve, j + (qf + 1), 0)
                heads(j - 1, j)
            split_lo(dve, qf + 4, 1)
            gates_and_decays(3)
            split_lo(dve, qf + 5, 0)
            heads(3, None)

            def gate_mul(u):
                dve.wait_ge(rrs_a, 2)
                if u >= 2:
                    dve.wait_ge(gT_done, 2 * (u - 1))
                for t in range(TT):
                    dve.wait_ge(g_silu, 4 * u + t + 1)
                    for h in range(2):
                        hs_ = slice(h * P, (h + 1) * P)
                        STT(out=og[:, u % 2, t, hs_], in0=ro[:, t, (2 * u + h) * P:(2 * u + h + 1) * P],
                            scalar=r_rs[:, 2, 2 * u + h, t:t + 1], in1=gate[:, u % 2, t, hs_],
                            op0=ALU.mult, op1=ALU.mult).then_inc(g_mul, 1)

            def gated_lo(c):
                dve.wait_ge(gT_hi, c + 1)
                STT(out=act_lo[:, c, :], in0=bank[4 + c % 2][:, :], scalar=cols[:, C_GN:C_GN + 1],
                    in1=fview(act_hi[:, c, :]), op0=ALU.mult, op1=ALU.subtract).then_inc(gT_lo, 1)
            split_lo(dve, qf + 5, 1)
            gate_mul(0)
            gate_mul(1)
            split_lo(dve, qf + 6, 0)
            for u in range(2):
                gated_lo(2 * u)
                gated_lo(2 * u + 1)
                gate_mul(u + 2)
            for c in range(4, KT):
                gated_lo(c)
            out_projection(REC_OUT, 3, mix_rec)
            ffn(1)


def constants():
    half = HD // 2
    inv = (10000.0 ** (-np.arange(0, HD, 2, dtype=np.float32) / HD)).astype(np.float32)
    ang = np.arange(T, dtype=np.float32)[None, :] * inv[:, None]
    cos, sin = (np.tile(f(ang).astype(np.float32), (P // half, 1)) for f in (np.cos, np.sin))
    rel = (T - P) + np.arange(P)[:, None] - np.arange(T)[None, :]
    causal = rel >= 0
    held = sum(((rel <= w) & (rel % d == 0) & causal).astype(np.int64) for w, d in ((128, 1), (512, 4), (2048, 16)))
    mask_a = np.where(held > 0, np.log(np.maximum(held, 1)) / SCALE, -BIG).astype(np.float32)
    mask_b = np.where(causal, 0.0, -BIG).astype(np.float32)
    s, t = np.arange(P)[:, None], np.arange(P)[None, :]
    levels = np.stack([(s // (2 * L) == t // (2 * L)) & (s % (2 * L) < L) & (t % (2 * L) >= L) for L in LEVELS], 1)
    return dict(cos_t=cos, sin_t=sin, mask_a=mask_a, mask_b=mask_b, ident_in=np.eye(P, dtype=np.float32),
                level_masks=levels.reshape(P, NL * P).astype(np.float32))


_INS = ["x", "norm_gains", "att_w_in", "att_lambda", "att_subln", "att_w_out", "rec_w_in",
        "rec_lower_bounds", "rec_gnorm", "rec_w_out", "ffn_w_in", "ffn_w_out"]


def kernel(**inputs):
    import concourse.bacc as bacc
    from concourse.bass_utils import run_bass_kernel_spmd

    nc = bacc.Bacc("TRN2", target_bir_lowering=False, num_devices=1)
    given = {n: np.ascontiguousarray(inputs[n]) for n in _INS} | constants()
    arrays, args = {}, []
    for name, a in given.items():
        arrays[f"in_{name}"] = a
        args.append(nc.dram_tensor(f"in_{name}", a.shape, mybir.dt.from_np(a.dtype), kind="ExternalInput").ap())
    args.append(nc.dram_tensor("out_0", (1, T, D), F32, kind="ExternalOutput").ap())
    trunk(nc, *args)
    return run_bass_kernel_spmd(nc, [arrays], core_ids=[0]).results[0]["out_0"]
```

```python
from contextlib import ExitStack

import numpy as np

import concourse.bass as bass
from concourse import mybir

P = 128
F32 = mybir.dt.float32
F32R = mybir.dt.float32r
U8 = mybir.dt.uint8
ALU = mybir.AluOpType
ACT = mybir.ActivationFunctionType
AXX = mybir.AxisListType.X

D = 1024
T = 512
KT = D // P
TT = T // P
HD = 64
SCALE = HD ** -0.5
FFN = 2816
FT = FFN // P
UC = 256
EPS = 1e-6
LAMBDA_INIT = 0.8 - 0.6 * float(np.exp(-0.3 * 0.0))
BIG = 1e30
CH = 128
LEVELS = (64, 32, 16, 8, 4, 2, 1)
NL = len(LEVELS)
EXP_LN = "natural_log_exp_and_others"

ATT_IN = 0
ATT_OUT = ATT_IN + 12
FFN_IN = (ATT_OUT + 4, ATT_OUT + 4 + 22 + 12 + 16 + 4)
FFN_OUT = (FFN_IN[0] + 22, FFN_IN[1] + 22)
REC_IN = FFN_OUT[0] + 12
REC_OUT = REC_IN + 16
UNITS = FFN_OUT[1] + 12

C_GAIN, C_SUB, C_GN, C_LB, C_ALL = 0, 64, 65, 66, 74


class Steps:

    def __init__(self, sem, names):
        self.sem, self.names, self.k = sem, names, 0
        self.at = {n: k + 1 for k, n in enumerate(names)}
        assert len(self.at) == len(names)

    def wait(self, eng, name, i=0):
        eng.wait_ge(self.sem, i * len(self.names) + self.at[name])

    def done(self, ins, name):
        assert self.names[self.k % len(self.names)] == name, (name, self.names[self.k % len(self.names)])
        self.k += 1
        ins.then_inc(self.sem, 1)


def trunk(nc, x, norm_gains, att_w_in, att_lambda, att_subln, att_w_out, rec_w_in,
          rec_lower_bounds, rec_gnorm, rec_w_out, ffn_w_in, ffn_w_out,
          cos_t, sin_t, mask_a, mask_b, ident_in, level_masks, out):
    with ExitStack() as ctx:
        def sb(name, shape, dt=F32):
            return ctx.enter_context(nc.sbuf_tensor(name, shape, dt))

        def sem(name):
            return ctx.enter_context(nc.semaphore(name))

        def phase(*items):
            with ExitStack() as e:
                return [e.enter_context(nc.sbuf_tensor(n, s, d)) for n, s, d in items]

        bank = [ctx.enter_context(nc.psum_tensor(f"bank{i}", [P, T], F32)) for i in range(8)]

        xres = sb("xres", [P, KT, T])
        act_hi = sb("act_hi", [P, KT, T], F32R)
        (act_lo,) = phase(("act_lo", [P, KT, T], F32R))
        mix_ffn = sb("mix_ffn", [P, KT, T])
        raw = sb("raw", [P, 2, 8, UC])
        whi = sb("whi", [P, 2, 8, UC], F32R)
        wlo = sb("wlo", [P, 2, 8, UC], F32R)
        ident = sb("ident", [P, P])
        ones = sb("ones", [P, P])
        eps_col = sb("eps_col", [P, 1])
        one_col = sb("one_col", [P, 1])
        pad = sb("pad", [P, 8])
        cols = sb("cols", [P, C_ALL])
        rB = sb("rB", [P, T])
        rM = sb("rM", [P, T])
        rT = sb("rT", [P, TT])
        ln_tmp = sb("ln_tmp", [P, T])
        lnT_tmp = sb("lnT_tmp", [P, TT])
        sq_ring = sb("sq_ring", [P, 2, T])
        xsq = sb("xsq", [P, T])
        (msq,) = (sb("msq", [P, T]),)

        (rope, vtok, qk_st, mskA, mskB, cosr, sinr, rtmp, prob, probT, rsum, nmax, rinv, oss,
         lam_s) = phase(
             ("rope", [P, 4, 2, 2, T], F32), ("vtok", [P, TT, D], F32),
             ("qk_st", [P, 2, 2, T], F32), ("mskA", [P, T], F32), ("mskB", [P, T], F32),
             ("cosr", [P, T], F32), ("sinr", [P, T], F32), ("rtmp", [P, 4, T], F32),
             ("prob", [P, 8, T], F32), ("probT", [P, 2, T], F32),
             ("rsum", [P, 4, 4], F32), ("nmax", [P, 4, 4], F32), ("rinv", [P, 4, 4], F32),
             ("oss", [P, 3, TT], F32), ("lam_s", [P, 8], F32))
        x_in, _skip, lam_in, colsrc = phase(
            ("x_in", [P, TT, D], F32), ("_skip", [P, TT, D], F32), ("lam_in", [P, 4, HD], F32),
            ("colsrc", [P, P], F32))
        _skip, sqs = phase(("_first", [P, KT, T], F32), ("sqs", [P, KT, T], F32))
        by_block = lambda ap: ap.rearrange("p (i d) -> p i d", i=TT)
        oA = [by_block(ap) for ap in (sq_ring[:, 0, :], sq_ring[:, 1, :], xsq[:, :], msq[:, :])]
        osq, oB = ln_tmp, (by_block(rM[:, :]), by_block(rB[:, :]))
        (mix_att,) = phase(("mix_att", [P, KT, T], F32))
        hid_hi, hid_lo, f_g, f_u = phase(
            ("hid_hi", [P, FT, T], F32R), ("hid_lo", [P, FT, T], F32R),
            ("f_g", [P, 2, T], F32), ("f_u", [P, T], F32))
        (y_out,) = phase(("y_out", [P, TT, D], F32))
        (rv, rmask, rzero, lb, ro, b_sb, e_sb, m_sb, qb_sb, ke_sb, keT, att, state, r_sq,
         r_rs, ebl, q_sb, k_sb) = phase(
             ("rv", [P, TT, D], F32), ("rmask", [P, NL, P], U8),
             ("rzero", [P, 2 * T], F32), ("lb", [P, 5, 8], F32), ("ro", [P, TT, D], F32),
             ("b_sb", [P, 2, T], F32), ("e_sb", [P, 2, 2, T], F32),
             ("m_sb", [P, 4, 2, T], F32), ("qb_sb", [P, 2, T], F32), ("ke_sb", [P, 2, T], F32),
             ("keT", [P, 2, 3, P], F32), ("att", [P, 2, T], F32), ("state", [P, 2, 3, P], F32),
             ("r_sq", [P, T], F32), ("r_rs", [P, 3, 8, TT], F32), ("ebl", [P, 2, TT], F32),
             ("q_sb", [P, 2, T], F32), ("k_sb", [P, 2, T], F32))
        (mix_rec,) = phase(("mix_rec", [P, KT, T], F32))
        gate, og = phase(
            ("_rv", [P, TT, D], F32), ("_rm", [P, NL, P], U8), ("_rz", [P, 2 * T], F32),
            ("_lb", [P, 5, 8], F32), ("_ro", [P, TT, D], F32), ("gate", [P, 2, TT, UC], F32),
            ("og", [P, 2, TT, UC], F32))[-2:]

        raw_in = [sem("raw_in0"), sem("raw_in1")]
        w_hi = sem("w_hi")
        w_lo = sem("w_lo")
        unit_done = sem("unit_done")
        x_in_sem = [sem(f"x_in{t}") for t in range(TT)]
        rmask_ready = sem("rmask_ready")
        ident_in_sem, small_in, rope_in, masks_in, rmask_in = (
            sem("ident_in"), sem("small_in"), sem("rope_in"), sem("masks_in"), sem("rmask_in"))
        setup = sem("setup")
        colsT, colsR = sem("colsT"), sem("colsR")
        lam_v, lam_a, lam_t = sem("lam_v"), sem("lam_a"), sem("lam_t")
        xT_done = sem("xT_done")
        x_new = sem("x_new")
        x_hi, x_lo = sem("x_hi"), sem("x_lo")
        x_sq = sem("x_sq")
        x_sumA, x_sumB = sem("x_sumA"), sem("x_sumB")
        x_odd = sem("x_odd")
        stat_mm, stat_ln, r_ready = sem("stat_mm"), sem("stat_ln"), sem("r_ready")
        m_evac, m_acc = sem("m_evac"), sem("m_acc")
        m_copy = sem("m_copy")
        m_mm, m_ln, rM_ready, m_scaled = sem("m_mm"), sem("m_ln"), sem("rM_ready"), sem("m_scaled")
        rope_tab, rope_mul, rope_out, v_evac = (
            sem("rope_tab"), sem("rope_mul"), sem("rope_out"), sem("v_evac"))
        qk_evac = sem("qk_evac")
        qk_in = [sem("qk_in0"), sem("qk_in1")]
        qd_in = [sem("qd_in0"), sem("qd_in1")]
        sc_done, neg_done, p_done, pT_done = sem("sc_done"), sem("neg_done"), sem("p_done"), sem("pT_done")
        pT_act, pT_dve, pv_done, rinv_done, o_done = (
            sem("pT_act"), sem("pT_dve"), sem("pv_done"), sem("rinv_done"), sem("o_done"))
        oT_done, oa_hi, oa_lo = sem("oT_done"), sem("oa_hi"), sem("oa_lo")
        bw_done, bn_a, bn_v = sem("bw_done"), sem("bn_a"), sem("bn_v")
        yT_done, y_copied, y_out_sem = sem("yT_done"), sem("y_copied"), sem("y_out_sem")
        ffn_v = [sem("ffn_v0"), sem("ffn_v1")]
        ffn_a = [sem("ffn_a0"), sem("ffn_a1")]
        lb_v, lb_a = sem("lb_v"), sem("lb_a")
        rv_evac = sem("rv_evac")
        s_qf = sem("qf_evac")
        hg_v, hg_a, hg_p = sem("hg_v"), sem("hg_a"), sem("hg_p")
        hg_t, hg_s, hg_k, hg_o = sem("hg_t"), sem("hg_s"), sem("hg_k"), sem("hg_o")
        g_evac = sem("g_evac")
        g_silu, g_mul, gT_done, gT_hi, gT_lo = (
            sem("g_silu"), sem("g_mul"), sem("gT_done"), sem("gT_hi"), sem("gT_lo"))
        rrs_a = sem("rrs_a")

        fview = lambda ap: ap.bitcast(F32)

        def weight_rows(w, k0, nk, col):
            return w.rearrange("(k p) n -> p k n", p=P)[:, k0:k0 + nk, bass.ds(col, UC)]

        def load(sp, pair, slot, src):
            if not (isinstance(pair, int) and pair == 0):
                sp.wait_ge(w_lo, pair * 2 + (slot - 1))
            nk = src.shape[1]
            sp.dma_start(raw[:, slot, 0:nk, :], src).then_inc(raw_in[slot], 16)

        def of_unit(w, slot, halves, part):
            if not halves:
                v = w[:, slot, :, :]
                return v if part is None else v[:, 4 * part:4 * part + 4, :]
            v = w[:, slot, :, :].rearrange("p k n -> p (k n)")
            if w is raw:
                v = v.rearrange("p (kh a x) -> p a kh x", a=2, x=HD // 2)
            else:
                v = v.rearrange("p (a kh x) -> p a kh x", a=2, x=HD // 2)
            n = v.shape[2] // 2
            return v if part is None else v[:, :, n * part:n * part + n, :]

        def split_hi(act, pair, slot, halves=False, part=None):
            if isinstance(pair, int) and pair * 2 + slot >= UNITS:
                return
            if not (isinstance(pair, int) and pair == 0):
                act.wait_ge(unit_done, pair * 2 + (slot - 1))
            act.wait_ge(raw_in[slot], pair * 16 + 16)
            a = nc.scalar.activation(of_unit(whi, slot, halves, part), of_unit(raw, slot, halves, part), ACT.Copy)
            if part != 0:
                a.then_inc(w_hi, 1)

        def split_lo(dve, pair, slot, halves=False, part=None):
            if isinstance(pair, int) and pair * 2 + slot >= UNITS:
                return
            dve.wait_ge(w_hi, pair * 2 + slot + 1)
            v = nc.vector.tensor_tensor(of_unit(wlo, slot, halves, part), of_unit(raw, slot, halves, part),
                                        fview(of_unit(whi, slot, halves, part)), ALU.subtract)
            if part != 0:
                v.then_inc(w_lo, 1)

        def unit_features(pe, pair, slot, nk, hi, lo, banks, k0=0, first=True, last=True,
                          rope_cols=False, ready=None, free=None, w0=0, part=False):
            pe.wait_ge(w_lo, pair * 2 + slot + 1)
            if free is not None:
                pe.wait_ge(*free)
            for k in range(nk):
                if ready is not None:
                    pe.wait_ge(ready[0], ready[1] + k0 + k + 1)
                for m in range(2):
                    if rope_cols:
                        pick = lambda w: w[:, slot].rearrange("p k n -> p (k n)")[:, (m * KT + w0 + k) * P:(m * KT + w0 + k + 1) * P]
                    else:
                        pick = lambda w: w[:, slot, w0 + k, m * P:(m + 1) * P]
                    o = bank[banks + m][:, :]
                    nc.tensor.matmul(o, pick(whi), hi[:, k0 + k, :], start=first and k == 0, stop=False)
                    nc.tensor.matmul(o, pick(whi), lo[:, k0 + k, :], start=False, stop=False)
                    mm = nc.tensor.matmul(o, pick(wlo), hi[:, k0 + k, :], start=False,
                                          stop=last and k == nk - 1)
            if not part:
                mm.then_inc(unit_done, 1)

        def unit_tokens(pe, pair, slot, banks, ready=None, free=None, ks=range(KT)):
            pe.wait_ge(w_lo, pair * 2 + slot + 1)
            if free is not None:
                pe.wait_ge(*free)
            for k in ks:
                if ready is not None:
                    pe.wait_ge(ready[0], ready[1] + k + 1)
                for t in range(TT):
                    o = bank[banks + t // 2][:, (t % 2) * UC:(t % 2 + 1) * UC]
                    a_hi, a_lo = (a[:, k, t * P:(t + 1) * P] for a in (act_hi, act_lo))
                    nc.tensor.matmul(o, a_hi, whi[:, slot, k, :], start=k == 0 and t % 2 == 0,
                                     stop=False, skip_group_check=True)
                    nc.tensor.matmul(o, a_lo, whi[:, slot, k, :], start=False, stop=False,
                                     skip_group_check=True)
                    mm = nc.tensor.matmul(o, a_hi, wlo[:, slot, k, :], start=False,
                                          stop=k == KT - 1, skip_group_check=True)
            if ks[-1] == KT - 1:
                mm.then_inc(unit_done, 1)

        def gain(row, c):
            return cols[:, C_GAIN + row * KT + c:C_GAIN + row * KT + c + 1]

        def tile_act(act, b, c):
            act.wait_ge(x_new, KT * b + c + 1)
            nc.scalar.activation(act_hi[:, c, :], xres[:, c, :], ACT.Copy, scale=gain(2 * b, c)).then_inc(x_hi, 1)
            nc.scalar.activation(sqs[:, c, :], xres[:, c, :], ACT.Square).then_inc(x_sq, 1)

        def tile_lo(dve, b, c):
            dve.wait_ge(x_hi, KT * b + c + 1)
            nc.vector.scalar_tensor_tensor(out=act_lo[:, c, :], in0=xres[:, c, :], scalar=gain(2 * b, c),
                                           in1=fview(act_hi[:, c, :]), op0=ALU.mult,
                                           op1=ALU.subtract).then_inc(x_lo, 1)

        def squares_sum(eng, engine, b, first, done):
            for c in range(first + 1, first + 4):
                eng.wait_ge(x_sq, KT * b + c + 1)
                if c > first + 1:
                    eng.wait_ge(done, (4 if first == 0 else 3) * b + c - first - 1)
                engine.tensor_tensor(sqs[:, first, :], sqs[:, first, :], sqs[:, c, :], ALU.add).then_inc(done, 1)

        def squares_join(eng, engine, b):
            eng.wait_ge(x_sumA, 4 * b + 3)
            eng.wait_ge(x_sumB, 3 * (b + 1))
            engine.tensor_tensor(sqs[:, 0, :], sqs[:, 0, :], sqs[:, 4, :], ALU.add).then_inc(x_sumA, 1)

        def stat_pe(pe, b):
            pe.wait_ge(x_sumA, 4 * (b + 1))
            nc.tensor.matmul(bank[4][:, :], ones[:, :], sqs[:, 0, :], start=True, stop=True)
            for t in range(TT):
                mm = nc.tensor.matmul(bank[5][:, t:t + 1], sqs[:, 0, t * P:(t + 1) * P], ones[:, 0:1],
                                      start=True, stop=True)
            mm.then_inc(stat_mm, 1)

        def stat_act(act, b):
            act.wait_ge(stat_mm, b + 1)
            nc.scalar.activation(ln_tmp[:, :], bank[4][:, :], ACT.Ln, scale=1.0 / D, bias=eps_col[:, :])
            nc.scalar.activation(lnT_tmp[:, :], bank[5][:, 0:TT], ACT.Ln, scale=1.0 / D,
                                 bias=eps_col[:, :]).then_inc(stat_ln, 1)
            act.wait_ge(stat_ln, b + 1)
            nc.scalar.activation(rB[:, :], ln_tmp[:, :], ACT.Exp, scale=-0.5)
            nc.scalar.activation(rT[:, :], lnT_tmp[:, :], ACT.Exp, scale=-0.5).then_inc(r_ready, 1)

        def mixer_evac_act(act, b, mix, unit, tile, banks):
            act.wait_ge(unit_done, unit + 1)
            for m in range(2):
                if not (isinstance(tile, int) and tile == 0):
                    act.wait_ge(m_acc, tile + (7 * (b - 1) + m))
                nc.scalar.activation(sq_ring[:, m, :], bank[banks + m][:, :], ACT.Square).then_inc(m_evac, 1)
            for m in range(2):
                nc.scalar.activation(mix[:, bass.ds(tile + m, 1), :].rearrange("p a t -> p (a t)"),
                                     bank[banks + m][:, :], ACT.Copy).then_inc(m_copy, 1)

        def mixer_zero_dve(dve, b):
            if b > 1:
                dve.wait_ge(m_mm, b - 1)
            nc.vector.memset(msq[:, :], 0.0).then_inc(m_acc, 1)

        def mixer_sum_dve(dve, b, tile):
            for m in range(2):
                dve.wait_ge(m_evac, tile + (KT * (b - 1) + m + 1))
                dve.wait_ge(m_acc, tile + (7 * (b - 1) + m + 1))
                nc.vector.tensor_tensor(msq[:, :], msq[:, :], sq_ring[:, m, :], ALU.add).then_inc(m_acc, 1)

        def sum_bank(b):
            return bank[6 if b == 1 else 4][:, :]

        def post_pe(pe, b):
            pe.wait_ge(m_acc, 7 * b)
            nc.tensor.matmul(sum_bank(b), ones[:, :], msq[:, :], start=True, stop=False)
            for m in range(2):
                pe.wait_ge(m_evac, KT * b - 1 + m)
                last = nc.tensor.matmul(sum_bank(b), ones[:, :], sq_ring[:, m, :], start=False, stop=m == 1)
            last.then_inc(m_mm, 1)

        NEXT = {1: FFN_IN[0], 2: REC_IN, 3: FFN_IN[1]}

        def post_act(act, b):
            if b < 4:
                split_hi(act, NEXT[b] // 2, 1)
            act.wait_ge(m_mm, b)
            nc.scalar.activation(ln_tmp[:, :], sum_bank(b), ACT.Ln, scale=1.0 / D,
                                 bias=eps_col[:, :]).then_inc(m_ln, 1)
            act.wait_ge(m_ln, b)
            nc.scalar.activation(rM[:, :], ln_tmp[:, :], ACT.Exp, scale=-0.5).then_inc(rM_ready, 1)
            if b < 4:
                for c in range(KT):
                    tile_act(act, b, c)

        def post_add(eng, engine, b, mix, c, done):
            eng.wait_ge(m_scaled, KT * (b - 1) + c + 1)
            engine.tensor_tensor(xres[:, c, :], xres[:, c, :], mix[:, c, :], ALU.add).then_inc(done, 1)

        def post_dve(dve, b, mix):
            if b < 4:
                split_lo(dve, NEXT[b] // 2, 1, part=0)
            dve.wait_ge(rM_ready, b)
            dve.wait_ge(m_copy, KT * b)
            for c in range(KT + 2):
                if c < KT:
                    nc.vector.scalar_tensor_tensor(out=mix[:, c, :], in0=mix[:, c, :], scalar=gain(2 * b - 1, c),
                                                   in1=rM[:, :], op0=ALU.mult, op1=ALU.mult).then_inc(m_scaled, 1)
                    if c < 2 and b < 4 or b == 4 and c % 2 == 0:
                        post_add(dve, nc.vector, b, mix, c, x_new)
                if c >= 2 and b < 4:
                    tile_lo(dve, b, c - 2)
            if b < 4:
                split_lo(dve, NEXT[b] // 2, 1, part=1)
                squares_sum(dve, nc.vector, b, 0, x_sumA)
                squares_join(dve, nc.vector, b)

        def post_pool(pool, b, mix):
            for c in range(1, KT, 2) if b == 4 else range(2, KT):
                post_add(pool, nc.gpsimd, b, mix, c, x_odd if b == 4 else x_new)
            if b < 4:
                squares_sum(pool, nc.gpsimd, b, 4, x_sumB)

        block = ctx.enter_context(nc.Block())

        @block.sync
        def _(sp):
            for t in range(TT):
                sp.dma_start(x_in[:, t, :], x[0, t * P:(t + 1) * P, :]).then_inc(x_in_sem[t], 16)
            w = att_w_in[0]
            def stage(h, slot, into):
                r, q = h % 4, h % 2
                for half in range(2):
                    d = HD * q + 32 * half
                    sp.dma_start(qk_st[d:d + 32, slot, :, :],
                                 rope[32 * r:32 * r + 32, h // 4, :, half, :]).then_inc(into, 16)

            def att_load(u):
                if u < 12:
                    col = (0, 512, 256, 768, 1024, 1280, 1536, 2048, 2560, 1792, 2304, 2816)[u]
                    load(sp, u // 2, u % 2, weight_rows(w, 0, KT, col))
                else:
                    load(sp, u // 2, u % 2, weight_rows(att_w_out[0], 0, KT, (u - ATT_OUT) * UC))

            def stage(h, slot, into):
                row, q = h % 4, h % 2
                for half in range(2):
                    d = HD * q + 32 * half
                    sp.dma_start(qk_st[d:d + 32, slot, :, :],
                                 rope[32 * row:32 * row + 32, h // 4, :, half, :]).then_inc(into, 16)

            def stage_a(h):
                if h == 4:
                    sp.wait_ge(rope_out, 8)
                sp.wait_ge(sc_done, 4 * (h - 1))
                stage(h, 0, qk_in[h % 2])

            def stage_b(d):
                if d == 0:
                    sp.wait_ge(rope_out, 12)
                elif d == 1:
                    sp.wait_ge(sc_done, 32)
                elif d == 2:
                    sp.wait_ge(rope_out, 16)
                if d >= 2:
                    sp.wait_ge(sc_done, 32 + 8 * (d - 1))
                for q in range(2):
                    stage(8 + 2 * d + q, (d + 1) % 2, qd_in[(d + 1) % 2])

            for u in range(6):
                if u < 2:
                    sp.wait_ge(x_in_sem[2 * u + 1], 16)
                att_load(u)
            sp.wait_ge(rope_out, 4)
            stage(0, 0, qk_in[0])
            stage(1, 0, qk_in[1])
            for u in (6, 7, 8):
                att_load(u)
            stage_a(2)
            att_load(9)
            stage_a(3)
            stage_a(4)
            att_load(10)
            stage_a(5)
            stage_a(6)
            att_load(11)
            stage_a(7)
            stage_b(0)
            att_load(12)
            stage_b(1)
            att_load(13)
            stage_b(2)
            stage_b(3)
            att_load(14)
            att_load(15)
            for layer in range(2):
                w1, w2 = ffn_w_in[layer], ffn_w_out[layer]
                with sp.Fori(0, FFN // UC) as i:
                    load(sp, i + FFN_IN[layer] // 2, 0, weight_rows(w1, 0, KT, i * UC))
                    load(sp, i + FFN_IN[layer] // 2, 1, weight_rows(w1, 0, KT, i * UC + FFN))
                with sp.Fori(0, 2) as i:
                    for v in range(6):
                        m, kc = divmod(v, 3)
                        load(sp, i * 3 + (FFN_OUT[layer] // 2 + v // 2), v % 2,
                             weight_rows(w2, 8 * kc, min(8, FT - 8 * kc), i * (2 * UC) + m * UC))
                if layer == 0:
                    w = rec_w_in[0]
                    with sp.Fori(0, 2) as i:
                        for s in range(2):
                            load(sp, i + REC_IN // 2, s, weight_rows(w, 0, KT, i * (2 * UC) + (2 * D + s * UC)))
                    sp.wait_ge(m_mm, 2)
                    sp.dma_start(qb_sb[:, :, :].rearrange("p a t -> p (a t)")[:, 0:NL * P], level_masks).then_inc(rmask_in, 16)
                    with sp.Fori(0, 4) as i:
                        for s in range(2):
                            load(sp, i + (REC_IN // 2 + 2), s, weight_rows(w, 0, KT, i * UC + s * D))
                    with sp.Fori(0, 2) as i:
                        for s in range(2):
                            load(sp, i + (REC_IN // 2 + 6), s, weight_rows(w, 0, KT, i * (2 * UC) + (3 * D + s * UC)))
                    with sp.Fori(0, 2) as i:
                        for s in range(2):
                            load(sp, i + REC_OUT // 2, s, weight_rows(rec_w_out[0], 0, KT, i * (2 * UC) + s * UC))
            for half in range(2):
                sp.wait_ge(y_copied, 4 * half + 4)
                cs = slice(half * T, half * T + T)
                sp.dma_start(out[0].rearrange("(a p) d -> p a d", p=P)[:, :, cs], y_out[:, :, cs]).then_inc(y_out_sem, 16)
            sp.wait_ge(y_out_sem, 32)

        H_STEPS_T = ["diag0", "diag1"] + [f"lev{l}_{a}" for l in range(4) for a in range(2)] + ["keT0", "keT1"] \
            + [f"lev{l}_{a}" for l in (4, 5) for a in range(2)] + ["u0", "u1", "lev6_0", "lev6_1", "o0", "o1"]
        H_STEPS_S = ["diag0", "diag1"] + [f"lev{l}_{a}" for l in range(NL) for a in range(2)]
        EV = ["forget", "key", "scan", "dke", "qgate", "d0", "d1", "mq0", "d2", "mq1", "d3",
              "mq2", "mq3", "d4", "d5", "mq4", "d6", "mq5", "mq6"]
        EA = ["fe", "fl", "fs", "qe", "ql", "g", "qs", "eb", "ebl", "eke"] \
            + [f"{x}{l}" for l in range(NL) for x in ("et", "es")]
        ev, ea = Steps(hg_v, EV), Steps(hg_a, EA)
        ep = Steps(hg_p, ["mk0", "mk1", "mk2", "mk3", "ke", "mk4", "mk5", "mk6", "qb"])
        ht, hs = Steps(hg_t, H_STEPS_T), Steps(hg_s, H_STEPS_S)
        hk = Steps(hg_k, ["keT0", "keT1", "ocopy0", "osq0", "ocopy1", "osq1"])
        ho = Steps(hg_o, [f"s{c}_{a}" for a in range(2) for c in range(1, 4)] + ["ss0", "ss1"])

        qf = REC_IN // 2 + 2
        bw = Steps(bw_done, ["rinv", "ratio", "w"])
        bn = Steps(bn_v, ["s2", "ss", "ss_eps", "o"])
        bna = Steps(bn_a, ["sq", "ln", "r"])
        FV = ["g0", "g1", "u0", "h0", "u1", "h1", "lo0", "lo1"]
        FA = ["s0", "s1", "hi0", "hi1"]
        fvs = [Steps(v, FV) for v in ffn_v]
        fas = [Steps(v, FA) for v in ffn_a]

        A_ITEMS, ITEMS = 32, 48

        def scores_of_step(m):
            if m + 3 < A_ITEMS:
                return [m + 3]
            b = m + 3 - A_ITEMS
            return [A_ITEMS + 2 * b, A_ITEMS + 2 * b + 1] if 0 <= b < 16 else []

        def score(n):
            if n < A_ITEMS:
                return n // 4, n // 4 % 2, n % 4, 2 + n // 4 % 2
            d, q = divmod(n - A_ITEMS, 8)
            return d, q % 2, q // 2, 2 * (d % 2) + q % 2

        UNIT_K = ((0, 1), (2, 3), (4,), (5, 6), (7,), ())

        def unit_of_step(m):
            return (6 + m // 6, UNIT_K[m % 6]) if m < 30 else (11, (m - 30,)) if m < 38 else (None, ())

        def evac_of_step(m):
            return 6 + m // 6 if m in (5, 11, 17, 23, 29) else 11 if m == 38 else None

        ROPE_UNITS = {0: (0, 0), 1: (0, 1), 2: (1, 0), 3: (1, 1), 6: (2, 0), 7: (2, 1), 9: (3, 0), 10: (3, 1)}
        ROPE_AT = {u: n for n, u in enumerate(ROPE_UNITS)}
        V_UNITS = (4, 5, 8, 11)
        HI_AT = {0: 7, 5: 8, 11: 9, 17: 10, 23: 11, 33: 12, 40: 13}

        def split_of_step(m, lag):
            for half in range(2):
                if m - lag - half in HI_AT:
                    return HI_AT[m - lag - half], half
            return None

        OUT_AT = {39: 0, 40: 1, 41: 2, 42: 3, 43: 4, 45: 5}
        OUT_BANK = (6, 7, 6, 7, 3, 3, 3, 3)

        def copied(eng, m):
            if m >= A_ITEMS:
                eng.wait_ge(pT_act, 24 + m - A_ITEMS + 1)
            elif m % 4 == 3:
                eng.wait_ge(pT_dve, m // 4 + 1)
            else:
                eng.wait_ge(pT_act, 3 * (m // 4) + m % 4 + 1)

        X_BANK = (4, 5, 6, 3)

        @block.tensor
        def _(pe):
            mm = nc.tensor.matmul
            tr = nc.tensor.transpose
            pe.wait_ge(ident_in_sem, 16)
            pe.wait_ge(small_in, 16 * 5)
            tr(bank[7][:, 0:C_ALL], colsrc[0:C_ALL, :], ident[0:C_ALL, 0:C_ALL]).then_inc(colsT, 1)
            def x_transposes(c):
                if c >= 4:
                    pe.wait_ge(x_new, c - 3)
                for t in range(TT):
                    if c == 0:
                        pe.wait_ge(x_in_sem[t], 16)
                    last = tr(bank[X_BANK[c % 4]][:, t * P:(t + 1) * P], x_in[:, t, c * P:(c + 1) * P], ident[:, :])
                last.then_inc(xT_done, 1)
            for c in range(4):
                x_transposes(c)
            for k in range(KT):
                if k + 4 < KT:
                    x_transposes(k + 4)
                unit_features(pe, 0, 0, 1, act_hi, act_lo, 0, k0=k, w0=k, first=k == 0, last=k == 7,
                              part=k < 7, rope_cols=True, ready=(x_lo, 0))
            stat_pe(pe, 0)
            pe.wait_ge(lam_v, 3)
            mm(bank[6][:, 0:1], ones[0:1, :], lam_s[0:1, 4:5], start=True, stop=True).then_inc(lam_t, 1)

            for u in range(1, 4):
                unit_features(pe, u // 2, u % 2, KT, act_hi, act_lo, 2 * (u % 2), rope_cols=True,
                              free=None if u < 2 else (qk_evac, u - 1))
            def scores(n):
                head, sub, i, _ = score(n)
                if n < A_ITEMS:
                    slot = 0
                    if i == 0:
                        pe.wait_ge(qk_in[sub], 32 * (head // 2 + 1))
                else:
                    slot = (head + 1) % 2
                    if i == 0 and sub == 0:
                        pe.wait_ge(qd_in[slot], 64 * (head // 2 + 1))
                if n >= 3:
                    pe.wait_ge(neg_done, n - 2)
                h = slice(HD * sub, HD * sub + HD)
                mm(bank[n % 3][:, 0:(i + 1) * P], qk_st[h, slot, 0, i * P:(i + 1) * P],
                   qk_st[h, slot, 1, 0:(i + 1) * P], start=True, stop=True).then_inc(sc_done, 1)

            def transposes(m):
                if m < A_ITEMS:
                    pe.wait_ge(p_done, m + 1)
                    slot = m % 8
                else:
                    bw.wait(pe, "w", m - A_ITEMS)
                    slot = 2 * (m % 4)
                if m:
                    copied(pe, m - 1)
                if m - 1 in OUT_AT and OUT_AT[m - 1] >= 4:
                    pe.wait_ge(oa_lo, OUT_AT[m - 1] + 1)
                for k in range(m % 4 + 1):
                    last = tr(bank[3][:, k * P:(k + 1) * P], prob[:, slot, k * P:(k + 1) * P], ident[:, :])
                last.then_inc(pT_done, 1)

            def values(m):
                copied(pe, m)
                h, i = divmod(m, 4)
                if m < A_ITEMS:
                    width, col = HD, h * HD
                    if i == 0 and h >= 2:
                        pe.wait_ge(o_done, h - 1)
                else:
                    d = h - 8
                    width, col = P, 512 + d * P
                    if i == 0 and d < 2:
                        pe.wait_ge(o_done, 7 + d)
                    elif i == 0:
                        bn.wait(pe, "o", d - 2)
                    if m == A_ITEMS + 8:
                        pe.wait_ge(v_evac, 4)
                for k in range(i + 1):
                    last = mm(bank[4 + h % 2][:, i * width:(i + 1) * width], probT[:, m % 2, k * P:(k + 1) * P],
                              vtok[:, k, col:col + width], start=k == 0, stop=k == i)
                last.then_inc(pv_done, 1)

            def output_tile(c):
                if c < 4:
                    src = oA[c]
                    if c == 0:
                        pe.wait_ge(v_evac, 4)
                    pe.wait_ge(o_done, 2 * c + 2)
                else:
                    src = oB[c % 2]
                    bn.wait(pe, "o", c - 4)
                    copied(pe, {4: 43, 5: 45}.get(c, ITEMS - 1))
                if c >= 2:
                    pe.wait_ge(oa_lo, c - 1 if c < 4 else c)
                for i in range(TT):
                    last = tr(bank[OUT_BANK[c]][:, i * P:(i + 1) * P], src[:, i, :], ident[:, :])
                last.then_inc(oT_done, 1)

            def output_part(u, k):
                unit_features(pe, ATT_OUT // 2, u, 1, act_hi, act_lo, (6, 0)[u], ready=(oa_lo, 0), k0=k, w0=k,
                              first=k == 0, last=k == 7, part=k < 7, free=((oa_lo, 4), (neg_done, 64))[u] if k == 0 else None)

            for u in (4, 5):
                unit_tokens(pe, u // 2, u % 2, 4 + 2 * (u % 2), free=((r_ready, 1), (lam_v, 4))[u - 4])
                if u == 4:
                    pe.wait_ge(qk_evac, 4)
                    for n in range(3):
                        scores(n)
            pe.wait_ge(v_evac, 1)

            for m in range(ITEMS):
                unit, ks = unit_of_step(m)
                half = 0
                def projections(ks):
                    for k in ks:
                        free = None
                        if k == 0:
                            before = unit - 1
                            free = (qk_evac, ROPE_AT[before] + 1) if before in ROPE_AT else (v_evac, V_UNITS.index(before) + 1)
                        if unit in ROPE_AT:
                            unit_features(pe, unit // 2, unit % 2, 1, act_hi, act_lo, 6, k0=k, w0=k, first=k == 0,
                                          last=k == KT - 1, rope_cols=True, free=free, part=k < KT - 1)
                        else:
                            unit_tokens(pe, unit // 2, unit % 2, 6, free=free, ks=(k,))
                transposes(m)
                for n in scores_of_step(m):
                    scores(n)
                projections(ks[0:1])
                if m:
                    if m == 1:
                        pe.wait_ge(v_evac, 2)
                    values(m - 1)
                projections(ks[1:])
                if m in OUT_AT:
                    output_tile(OUT_AT[m])
                if m >= 43:
                    output_part(0, m - 43)
            values(ITEMS - 1)
            output_part(0, 5)
            output_tile(6)
            for k in range(3):
                output_part(1, k)
            output_tile(7)
            output_part(0, 6)
            output_part(0, 7)
            for k in range(3, KT):
                output_part(1, k)

            def out_projection(base, b):
                for u in range(2 if base == ATT_OUT else 1, 4):
                    unit_features(pe, base // 2 + u // 2, u % 2, KT, act_hi, act_lo,
                                  2 * (u % 2) + (2 if base == ATT_OUT else 0),
                                  free=None if base == ATT_OUT else (g_silu, 16) if u == 1 else (m_copy, KT * (b - 1) + 2 * (u - 1)))
                post_pe(pe, b)

            def ffn(layer):
                b = 1 + 2 * layer
                fv = fvs[layer]

                def pair(i):
                    peeled = isinstance(i, int)
                    for s in range(2):
                        unit_features(pe, i + FFN_IN[layer] // 2, s, KT, act_hi, act_lo, 2 * s,
                                      ready=(x_lo, KT * b) if peeled and s == 0 else None,
                                      free=None if peeled else (fv.sem, i * len(fv.names) - (len(fv.names) - fv.at["g1" if s == 0 else "u1"])))
                        if peeled and s == 0:
                            stat_pe(pe, b)
                pair(0)
                with pe.Fori(1, FFN // UC) as i:
                    pair(i)
                with pe.Fori(0, 2) as i:
                    for v in range(6):
                        m, kc = divmod(v, 3)
                        nk = min(8, FT - 8 * kc)
                        if kc == 0:
                            fv.wait(pe, ("g1", "u1")[m], FFN // UC - 1)
                            if m == 0:
                                pe.wait_ge(m_copy, i * 4 + KT * b - 2)
                            else:
                                pe.wait_ge(m_copy, i * 4 + KT * b)
                        fv.wait(pe, "lo1", (8 * kc + nk) // 2 - 1)
                        unit_features(pe, i * 3 + (FFN_OUT[layer] // 2 + v // 2), v % 2, nk, hid_hi, hid_lo,
                                      2 * m, k0=8 * kc, first=kc == 0, last=kc == 2)
                post_pe(pe, b + 1)

            out_projection(ATT_OUT, 1)
            ffn(0)

            for u in range(4):
                unit_tokens(pe, REC_IN // 2 + u // 2, u % 2, 2 * (u % 2),
                            ready=(x_lo, 2 * KT) if u == 0 else None,
                            free=(rv_evac, u - 1) if u >= 2 else (m_copy, 2 * KT))
                if u == 0:
                    stat_pe(pe, 2)

            def qf_pair(j):
                for s in range(2):
                    unit_features(pe, j + (REC_IN // 2 + 2), s, KT, act_hi, act_lo, 2 * s,
                                  free=(rv_evac, 3 + s) if isinstance(j, int) else (s_qf, j * 2))

            def heads(j):
                ev.wait(pe, "qgate", j)
                for a in range(2):
                    for c in range(TT):
                        cs = slice(c * P, (c + 1) * P)
                        last = mm(bank[6 + a][:, cs], k_sb[:, a, cs], q_sb[:, a, cs], start=True, stop=True)
                    ht.done(last, f"diag{a}")
                for l in range(NL):
                    if l == 4:
                        ep.wait(pe, "ke", j)
                        for a in range(2):
                            for c in range(3):
                                last = tr(bank[4 + a][:, c * P:(c + 1) * P], ke_sb[:, a, c * P:(c + 1) * P], ident[:, :])
                            ht.done(last, f"keT{a}")
                    if l == NL - 1:
                        for a in range(2):
                            hk.wait(pe, f"keT{a}", j)
                            for c in range(3):
                                last = mm(bank[4 + a][:, c * P:(c + 1) * P], keT[:, a, c, :],
                                          rv[:, c, bass.ds(j * UC + a * P, P)], start=True, stop=True)
                            ht.done(last, f"u{a}")
                    for a in range(2):
                        if a == 0:
                            ev.wait(pe, f"mq{l}", j)
                            ep.wait(pe, f"mk{l}", j)
                        hs.wait(pe, f"diag{a}" if l == 0 else f"lev{l - 1}_{a}", j)
                        for c in range(TT):
                            m = m_sb[:, l % 4, a, c * P:(c + 1) * P]
                            last = mm(bank[6 + a][:, c * P:(c + 1) * P], m, m, start=True, stop=True)
                        ht.done(last, f"lev{l}_{a}")
                for a in range(2):
                    hs.wait(pe, f"lev{NL - 1}_{a}", j)
                    ep.wait(pe, "qb", j)
                    ho.wait(pe, f"s3_{a}", j)
                    for c in range(TT):
                        cs = slice(c * P, (c + 1) * P)
                        last = mm(bank[6 + a][:, cs], att[:, a, cs], rv[:, c, bass.ds(j * UC + a * P, P)],
                                  start=True, stop=c == 0)
                        if c:
                            last = mm(bank[6 + a][:, cs], qb_sb[:, a, cs], state[:, a, c - 1, :],
                                      start=False, stop=True)
                    ht.done(last, f"o{a}")
                hk.wait(pe, "ocopy1", j)

            def gates(u, free):
                unit_tokens(pe, REC_IN // 2 + 6 + u // 2, u % 2, 2 * (u % 2), free=free)

            def gated_transposes(u):
                pe.wait_ge(g_mul, 8 * (u + 1))
                for h in range(2):
                    if 2 * u + h >= 4:
                        pe.wait_ge(gT_lo, 2 * u + h - 3)
                    for t in range(TT):
                        last = tr(bank[4 + (2 * u + h) % 4][:, t * P:(t + 1) * P], og[:, u % 2, t, h * P:(h + 1) * P], ident[:, :])
                    last.then_inc(gT_done, 1)

            qf_pair(0)
            with pe.Fori(1, 4) as j:
                qf_pair(j)
                heads(j - 1)
            gates(0, (s_qf, 8))
            gates(1, None)
            heads(3)
            gates(2, (g_evac, 1))
            gated_transposes(0)
            gated_transposes(1)
            gates(3, (g_evac, 2))
            unit_features(pe, REC_OUT // 2, 0, 4, act_hi, act_lo, 0, ready=(gT_lo, 0), last=False, part=True,
                          free=(g_silu, 12))
            gated_transposes(2)
            gated_transposes(3)
            unit_features(pe, REC_OUT // 2, 0, 4, act_hi, act_lo, 0, ready=(gT_lo, 0), k0=4, w0=4, first=False)
            out_projection(REC_OUT, 3)
            ffn(1)
            for c in range(KT):
                if c % 2:
                    pe.wait_ge(x_odd, c // 2 + 1)
                else:
                    pe.wait_ge(x_new, 4 * KT + c // 2 + 1)
                b = (0, 1, 2, 3, 5, 6, 7, 4)[c]
                for t in range(TT):
                    last = tr(bank[b][:, t * P:(t + 1) * P], xres[:, c, t * P:(t + 1) * P], ident[:, :])
                last.then_inc(yT_done, 1)

        @block.gpsimd
        def _(pool):
            g = nc.gpsimd
            g.memset(ones[:, :], 1.0)
            g.memset(eps_col[:, :], EPS)
            g.memset(one_col[:, :], 1.0).then_inc(setup, 1)
            squares_sum(pool, g, 0, 0, x_sumA)
            squares_sum(pool, g, 0, 4, x_sumB)
            squares_join(pool, g, 0)

            for n, (p, s) in enumerate(ROPE_UNITS.values()):
                pool.wait_ge(rope_mul, 2 * (n + 1))
                g.tensor_tensor(rope[:, p, s, 0, :], rtmp[:, 0, :], rtmp[:, 3, :], ALU.subtract).then_inc(rope_out, 1)
                g.tensor_tensor(rope[:, p, s, 1, :], rtmp[:, 1, :], rtmp[:, 2, :], ALU.add).then_inc(rope_out, 1)
            post_pool(pool, 1, mix_att)
            post_pool(pool, 2, mix_ffn)
            pool.wait_ge(r_ready, 3)
            g.memset(rzero[:, :], 1.0).then_inc(setup, 1)
            pool.wait_ge(setup, 2)
            g.memset(rzero[:, :].rearrange("p (c t) -> p c t", t=CH)[:, :, 0:1], 0.0).then_inc(setup, 1)

            def level_keys(j):
                def scaled(x, e, src, decay):
                    ea.wait(pool, decay, j)
                    v = lambda ap: ap.rearrange("p a t -> p (a t)")
                    ep.done(g.tensor_tensor(v(e[:, :, :]), v(e[:, :, :]), v(src[:, :, :]), ALU.mult), x)

                for l, L in enumerate(LEVELS):
                    if l == 4:
                        scaled("ke", ke_sb, k_sb, "eke")
                    ea.wait(pool, f"es{l}", j)
                    if l >= 4:
                        ht.wait(pool, f"lev{l - 4}_1", j)
                    elif not isinstance(j, int):
                        ht.wait(pool, f"lev{l + 4 if l < 3 else 3}_1", j - 1)
                    v = lambda ap: ap.rearrange("p a t -> p (a t)").rearrange("p (b h t) -> p b h t", h=2, t=L)[:, :, 0, :]
                    ep.done(g.tensor_tensor(v(m_sb[:, l % 4]), v(e_sb[:, l % 2]), v(k_sb[:, :, :]), ALU.mult), f"mk{l}")
                scaled("qb", qb_sb, q_sb, "eb")
            level_keys(0)
            with pool.Fori(1, 4) as j:
                level_keys(j)
            post_pool(pool, 3, mix_rec)
            post_pool(pool, 4, mix_ffn)

        @block.scalar
        def _(act):
            A = nc.scalar.activation
            act.preload_act_table_set(EXP_LN)
            act.dma_start(ident[:, :], ident_in).then_inc(ident_in_sem, 16)
            act.dma_start(colsrc[C_GAIN:C_GAIN + 64, :], norm_gains.rearrange("l n (k p) -> (l n k) p", p=P)).then_inc(small_in, 16)
            act.dma_start(colsrc[C_SUB:C_SUB + 1, :], att_subln).then_inc(small_in, 16)
            act.dma_start(colsrc[C_GN:C_GN + 1, :], rec_gnorm).then_inc(small_in, 16)
            act.dma_start(colsrc[C_LB:C_LB + 8, :], rec_lower_bounds.rearrange("a (h p) -> (a h) p", p=P)).then_inc(small_in, 16)
            act.dma_start(lam_in[0:1, :, :], att_lambda).then_inc(small_in, 16)
            act.wait_ge(colsT, 1)
            A(cols[:, :], bank[7][:, 0:C_ALL], ACT.Copy).then_inc(colsR, 1)
            act.wait_ge(colsR, 1)
            for c in range(KT):
                tile_act(act, 0, c)
                if c == 1:
                    split_hi(act, 0, 0, True)
            act.dma_start(cosr[:, :], cos_t).then_inc(rope_in, 16)
            act.dma_start(sinr[:, :], sin_t).then_inc(rope_in, 16)
            act.dma_start(mskA[:, :], mask_a).then_inc(masks_in, 16)
            act.dma_start(mskB[:, :], mask_b).then_inc(masks_in, 16)
            split_hi(act, 0, 1, True)
            act.wait_ge(lam_v, 2)
            A(lam_s[0:1, 2:4], lam_s[0:1, 0:2], ACT.Exp).then_inc(lam_a, 1)

            def evac_qk(u, banks):
                n = ROPE_AT[u]
                act.wait_ge(unit_done, u + 1)
                if n:
                    act.wait_ge(rope_out, 2 * n)
                for h in range(2):
                    last = A(rtmp[:, h, :], bank[banks + h][:, :], ACT.Copy)
                last.then_inc(qk_evac, 1)
            stat_act(act, 0)
            for u in range(4):
                split_hi(act, (u + 2) // 2, u % 2, u + 2 in ROPE_AT)
                evac_qk(u, 2 * (u % 2))

            def tokens_evac(u, unit, dst, base, count, stat, banks, tiles=range(TT)):
                act.wait_ge(r_ready, stat + 1)
                act.wait_ge(unit_done, unit + 1)
                for t in tiles:
                    last = A(dst[:, t, base:base + UC], bank[banks + 2 * (u % 2) + t // 2][:, (t % 2) * UC:(t % 2 + 1) * UC],
                             ACT.Copy, scale=rT[:, t:t + 1])
                last.then_inc(count, 1)
            def exponential(n):
                _, _, i, row = score(n)
                act.wait_ge(neg_done, n + 1)
                A(prob[:, n % 8, 0:(i + 1) * P], prob[:, n % 8, 0:(i + 1) * P], ACT.Exp, scale=-1.0,
                  bias=nmax[:, row, i:i + 1], accum_out=rsum[:, row, i:i + 1]).then_inc(p_done, 1)

            def copy_pT(m):
                N = (m % 4 + 1) * P
                act.wait_ge(pT_done, m + 1)
                if m >= 2:
                    act.wait_ge(pv_done, m - 1)
                A(probT[:, m % 2, 0:N], bank[3][:, 0:N], ACT.Copy).then_inc(pT_act, 1)

            def output_hi(c):
                act.wait_ge(oT_done, c + 1)
                A(act_hi[:, c, :], bank[OUT_BANK[c]][:, :], ACT.Copy,
                  scale=1.0 if c < 4 else lam_s[:, 6:7]).then_inc(oa_hi, 1)

            def norm_squares(d):
                act.wait_ge(pv_done, A_ITEMS + 4 * (d + 1))
                bna.done(A(osq[:, :], bank[4 + d % 2][:, :], ACT.Square), "sq")

            def norm_root(d):
                bn.wait(act, "ss_eps", d)
                bna.done(A(oss[:, 1, :], oss[:, 0, :], ACT.Ln, scale=1.0 / P), "ln")
                bna.wait(act, "ln", d)
                bna.done(A(oss[:, 2, :], oss[:, 1, :], ACT.Exp, scale=-0.5), "r")

            tokens_evac(0, 4, vtok, 0, v_evac, 0, 4)
            split_hi(act, 3, 0, True)
            for n in range(3):
                exponential(n)
            tokens_evac(1, 5, vtok, UC, v_evac, 0, 4)
            for m in range(ITEMS):
                if m >= A_ITEMS or m % 4 != 3:
                    copy_pT(m)
                for n in scores_of_step(m):
                    exponential(n)
                u = evac_of_step(m)
                if u in ROPE_AT:
                    evac_qk(u, 6)
                elif u is not None:
                    tokens_evac(1, u, vtok, V_UNITS.index(u) * UC, v_evac, 0, 4)
                if split_of_step(m, 0):
                    u, half = split_of_step(m, 0)
                    split_hi(act, u // 2, u % 2, u in ROPE_AT, half)
                d, phase_ = divmod(m - A_ITEMS - 4, 4)
                if d >= 0 and phase_ == 0:
                    norm_squares(d)
                elif d >= 0 and phase_ == 2:
                    norm_root(d)
                if m in OUT_AT:
                    output_hi(OUT_AT[m])
            output_hi(6)
            norm_squares(3)
            norm_root(3)
            output_hi(7)

            def out_projection(base, b, mix):
                for u in range(4):
                    if u == 2 or u == 0 and base != ATT_OUT:
                        split_hi(act, base // 2 + u // 2, 1)
                    banks = (6, 0, 2, 4)[u] if base == ATT_OUT else 2 * (u % 2)
                    mixer_evac_act(act, b, mix, base + u, 2 * u, banks)
                    if u % 2 == 0:
                        split_hi(act, base // 2 + u // 2 + 1, 0)
                post_act(act, b)

            def ffn(layer):
                b = 1 + 2 * layer
                fv, fa = fvs[layer], fas[layer]
                base = FFN_IN[layer] // 2

                def pair(i):
                    if isinstance(i, int):
                        stat_act(act, b)
                    else:
                        split_hi(act, i + base, 1)
                    for m in range(2):
                        fv.wait(act, f"g{m}", i)
                        fa.done(A(f_g[:, m, :], f_g[:, m, :], ACT.Silu), f"s{m}")
                    split_hi(act, i + (base + 1), 0)
                    for m in range(2):
                        fv.wait(act, f"h{m}", i)
                        fa.done(A(hid_hi[:, bass.ds(i * 2 + m, 1), :].rearrange("p a t -> p (a t)"),
                                  f_g[:, m, :], ACT.Copy), f"hi{m}")
                pair(0)
                with act.Fori(1, FFN // UC) as i:
                    pair(i)
                act.preload_act_table_set(EXP_LN)
                base = FFN_OUT[layer] // 2

                def six_units(i):
                    for v in range(6):
                        m, kc = divmod(v, 3)
                        if v % 2 == 0:
                            split_hi(act, i * 3 + (base + v // 2), 1)
                        if kc == 2:
                            mixer_evac_act(act, b + 1, mix_ffn, i * 6 + (FFN_OUT[layer] + v), i * 4 + 2 * m, 2 * m)
                        if v % 2 == 0:
                            split_hi(act, i * 3 + (base + v // 2 + 1), 0)
                if layer == 0:
                    with act.Fori(0, 2) as i:
                        six_units(i)
                else:
                    six_units(0)
                    six_units(1)
                post_act(act, b + 1)

            out_projection(ATT_OUT, 1, mix_att)
            ffn(0)

            for u in range(4):
                pair = REC_IN // 2 + u // 2
                if u == 2:
                    split_hi(act, pair, 1)
                if u == 0:
                    stat_act(act, 2)
                    act.wait_ge(lb_v, 1)
                    A(lb[:, 1, :], lb[:, 0, :], ACT.Exp).then_inc(lb_a, 1)
                tokens_evac(u, REC_IN + u, rv, u * UC, rv_evac, 2, 0)
                if u % 2 == 0:
                    split_hi(act, pair + 1, 0)

            flat = lambda ap: ap.rearrange("p a t -> p (a t)")
            blocks = lambda ap, L: flat(ap).rearrange("p (b h t) -> p b h t", h=2, t=L)

            def level_exps(j, ls):
                for l in ls:
                    ev.wait(act, f"d{l}", j)
                    for x, h, sgn in (("et", 1, 1.0), ("es", 0, -1.0)):
                        v = blocks(e_sb[:, l % 2], LEVELS[l])[:, :, h, :]
                        ea.done(A(v, v, ACT.Exp, scale=sgn), f"{x}{l}")

            def gates_and_decays(j):
                def exp_ln(x, src, e, count):
                    v = flat(e_sb[:, e])
                    act.wait_ge(s_qf, j * 2 + count)
                    ea.done(A(v, flat(src[:, :, :]), ACT.Exp, scale=-1.0), f"{x}e")
                    ea.wait(act, f"{x}e", j)
                    ea.done(A(v, v, ACT.Ln, bias=one_col[:, :]), f"{x}l")
                    ea.wait(act, f"{x}l", j)

                exp_ln("f", k_sb, 1, 1)
                ea.done(A(flat(e_sb[:, 1]), flat(e_sb[:, 1]), ACT.Exp, scale=-1.0), "fs")
                exp_ln("q", q_sb, 0, 2)
                ev.wait(act, "key", j)
                ea.done(A(flat(e_sb[:, 1]), flat(e_sb[:, 1]), ACT.Ln), "g")
                ea.done(A(flat(e_sb[:, 0]), flat(e_sb[:, 0]), ACT.Exp, scale=-1.0), "qs")
                ev.wait(act, "scan", j)
                ea.done(A(flat(qb_sb[:, :, :]), flat(b_sb[:, :, :]), ACT.Exp), "eb")
                ea.done(A(ebl[:, :, :], b_sb[:, :, :].rearrange("p a (c t) -> p a c t", t=CH)[:, :, :, CH - 1], ACT.Exp), "ebl")
                ev.wait(act, "dke", j)
                ea.done(A(flat(ke_sb[:, :, :]), flat(ke_sb[:, :, :]), ACT.Exp, scale=-1.0), "eke")
                level_exps(j, range(4))

            def heads(j, splits):
                level_exps(j, range(4, NL))
                for a in range(2):
                    ht.wait(act, f"keT{a}", j)
                    hk.done(A(keT[:, a, :, :].rearrange("p c t -> p (c t)"), bank[4 + a][:, 0:3 * P], ACT.Copy), f"keT{a}")
                for slot in range(2):
                    split_hi(act, splits, slot)
                if isinstance(j, int):
                    ev.wait(act, "mq6", j)
                    ep.wait(act, "mk6", j)
                    tokens_evac(0, REC_IN + 12, gate[:, 0], 0, g_evac, 2, 0)
                    tokens_evac(1, REC_IN + 13, gate[:, 1], 0, g_evac, 2, 0)
                for a in range(2):
                    ht.wait(act, f"o{a}", j)
                    v = bank[6 + a][:, :].rearrange("p (c t) -> p c t", c=TT)
                    hk.done(A(ro[:, :, bass.ds(j * UC + a * P, P)], v, ACT.Copy), f"ocopy{a}")
                    if a:
                        ho.wait(act, "ss0", j)
                    hk.wait(act, f"ocopy{a}", j)
                    if not isinstance(j, int):
                        A(lnT_tmp[:, a:a + 1], one_col[:, :], ACT.Copy)
                    hk.done(A(r_sq[:, :].rearrange("p (c t) -> p c t", c=TT), ro[:, :, bass.ds(j * UC + a * P, P)],
                              ACT.Square), f"osq{a}")

            split_hi(act, qf, 1)
            split_hi(act, qf + 1, 0)
            split_hi(act, qf + 1, 1)
            with act.Fori(1, 4) as j:
                gates_and_decays(j - 1)
                heads(j - 1, j + (qf + 1))
            gates_and_decays(3)
            heads(3, qf + 5)
            ho.wait(act, "ss1", 3)
            A(r_rs[:, 1, :, :], r_rs[:, 0, :, :], ACT.Ln, scale=1.0 / P, bias=eps_col[:, :]).then_inc(rrs_a, 1)
            act.wait_ge(rrs_a, 1)
            A(r_rs[:, 2, :, :], r_rs[:, 1, :, :], ACT.Exp, scale=-0.5).then_inc(rrs_a, 1)

            def gate_silu(u):
                if u < 2:
                    act.wait_ge(g_evac, u + 1)
                    for t in range(TT):
                        A(gate[:, u, t, :], gate[:, u, t, :], ACT.Silu).then_inc(g_silu, 1)
                    return
                act.wait_ge(unit_done, REC_IN + 12 + u + 1)
                act.wait_ge(g_mul, 8 * (u - 1))
                for t in range(TT):
                    A(gate[:, u % 2, t, :], bank[2 * (u % 2) + t // 2][:, (t % 2) * UC:(t % 2 + 1) * UC],
                      ACT.Silu, scale=rT[:, t:t + 1]).then_inc(g_silu, 1)
            gate_silu(0)
            gate_silu(1)
            gate_silu(2)
            split_hi(act, qf + 6, 0)
            for c in range(KT):
                if c == 2:
                    gate_silu(3)
                act.wait_ge(gT_done, c + 1)
                act.wait_ge(unit_done, REC_IN + 16)
                A(act_hi[:, c, :], bank[4 + c % 4][:, :], ACT.Copy, scale=cols[:, C_GN:C_GN + 1]).then_inc(gT_hi, 1)
            act.preload_act_table_set(EXP_LN)
            out_projection(REC_OUT, 3, mix_rec)
            ffn(1)
            for c in range(KT):
                act.wait_ge(yT_done, c + 1)
                b = (0, 1, 2, 3, 5, 6, 7, 4)[c]
                A(y_out[:, :, c * P:(c + 1) * P], bank[b][:, :].rearrange("p (a f) -> p a f", a=TT), ACT.Copy).then_inc(y_copied, 1)

        @block.vector
        def _(dve):
            V = nc.vector
            TTo, STT, TS = V.tensor_tensor, V.scalar_tensor_tensor, V.tensor_scalar
            turn = [0]

            def waited(dve):
                turn[0] += 1
                k = turn[0] % 8
                V.memset(pad[:, k:k + 1], 0.0)

            dve.wait_ge(small_in, 16 * 5)
            TTo(lam_in[0:1, 0, :], lam_in[0:1, 0, :], lam_in[0:1, 1, :], ALU.mult)
            TTo(lam_in[0:1, 2, :], lam_in[0:1, 2, :], lam_in[0:1, 3, :], ALU.mult).then_inc(lam_v, 1)
            dve.wait_ge(lam_v, 1)
            V.tensor_reduce(lam_s[0:1, 0:2], lam_in[0:1, :, :].rearrange("p (a b) d -> p a b d", b=2)[:, :, 0, :],
                            axis=AXX, op=ALU.add).then_inc(lam_v, 1)
            for c in range(KT + 1):
                if c < KT:
                    dve.wait_ge(xT_done, c + 1)
                    V.tensor_copy(xres[:, c, :], bank[X_BANK[c % 4]][:, :]).then_inc(x_new, 1)
                if c >= 1:
                    tile_lo(dve, 0, c - 1)
                if c == 2:
                    split_lo(dve, 0, 0, True)
            split_lo(dve, 0, 1, True)
            dve.wait_ge(lam_a, 1)
            STT(out=lam_s[0:1, 4:5], in0=lam_s[0:1, 2:3], scalar=LAMBDA_INIT, in1=lam_s[0:1, 3:4],
                op0=ALU.add, op1=ALU.subtract).then_inc(lam_v, 1)
            dve.wait_ge(lam_t, 1)
            TS(lam_s[:, 5:6], bank[6][:, 0:1], -1.0, None, ALU.mult)
            dve.wait_ge(colsR, 1)
            TS(lam_s[:, 6:7], cols[:, C_SUB:C_SUB + 1], 1.0 - LAMBDA_INIT, None, ALU.mult).then_inc(lam_v, 1)
            dve.wait_ge(r_ready, 1)
            dve.wait_ge(rope_in, 32)
            TTo(cosr[:, :], cosr[:, :], rB[:, :], ALU.mult)
            TTo(sinr[:, :], sinr[:, :], rB[:, :], ALU.mult).then_inc(rope_tab, 1)
            dve.wait_ge(rope_tab, 1)

            def rotate(u, step):
                n = ROPE_AT[u]
                tab = (sinr, cosr)[step][:, :].unsqueeze(1).to_broadcast([P, 2, T])
                if step == 0:
                    dve.wait_ge(qk_evac, n + 1)
                else:
                    dve.wait_ge(rope_mul, 2 * n + 1)
                dst = rtmp[:, 2:4, :] if step == 0 else rtmp[:, 0:2, :]
                TTo(dst, rtmp[:, 0:2, :], tab, ALU.mult).then_inc(rope_mul, 1)
            for u in range(4):
                split_lo(dve, (u + 2) // 2, u % 2, u + 2 in ROPE_AT)
                rotate(u, 0)
                rotate(u, 1)

            def negated(n):
                _, _, i, row = score(n)
                N, msk = (i + 1) * P, mskA if n < A_ITEMS else mskB
                dve.wait_ge(sc_done, n + 1)
                if n >= 8:
                    dve.wait_ge(pT_done, n - 7 if n < A_ITEMS + 8 else A_ITEMS + (n - A_ITEMS) // 2 - 3)
                waited(dve)
                V.tensor_tensor_reduce(out=prob[:, n % 8, 0:N], in0=bank[n % 3][:, 0:N], in1=msk[:, T - N:T],
                                       scale=-SCALE, scalar=3e38, op0=ALU.add, op1=ALU.min,
                                       accum_out=nmax[:, row, i:i + 1]).then_inc(neg_done, 1)

            def copy_pT(m):
                dve.wait_ge(pT_done, m + 1)
                dve.wait_ge(pv_done, m - 1)
                V.tensor_copy(probT[:, m % 2, :], bank[3][:, :]).then_inc(pT_dve, 1)

            def head_out(h):
                row = 2 + h % 2
                dve.wait_ge(p_done, 4 * (h + 1))
                V.reciprocal(rinv[:, row, :], rsum[:, row, :]).then_inc(rinv_done, 1)
                dve.wait_ge(rinv_done, h + 1)
                dve.wait_ge(pv_done, 4 * (h + 1))
                TTo(oA[h // 2][:, :, HD * (h % 2):HD * (h % 2 + 1)], by_block(bank[4 + h % 2][:, 0:TT * HD]),
                    rinv[:, row, :].unsqueeze(2).to_broadcast([P, TT, HD]), ALU.mult).then_inc(o_done, 1)

            def weights(b):
                d, i = divmod(b, 4)
                N, q = (i + 1) * P, 2 * (d % 2)
                s0, r1 = rsum[:, q, i:i + 1], rinv[:, q + 1, i:i + 1]
                p0, p1 = prob[:, 2 * (b % 4), 0:N], prob[:, 2 * (b % 4) + 1, 0:N]
                dve.wait_ge(p_done, A_ITEMS + 2 * b + 2)
                bw.done(V.reciprocal(r1, rsum[:, q + 1, i:i + 1]), "rinv")
                bw.wait(dve, "rinv", b)
                bw.done(STT(out=r1, in0=s0, scalar=lam_s[:, 5:6], in1=r1, op0=ALU.mult, op1=ALU.mult), "ratio")
                bw.wait(dve, "ratio", b)
                bw.done(STT(out=p0, in0=p1, scalar=r1, in1=p0, op0=ALU.mult, op1=ALU.add), "w")

            def norm_s2(d):
                s0 = rsum[:, 2 * (d % 2), :]
                if d:
                    bn.wait(dve, "o", d - 1)
                bn.done(TTo(oss[:, 2, :], s0, s0, ALU.mult), "s2")

            def norm_sum(d):
                bna.wait(dve, "sq", d)
                bn.done(V.tensor_reduce(oss[:, 0, :], by_block(osq[:, :]), axis=AXX, op=ALU.add), "ss")
                bn.wait(dve, "ss", d)
                bn.done(STT(out=oss[:, 0, :], in0=oss[:, 2, :], scalar=EPS * P, in1=oss[:, 0, :],
                            op0=ALU.mult, op1=ALU.add), "ss_eps")

            def norm_out(d):
                bna.wait(dve, "r", d)
                if d >= 2:
                    dve.wait_ge(oT_done, 3 + d)
                bn.done(TTo(oB[d % 2], by_block(bank[4 + d % 2][:, :]),
                            oss[:, 2, :].unsqueeze(2).to_broadcast([P, TT, P]), ALU.mult), "o")

            def output_lo(c):
                dve.wait_ge(oa_hi, c + 1)
                STT(out=act_lo[:, c, :], in0=bank[OUT_BANK[c]][:, :], scalar=1.0 if c < 4 else lam_s[:, 6:7],
                    in1=fview(act_hi[:, c, :]), op0=ALU.mult, op1=ALU.subtract).then_inc(oa_lo, 1)

            dve.wait_ge(lam_v, 4)
            dve.wait_ge(masks_in, 32)
            split_lo(dve, 3, 0, True)
            for n in range(3):
                negated(n)
            for m in range(ITEMS):
                if m < A_ITEMS and m % 4 == 3:
                    copy_pT(m)
                if A_ITEMS - 1 <= m < ITEMS - 1:
                    weights(m + 1 - A_ITEMS)
                if m - 1 in OUT_AT:
                    output_lo(OUT_AT[m - 1])
                for n in scores_of_step(m):
                    negated(n)
                for step in range(2):
                    if evac_of_step(m - step) in ROPE_AT:
                        rotate(evac_of_step(m - step), step)
                if m <= A_ITEMS and m % 4 == 0 and m:
                    head_out(m // 4 - 1)
                if split_of_step(m, 2):
                    u, half = split_of_step(m, 2)
                    split_lo(dve, u // 2, u % 2, u in ROPE_AT, half)
                d, phase_ = divmod(m - A_ITEMS - 4, 4)
                if d >= 0 and phase_ == 0:
                    norm_s2(d)
                elif d >= 0 and phase_ == 1:
                    norm_sum(d)
                if d >= 0 and phase_ == 3:
                    norm_out(d)
            norm_s2(3)
            output_lo(6)
            norm_sum(3)
            norm_out(3)
            output_lo(7)

            def out_projection(base, b, mix):
                mixer_zero_dve(dve, b)
                for u in range(4):
                    if u % 2 == 0:
                        if u == 2 or base != ATT_OUT:
                            split_lo(dve, base // 2 + u // 2, 1)
                        split_lo(dve, base // 2 + u // 2 + 1, 0)
                    if u < 3:
                        mixer_sum_dve(dve, b, 2 * u)
                post_dve(dve, b, mix)

            def ffn(layer):
                b = 1 + 2 * layer
                fv, fa = fvs[layer], fas[layer]
                base = FFN_IN[layer] // 2

                def pair(i):
                    if isinstance(i, int):
                        dve.wait_ge(r_ready, b + 1)
                    else:
                        split_lo(dve, i + base, 1)
                    dve.wait_ge(unit_done, i * 2 + (FFN_IN[layer] + 1))
                    for m in range(2):
                        if not isinstance(i, int):
                            fv.wait(dve, f"lo{m}", i - 1)
                        fv.done(TTo(f_g[:, m, :], bank[m][:, :], rB[:, :], ALU.mult), f"g{m}")
                    split_lo(dve, i + (base + 1), 0)
                    dve.wait_ge(unit_done, i * 2 + (FFN_IN[layer] + 2))
                    for m in range(2):
                        if m:
                            fv.wait(dve, "h0", i)
                        elif not isinstance(i, int):
                            fv.wait(dve, "h1", i - 1)
                        fv.done(TTo(f_u[:, :], bank[2 + m][:, :], rB[:, :], ALU.mult), f"u{m}")
                        fv.wait(dve, f"u{m}", i)
                        fa.wait(dve, f"s{m}", i)
                        fv.done(TTo(f_g[:, m, :], f_g[:, m, :], f_u[:, :], ALU.mult), f"h{m}")
                    for m in range(2):
                        fa.wait(dve, f"hi{m}", i)
                        dst, hi = (t[:, bass.ds(i * 2 + m, 1), :].rearrange("p a t -> p (a t)") for t in (hid_lo, hid_hi))
                        fv.done(TTo(dst, f_g[:, m, :], fview(hi), ALU.subtract), f"lo{m}")
                pair(0)
                with dve.Fori(1, FFN // UC) as i:
                    pair(i)
                mixer_zero_dve(dve, b + 1)
                base = FFN_OUT[layer] // 2

                def six_units(i):
                    for v in range(6):
                        m, kc = divmod(v, 3)
                        if v % 2 == 0:
                            split_lo(dve, i * 3 + (base + v // 2), 1)
                        if kc == 2 and (i, m) != (1, 1):
                            mixer_sum_dve(dve, b + 1, i * 4 + 2 * m)
                        if v % 2 == 0:
                            split_lo(dve, i * 3 + (base + v // 2 + 1), 0)
                six_units(0)
                six_units(1)
                post_dve(dve, b + 1, mix_ffn)

            out_projection(ATT_OUT, 1, mix_att)
            ffn(0)

            lbc = cols[:, C_LB:C_LB + 8]
            TTo(lb[:, 0, :], lbc, lbc, ALU.subtract).then_inc(lb_v, 1)
            dve.wait_ge(lb_a, 1)
            V.reciprocal(lb[:, 2, :], lb[:, 1, :]).then_inc(lb_v, 1)
            dve.wait_ge(lb_v, 2)
            TTo(lb[:, 1, :], lb[:, 1, :], lb[:, 2, :], ALU.mult).then_inc(lb_v, 1)
            dve.wait_ge(lb_v, 3)
            TTo(lb[:, 3, :], lb[:, 1, :], lb[:, 1, :], ALU.subtract).then_inc(lb_v, 1)
            dve.wait_ge(lb_v, 4)
            TS(lb[:, 4, :], lb[:, 3, :], -1.0, 1.0, ALU.mult, ALU.add).then_inc(lb_v, 1)
            split_lo(dve, REC_IN // 2 + 1, 0)
            split_lo(dve, REC_IN // 2 + 1, 1)
            split_lo(dve, REC_IN // 2 + 2, 0)

            flat = lambda ap: ap.rearrange("p a t -> p (a t)")
            blocks = lambda ap, L: flat(ap).rearrange("p (b h t) -> p b h t", h=2, t=L)
            chunks = lambda ap: flat(ap).rearrange("p (c t) -> p c t", t=CH)

            def qf_evac(j, s):
                dve.wait_ge(unit_done, j * 2 + (REC_IN + 4 + s + 1))
                for a in range(2):
                    last = TTo((q_sb, k_sb)[s][:, a, :], bank[2 * s + a][:, :], rB[:, :], ALU.mult)
                last.then_inc(s_qf, 1)

            def diff(j, l):
                L = LEVELS[l]
                if l >= 2:
                    ev.wait(dve, f"mq{l - 2}", j)
                    ep.wait(dve, f"mk{l - 2}", j)
                else:
                    ev.wait(dve, "scan", j)
                v = flat(b_sb[:, :, :]).rearrange("p (b t) -> p b t", t=2 * L)
                ev.done(TTo(flat(e_sb[:, l % 2]).rearrange("p (b t) -> p b t", t=2 * L), v,
                            v[:, :, L - 1:L].to_broadcast([P, 2 * T // (2 * L), 2 * L]), ALU.subtract), f"d{l}")

            def queries(j, l):
                ea.wait(dve, f"et{l}", j)
                if l >= 4:
                    ht.wait(dve, f"lev{l - 4}_1", j)
                v = lambda ap: blocks(ap, LEVELS[l])[:, :, 1, :]
                ev.done(TTo(v(m_sb[:, l % 4]), v(e_sb[:, l % 2]), v(q_sb[:, :, :]), ALU.mult), f"mq{l}")

            def gates_and_decays(j):
                ea.wait(dve, "fs", j)
                for a in range(2):
                    col = lambda r: lb[:, r, bass.ds(j * 2 + a, 1)]
                    last = TS(e_sb[:, 1, a, :], e_sb[:, 1, a, :], col(4), col(3), ALU.mult, ALU.add)
                ev.done(last, "forget")
                ev.wait(dve, "forget", j)
                ev.done(TS(flat(k_sb[:, :, :]), flat(e_sb[:, 1]), -1.0, 1.0, ALU.mult, ALU.add), "key")
                ea.wait(dve, "g", j)
                dve.wait_ge(setup, 3)
                ev.done(V.tensor_tensor_scan(flat(b_sb[:, :, :]), rzero[:, :], flat(e_sb[:, 1]), 0.0,
                                             ALU.mult, ALU.add), "scan")
                ev.wait(dve, "scan", j)
                ev.done(TTo(chunks(ke_sb[:, :, :]), chunks(b_sb[:, :, :]),
                            chunks(b_sb[:, :, :])[:, :, CH - 1:CH].to_broadcast([P, 2 * TT, CH]), ALU.subtract), "dke")
                ea.wait(dve, "qs", j)
                ev.done(STT(out=flat(q_sb[:, :, :]), in0=flat(q_sb[:, :, :]), scalar=float(P) ** -0.5,
                            in1=flat(e_sb[:, 0]), op0=ALU.mult, op1=ALU.mult), "qgate")
                ev.wait(dve, "qgate", j)
                diff(j, 0)
                diff(j, 1)
                queries(j, 0)
                diff(j, 2)
                queries(j, 1)
                diff(j, 3)
                queries(j, 2)
                queries(j, 3)

            def select(j, name, l, a):
                ht.wait(dve, name, j)
                v = lambda ap: ap.rearrange("p (c t) -> p c t", t=CH)
                if l is None:
                    hs.done(TTo(v(att[:, a, :]), v(bank[6 + a][:, :]),
                                ident[:, :].unsqueeze(1).to_broadcast([P, TT, P]), ALU.mult), name)
                else:
                    hs.wait(dve, f"diag{a}" if l == 0 else f"lev{l - 1}_{a}", j)
                    if not isinstance(j, int):
                        waited(dve)
                    hs.done(V.copy_predicated(v(att[:, a, :]), rmask[:, l, :].unsqueeze(1).to_broadcast([P, TT, P]),
                                              v(bank[6 + a][:, :])), name)

            def heads(j, then, split):
                lev = lambda l: [select(j, f"lev{l}_{a}", l, a) for a in range(2)]
                for a in range(2):
                    select(j, f"diag{a}", None, a)
                diff(j, 4)
                lev(0)
                diff(j, 5)
                queries(j, 4)
                lev(1)
                diff(j, 6)
                queries(j, 5)
                lev(2)
                queries(j, 6)
                lev(3)
                lev(4)
                lev(5)
                if then is not None:
                    ep.wait(dve, "qb", j)
                    ev.wait(dve, "mq6", j)
                    qf_evac(then, 1)
                for a in range(2):
                    ht.wait(dve, f"u{a}", j)
                    for c in range(1, 4):
                        u = bank[4 + a][:, (c - 1) * P:c * P]
                        if c == 1:
                            ho.done(V.tensor_copy(state[:, a, 0, :], u), f"s1_{a}")
                        else:
                            ho.wait(dve, f"s{c - 1}_{a}", j)
                            ho.done(STT(out=state[:, a, c - 1, :], in0=state[:, a, c - 2, :],
                                        scalar=ebl[:, a, c - 1:c], in1=u, op0=ALU.mult, op1=ALU.add), f"s{c}_{a}")
                lev(6)
                if then is not None:
                    qf_evac(then, 0)
                split_lo(dve, split, 0)
                for a in range(2):
                    hk.wait(dve, f"osq{a}", j)
                    ho.done(V.tensor_reduce(r_rs[:, 0, bass.ds(j * 2 + a, 1), :].rearrange("p a c -> p (a c)"),
                                            r_sq[:, :].rearrange("p (c v) -> p c v", c=TT), axis=AXX, op=ALU.add), f"ss{a}")

            dve.wait_ge(rmask_in, 16)
            dve.wait_ge(r_ready, 3)
            V.tensor_copy(rmask[:, :, :], flat(qb_sb[:, :, :])[:, 0:NL * P].rearrange("p (l t) -> p l t", l=NL)).then_inc(rmask_ready, 1)
            dve.wait_ge(rmask_ready, 1)
            split_lo(dve, qf, 1)
            split_lo(dve, qf + 1, 0)
            qf_evac(0, 1)
            qf_evac(0, 0)
            with dve.Fori(1, 4) as j:
                split_lo(dve, j + qf, 1)
                gates_and_decays(j - 1)
                heads(j - 1, j, j + (qf + 1))
            split_lo(dve, qf + 4, 1)
            gates_and_decays(3)
            heads(3, None, qf + 5)
            split_lo(dve, qf + 5, 1)

            def gate_mul(u):
                dve.wait_ge(rrs_a, 2)
                if u >= 2:
                    dve.wait_ge(gT_done, 2 * (u - 1))
                for t in range(TT):
                    dve.wait_ge(g_silu, 4 * u + t + 1)
                    for h in range(2):
                        hs_ = slice(h * P, (h + 1) * P)
                        STT(out=og[:, u % 2, t, hs_], in0=ro[:, t, (2 * u + h) * P:(2 * u + h + 1) * P],
                            scalar=r_rs[:, 2, 2 * u + h, t:t + 1], in1=gate[:, u % 2, t, hs_],
                            op0=ALU.mult, op1=ALU.mult).then_inc(g_mul, 1)

            def gated_lo(c):
                dve.wait_ge(gT_hi, c + 1)
                STT(out=act_lo[:, c, :], in0=bank[4 + c % 4][:, :], scalar=cols[:, C_GN:C_GN + 1],
                    in1=fview(act_hi[:, c, :]), op0=ALU.mult, op1=ALU.subtract).then_inc(gT_lo, 1)
            gate_mul(0)
            gate_mul(1)
            split_lo(dve, qf + 6, 0)
            gate_mul(2)
            for c in range(4):
                gated_lo(c)
            gate_mul(3)
            for c in range(4, KT):
                gated_lo(c)
            out_projection(REC_OUT, 3, mix_rec)
            ffn(1)


def constants():
    half = HD // 2
    inv = (10000.0 ** (-np.arange(0, HD, 2, dtype=np.float32) / HD)).astype(np.float32)
    ang = np.arange(T, dtype=np.float32)[None, :] * inv[:, None]
    cos, sin = (np.tile(f(ang).astype(np.float32), (P // half, 1)) for f in (np.cos, np.sin))
    rel = (T - P) + np.arange(P)[:, None] - np.arange(T)[None, :]
    causal = rel >= 0
    held = sum(((rel <= w) & (rel % d == 0) & causal).astype(np.int64) for w, d in ((128, 1), (512, 4), (2048, 16)))
    mask_a = np.where(held > 0, np.log(np.maximum(held, 1)) / SCALE, -BIG).astype(np.float32)
    mask_b = np.where(causal, 0.0, -BIG).astype(np.float32)
    s, t = np.arange(P)[:, None], np.arange(P)[None, :]
    levels = np.stack([(s // (2 * L) == t // (2 * L)) & (s % (2 * L) < L) & (t % (2 * L) >= L) for L in LEVELS], 1)
    return dict(cos_t=cos, sin_t=sin, mask_a=mask_a, mask_b=mask_b, ident_in=np.eye(P, dtype=np.float32),
                level_masks=levels.reshape(P, NL * P).astype(np.float32))


_INS = ["x", "norm_gains", "att_w_in", "att_lambda", "att_subln", "att_w_out", "rec_w_in",
        "rec_lower_bounds", "rec_gnorm", "rec_w_out", "ffn_w_in", "ffn_w_out"]


def kernel(**inputs):
    import concourse.bacc as bacc
    from concourse.bass_utils import run_bass_kernel_spmd

    nc = bacc.Bacc("TRN2", target_bir_lowering=False, num_devices=1)
    given = {n: np.ascontiguousarray(inputs[n]) for n in _INS} | constants()
    arrays, args = {}, []
    for name, a in given.items():
        arrays[f"in_{name}"] = a
        args.append(nc.dram_tensor(f"in_{name}", a.shape, mybir.dt.from_np(a.dtype), kind="ExternalInput").ap())
    args.append(nc.dram_tensor("out_0", (1, T, D), F32, kind="ExternalOutput").ap())
    trunk(nc, *args)
    return run_bass_kernel_spmd(nc, [arrays], core_ids=[0]).results[0]["out_0"]
```
